# Optimizing a Trainium2 kernel written in Bass

```python
import math
import jax
import jax.numpy as jnp
from jax import lax
import numpy as np

D_MODEL = 1024
BATCH = 1
SEQ = 512
DEPTH = 2

N_HEADS = 4
HEAD_DIM = D_MODEL // N_HEADS
BLOCK = 128
D_FF = 2816
N_EXPERTS = 8
TOP_K = 2
D_FF_EXPERT = D_FF // 4
PLE_DIM = 256
N_A = DEPTH // 2
N_B = DEPTH - N_A
N_DENSE = (DEPTH + 1) // 2
N_MOE = DEPTH // 2
DEEPNORM_ALPHA = (2.0 * DEPTH) ** 0.25
DEEPNORM_BETA = (8.0 * DEPTH) ** -0.25
FORGET_BIAS_INIT = 2.0
LN_EPS = 1e-5

kernel_name = "yoco_stickbreak_fox_moe_deepnorm"

def layer_norm(x, g, b):
    xf = x.astype(jnp.float32)
    mu = jnp.mean(xf, axis=-1, keepdims=True)
    var = jnp.mean(jnp.square(xf - mu), axis=-1, keepdims=True)
    y = (xf - mu) * lax.rsqrt(var + LN_EPS) * g.astype(jnp.float32) + b.astype(jnp.float32)
    return y.astype(x.dtype)

def split_heads(t):
    b, s, _ = t.shape
    return t.reshape(b, s, N_HEADS, HEAD_DIM).transpose(0, 2, 1, 3)

def merge_heads(o):
    b, h, s, dh = o.shape
    return o.transpose(0, 2, 1, 3).reshape(b, s, h * dh)

def stick_breaking_attention(q, k, v):
    b, h, s_len, _ = q.shape
    nb = s_len // BLOCK
    scale = 1.0 / math.sqrt(HEAD_DIM)
    r = jnp.arange(BLOCK)
    tri_in = (r[:, None] > r[None, :]).astype(jnp.float32)
    outs = []
    for bi in range(nb):
        lo, hi = bi * BLOCK, (bi + 1) * BLOCK
        nk = bi + 1
        z = jnp.einsum('bhqd,bhkd->bhqk', q[:, :, lo:hi], k[:, :, :hi]).astype(jnp.float32) * scale
        mask = jnp.arange(hi)[None, :] < (lo + r)[:, None]
        log_1m = jnp.where(mask, -jax.nn.softplus(z), 0.0)
        lb = log_1m.reshape(b, h, BLOCK, nk, BLOCK)
        tail_in = jnp.einsum('bhqnj,js->bhqns', lb, tri_in)
        rb = jnp.arange(nk)
        tri_x = (rb[:, None] > rb[None, :]).astype(jnp.float32)
        tail_x = jnp.einsum('bhqm,mn->bhqn', jnp.sum(lb, axis=-1), tri_x)
        tail = (tail_in + tail_x[..., None]).reshape(b, h, BLOCK, hi)
        a = jnp.where(mask, jnp.exp(jax.nn.log_sigmoid(z) + tail), 0.0)
        outs.append(jnp.einsum('bhqk,bhkd->bhqd', a.astype(v.dtype), v[:, :, :hi]))
    return merge_heads(jnp.concatenate(outs, axis=2))

def forgetting_attention(q, k, v, c):
    s_len = q.shape[2]
    nb = s_len // BLOCK
    scale = 1.0 / math.sqrt(HEAD_DIM)
    r = jnp.arange(BLOCK)
    outs = []
    for bi in range(nb):
        lo, hi = bi * BLOCK, (bi + 1) * BLOCK
        z = jnp.einsum('bhqd,bhkd->bhqk', q[:, :, lo:hi], k[:, :, :hi]).astype(jnp.float32) * scale
        z = z + c[:, :, lo:hi, None] - c[:, :, None, :hi]
        mask = jnp.arange(hi)[None, :] <= (lo + r)[:, None]
        w = jax.nn.softmax(jnp.where(mask, z, -jnp.inf), axis=-1)
        outs.append(jnp.einsum('bhqk,bhkd->bhqd', w.astype(v.dtype), v[:, :, :hi]))
    return merge_heads(jnp.concatenate(outs, axis=2))

def swiglu(x, w_gu, w_down):
    g, u = jnp.split(x @ w_gu, 2, axis=-1)
    return (jax.nn.silu(g) * u) @ w_down

def moe_swiglu(x, w_router, w_gu, w_down):
    logits = jnp.einsum('bsd,de->bse', x, w_router).astype(jnp.float32)
    top_val, top_idx = lax.top_k(logits, TOP_K)
    gates = jax.nn.softmax(top_val, axis=-1)
    gate_full = jnp.einsum('bsk,bske->bse', gates,
                           jax.nn.one_hot(top_idx, N_EXPERTS, dtype=jnp.float32))
    gate_full = gate_full.astype(x.dtype)
    out = jnp.zeros_like(x)
    for e in range(N_EXPERTS):
        out = out + gate_full[..., e:e + 1] * swiglu(x, w_gu[e], w_down[e])
    return out

def setup_inputs(seed: int = 0) -> dict:
    key = jax.random.key(seed)
    ks = jax.random.split(key, 20)
    d = D_MODEL
    f32 = jnp.float32
    sd = d ** -0.5
    beta = DEEPNORM_BETA
    nrm = lambda k, shape: jax.random.normal(k, shape, f32)

    x = nrm(ks[0], (BATCH, SEQ, d))
    p = nrm(ks[1], (DEPTH, BATCH, SEQ, PLE_DIM))
    qkv_col_scale = jnp.concatenate([jnp.ones((2 * d,), f32), jnp.full((d,), beta, f32)])
    a_w_qkv = nrm(ks[2], (N_A, d, 3 * d)) * sd * qkv_col_scale
    a_w_o = nrm(ks[3], (N_A, d, d)) * sd * beta
    kvf_col_scale = jnp.concatenate([jnp.ones((d,), f32), jnp.full((d,), beta, f32),
                                     jnp.ones((N_HEADS,), f32)])
    kvf_w = nrm(ks[4], (d, 2 * d + N_HEADS)) * sd * kvf_col_scale
    kvf_b_f = FORGET_BIAS_INIT + 0.1 * nrm(ks[5], (N_HEADS,))
    b_w_q = nrm(ks[6], (N_B, d, d)) * sd
    b_w_o = nrm(ks[7], (N_B, d, d)) * sd * beta
    ffn_w_gu = nrm(ks[8], (N_DENSE, d, 2 * D_FF)) * sd
    ffn_w_down = nrm(ks[9], (N_DENSE, D_FF, d)) * (D_FF ** -0.5) * beta
    moe_w_router = nrm(ks[10], (N_MOE, d, N_EXPERTS)) * sd
    moe_w_gu = nrm(ks[11], (N_MOE, N_EXPERTS, d, 2 * D_FF_EXPERT)) * sd
    moe_w_down = nrm(ks[12], (N_MOE, N_EXPERTS, D_FF_EXPERT, d)) * (D_FF_EXPERT ** -0.5) * beta
    ple_w_proj = nrm(ks[13], (DEPTH, PLE_DIM, d)) * (PLE_DIM ** -0.5) * beta
    ple_w_gate = nrm(ks[14], (DEPTH, d, d)) * sd
    ln_g = 1.0 + 0.02 * nrm(ks[15], (DEPTH, 2, d))
    ln_b = 0.02 * nrm(ks[16], (DEPTH, 2, d))
    return {"x": x, "p": p, "a_w_qkv": a_w_qkv, "a_w_o": a_w_o,
            "kvf_w": kvf_w, "kvf_b_f": kvf_b_f, "b_w_q": b_w_q, "b_w_o": b_w_o,
            "ffn_w_gu": ffn_w_gu, "ffn_w_down": ffn_w_down,
            "moe_w_router": moe_w_router, "moe_w_gu": moe_w_gu, "moe_w_down": moe_w_down,
            "ple_w_proj": ple_w_proj, "ple_w_gate": ple_w_gate,
            "ln_g": ln_g, "ln_b": ln_b}

def reference(x, p, a_w_qkv, a_w_o, kvf_w, kvf_b_f, b_w_q, b_w_o,
              ffn_w_gu, ffn_w_down, moe_w_router, moe_w_gu, moe_w_down,
              ple_w_proj, ple_w_gate, ln_g, ln_b):
    d = D_MODEL
    k_sh = v_sh = c_sh = None
    for i in range(DEPTH):
        if i < N_A:
            q, k, v = jnp.split(x @ a_w_qkv[i], 3, axis=-1)
            mix = stick_breaking_attention(split_heads(q), split_heads(k), split_heads(v))
            mix = mix @ a_w_o[i]
        else:
            if i == N_A:
                kvf = x @ kvf_w
                k_sh = split_heads(kvf[..., :d])
                v_sh = split_heads(kvf[..., d:2 * d])
                log_f = jax.nn.log_sigmoid(kvf[..., 2 * d:].astype(jnp.float32)
                                           + kvf_b_f.astype(jnp.float32))
                c_sh = jnp.cumsum(log_f.transpose(0, 2, 1), axis=-1)
            j = i - N_A
            q = split_heads(x @ b_w_q[j])
            mix = forgetting_attention(q, k_sh, v_sh, c_sh) @ b_w_o[j]
        x = layer_norm(DEEPNORM_ALPHA * x + mix, ln_g[i, 0], ln_b[i, 0])
        if i % 2 == 0:
            ff = swiglu(x, ffn_w_gu[i // 2], ffn_w_down[i // 2])
        else:
            ff = moe_swiglu(x, moe_w_router[i // 2], moe_w_gu[i // 2], moe_w_down[i // 2])
        x = layer_norm(DEEPNORM_ALPHA * x + ff, ln_g[i, 1], ln_b[i, 1])
        x = x + (p[i] @ ple_w_proj[i]) * jax.nn.sigmoid(x @ ple_w_gate[i])
    return x


_drawn_inputs = setup_inputs


def setup_inputs(seed=0):
    import zlib

    import numpy as np

    out = dict(_drawn_inputs(seed))
    spreads = {}
    factors = {'kvf_b_f': 64.0}
    for name, (base, spread) in spreads.items():
        noise = np.random.default_rng([zlib.crc32(name.encode()), seed]).standard_normal(out[name].shape)
        drawn = base * np.exp(spread * noise) if base else spread * noise
        out[name] = jnp.asarray(drawn.astype(out[name].dtype))
    for name, factor in factors.items():
        out[name] = (out[name] * factor).astype(out[name].dtype)
    return out
```

```python
from contextlib import ExitStack

import concourse.bass as bass
from concourse import mybir

F32 = mybir.dt.float32
R32 = mybir.dt.float32r
U32 = mybir.dt.uint32
ACT = mybir.ActivationFunctionType
ALU = mybir.AluOpType
AX = mybir.AxisListType

P = 128
SEQ = 512
D = 1024
KD = D // P
TT = SEQ // P
H = 4
DH = D // H
DT = DH // P
FF = 2816
KF = FF // P
NE = 8
FE = 704
FC = FE // 2
KE = -(-FE // P)
FE_LAST = FE - (KE - 1) * P
PD = 256
KP = PD // P
DEPTH = 2
ALPHA = (2.0 * DEPTH) ** 0.25
SCALE = 1.0 / float(DH) ** 0.5
EPS = 1e-5
NEG = -1e30
BIG = 3e38

RAW = 4
SPLIT = 2
CH = 1536

WID = [SEQ - n * P for n in range(TT)]
OFF = [sum(WID[:n]) for n in range(TT)]
TRI = sum(WID)

PHASES = [
    ("q0", 8, KD * P), ("k0", 8, KD * P), ("v0", 8, 4 * 256), ("o0", 8, KD * P),
    ("gu", 2 * KF, KD * P), ("down", 16, KF // 2 * P), ("proj0", 4, KP * 256), ("gate0", 8, KD * P),
    ("q1", 8, KD * P), ("k1", 8, KD * P), ("v1", 8, 4 * 256), ("o1", 8, KD * P),
    ("moe", NE * 12, 4 * FC), ("proj1", 4, KP * 256), ("gate1", 8, KD * P),
]
BASE, SIZE, COUNT, NEXT_SIZE = {}, {}, {}, {}
_at = 0
for _n, (_name, _count, _size) in enumerate(PHASES):
    BASE[_name], SIZE[_name], COUNT[_name] = _at, _size, _count
    NEXT_SIZE[_name] = PHASES[_n + 1][2] if _n + 1 < len(PHASES) else 0
    _at += _count
CHUNKS = _at
assert all(b % RAW == 0 for b in BASE.values())

DRAINED, _n = {}, 0
for _name in ("q0", "k0", "v0", "o0", "gu", "down", "proj0", "gate0", "q1", "k1", "v1", "o1", "turn", "proj1", "gate1"):
    DRAINED[_name] = _n
    _n += COUNT.get(_name, KD)
OUT_HI, _n = {}, 0
for _name in ("q0", "k0", "v0", "gu", "q1", "k1", "v1"):
    OUT_HI[_name] = _n
    _n += COUNT[_name]
GATED = {"gu": 0, "gate0": KF, "gate1": KF + KD}


def quads(eng, name, step, peel=False):
    first, rounds = BASE[name] // RAW, COUNT[name] // RAW
    looped = rounds - 1 if peel else rounds
    if looped > 2:
        with eng.Fori(0, looped) as i:
            for j in range(RAW):
                step(first + i, i, j, False)
        done = looped
    else:
        done = 0
    for i in range(done, rounds):
        for j in range(RAW):
            step(first + i, i, j, i == rounds - 1 and j == RAW - 1)


def build(nc, x, p, a_w_qkv, a_w_o, kvf_w, kvf_b_f, b_w_q, b_w_o, ffn_w_gu, ffn_w_down,
          moe_w_router, moe_w_gu, moe_w_down, ple_w_proj, ple_w_gate, ln_g, ln_b, out):
    with ExitStack() as ctx:
        base = (nc.sbuf_base + 63) // 64 * 64
        place = [base]

        def at(name, shape, dt, offset):
            return nc.alloc_sbuf_tensor_at(name, shape, dt, offset=offset)

        def sb(name, shape, dt=F32):
            n = 4
            for s in shape[1:]:
                n *= s
            t = at(name, shape, dt, place[0])
            place[0] += (n + 31) // 32 * 32
            return t

        def sem(name):
            return ctx.enter_context(nc.semaphore(name))

        x_exact = sb("x_exact", [P, KD, SEQ])
        work0 = place[0]
        x_hi = sb("x_hi", [P, KD, SEQ], R32)
        x_lo = sb("x_lo", [P, KD, SEQ], R32)
        raw = [sb(f"raw{i}", [P, CH]) for i in range(RAW)]
        w_hi = [sb(f"w_hi{i}", [P, CH], R32) for i in range(SPLIT)]
        w_lo = [sb(f"w_lo{i}", [P, CH], R32) for i in range(SPLIT)]
        ident = sb("ident", [P, P])
        ones = sb("ones", [P, P])
        mean_f = sb("mean_f", [P, P])
        mean_r = sb("mean_r", [P, P], R32)
        neg_ones = sb("neg_ones", [P, P], R32)
        neg_incl = sb("neg_incl", [P, P], R32)
        cum = sb("cum", [P, P])
        keep = sb("keep", [P, P])
        floor_a = sb("floor_a", [P, P])
        clip_b = sb("clip_b", [P, P])
        ln_rows = sb("ln_rows", [64, P])
        ln_cols = sb("ln_cols", [P, 64])
        w_f = sb("w_f", [P, KD, H])
        w_r = sb("w_r", [P, KD, NE])
        b_f = sb("b_f", [P, H])
        p_tok = sb("p_tok", [P, TT, PD])
        h_tmp = [sb(f"h_tmp{i}", [P, SEQ]) for i in range(2)]
        eps = sb("eps", [P, 1])
        log_f = sb("log_f", [P, TT, H])
        f_abs = sb("f_abs", [P, TT, H])
        f_pre = sb("f_pre", [P, TT, H])
        c_col = sb("c_col", [P, TT, H])
        neg_max = sb("neg_max", [P, TT])
        row_sum = sb("row_sum", [P, TT])
        row_inv = sb("row_inv", [P, TT])
        logits = sb("logits", [P, TT, NE])
        top = sb("top", [P, TT, NE])
        top_at = sb("top_at", [P, TT, NE], U32)
        top_f = sb("top_f", [P, TT, 2])
        g_diff = sb("g_diff", [P, TT])
        g_exp = sb("g_exp", [P, TT])
        g_sum = sb("g_sum", [P, TT])
        g_one = sb("g_one", [P, TT])
        g_two = sb("g_two", [P, TT])
        lanes = sb("lanes", [P, NE])
        gates_a = sb("gates_a", [P, TT, NE])
        gates_b = sb("gates_b", [P, TT, NE])
        gates = sb("gates", [P, TT, NE])
        G = (place[0] + 63) // 64 * 64
        KB = 1024
        assert G + 96 * KB <= nc.sbuf_usable_end, (G, nc.sbuf_usable_end)

        x_tok = at("x_tok", [P, TT, D], F32, G)
        neg_incl_f = at("neg_incl_f", [P, P], F32, G + 92 * KB)
        q_hi = at("q_hi", [P, KD, SEQ], R32, G)
        q_lo = at("q_lo", [P, KD, SEQ], R32, G + 16 * KB)
        k_hi = at("k_hi", [P, KD, SEQ], R32, G + 32 * KB)
        k_lo = at("k_lo", [P, KD, SEQ], R32, G + 48 * KB)
        v_hi = at("v_hi", [P, TT, D], R32, G + 64 * KB)
        v_lo = at("v_lo", [P, TT, D], R32, G + 80 * KB)
        h_hi = at("h_hi", [P, KF, SEQ], R32, G)
        h_lo = at("h_lo", [P, KF, SEQ], R32, G + 44 * KB)
        proj = at("proj", [P, KD, SEQ], F32, G)
        sig = at("sig", [P, KD, SEQ], F32, G + 16 * KB)
        pt_hi = at("pt_hi", [P, KP, SEQ], R32, G + 88 * KB)
        pt_lo = at("pt_lo", [P, KP, SEQ], R32, G + 92 * KB)
        sq = [at(f"sq{i}", [P, SEQ], F32, G + (64 + 2 * i) * KB) for i in range(2)]
        rstd = at("rstd", [P, SEQ], F32, G + 68 * KB)
        acc = at("acc", [P, TT, D], F32, G)
        he = at("he", [P, TT, KE * P], F32, G + 16 * KB)
        het_hi = at("het_hi", [P, KE, SEQ], R32, G + 28 * KB)
        het_lo = at("het_lo", [P, KE, SEQ], R32, G + 40 * KB)
        o_tok = at("o_tok", [P, TT, D], F32, G)

        wk = lambda name, shape, dt, o: at(name, shape, dt, work0 + o)
        ln_a = wk("ln_a", [P, TRI], F32, 0)
        sp = wk("sp", [P, TRI], F32, 5 * KB)
        sp_hi = wk("sp_hi", [P, TRI], R32, 10 * KB)
        sp_lo = wk("sp_lo", [P, TRI], R32, 15 * KB)
        a_hi = wk("a_hi", [P, TRI], R32, 20 * KB)
        a_lo = wk("a_lo", [P, TRI], R32, 25 * KB)
        a_diag = wk("a_diag", [P, TT, P], F32, 30 * KB)
        zb = wk("zb", [P, TRI], F32, 0)
        wt_hi = wk("wt_hi", [P, TT, SEQ], R32, 5 * KB)
        wt_lo = wk("wt_lo", [P, TT, SEQ], R32, 13 * KB)
        c_row = wk("c_row", [P, H, SEQ], F32, 21 * KB)
        c_diag = wk("c_diag", [P, TT, P], F32, 29 * KB)
        WB = [(m + 1) * P for m in range(TT)]
        OB = [sum(WB[:m]) for m in range(TT)]

        bank = [ctx.enter_context(nc.psum_tensor(f"bank{i}", [P, 512], F32)) for i in range(8)]

        raw_loaded = [sem(f"raw_loaded{i}") for i in range(RAW)]
        last_loaded = [sem(f"last_loaded{i}") for i in range(2)]
        small_loaded = sem("small_loaded")
        ln_loaded = sem("ln_loaded")
        x_loaded = sem("x_loaded")
        p_loaded = sem("p_loaded")
        out_stored = sem("out_stored")
        hi_ready = sem("hi_ready")
        lo_ready = sem("lo_ready")
        chunk_done = sem("chunk_done")
        drained = sem("drained")
        out_hi = sem("out_hi")
        gated = sem("gated")
        hidden = sem("hidden")
        built = sem("built")
        consts = sem("consts")
        turned = sem("turned")
        turned_out = sem("turned_out")
        turned_hi = sem("turned_hi")
        turned_lo = sem("turned_lo")
        summed = sem("summed")
        y_hi_ready = sem("y_hi_ready")
        mean_done = sem("mean_done")
        centred = sem("centred")
        squared = sem("squared")
        var_done = sem("var_done")
        std_ready = sem("std_ready")
        rstd_ready = sem("rstd_ready")
        normed = sem("normed")
        affine = sem("affine")
        x_ready = sem("x_ready")
        embedded = sem("embedded")
        ple_step = sem("ple_step")
        z_done = sem("z_done")
        absed = sem("absed")
        exped = sem("exped")
        logged = sem("logged")
        sp_raw = sem("sp_raw")
        sp_ready = sem("sp_ready")
        sp_hi_ready = sem("sp_hi_ready")
        sp_lo_ready = sem("sp_lo_ready")
        tail_done = sem("tail_done")
        diag_cut = sem("diag_cut")
        a_ready = sem("a_ready")
        a_hi_ready = sem("a_hi_ready")
        a_lo_ready = sem("a_lo_ready")
        mixed = sem("mixed")
        mix_hi = sem("mix_hi")
        mix_lo = sem("mix_lo")
        f_done = sem("f_done")
        f_step = sem("f_step")
        f_act = sem("f_act")
        c_done = sem("c_done")
        c_copied = sem("c_copied")
        diag_ready = sem("diag_ready")
        row_done = sem("row_done")
        row_copied = sem("row_copied")
        z2_done = sem("z2_done")
        z2_step = sem("z2_step")
        e_ready = sem("e_ready")
        inv_ready = sem("inv_ready")
        w_ready = sem("w_ready")
        w_turned = sem("w_turned")
        wt_hi_ready = sem("wt_hi_ready")
        wt_ready = sem("wt_ready")
        router_done = sem("router_done")
        route_step = sem("route_step")
        gate_exp = sem("gate_exp")
        gates_ready = sem("gates_ready")
        silu_ready = sem("silu_ready")
        he_ready = sem("he_ready")
        he_turned = sem("he_turned")
        het_hi_ready = sem("het_hi_ready")
        het_ready = sem("het_ready")
        group_done = sem("group_done")
        acc_ready = sem("acc_ready")
        acc_turned = sem("acc_turned")
        final_turned = sem("final_turned")
        final_dve = sem("final_dve")
        final_act = sem("final_act")

        def cols(w, c, n=P):
            return w.rearrange("(k p) n -> p k n", p=P)[:, :, bass.ds(c, n)]

        def view(slot, k):
            return raw[slot][:, :].rearrange("p (k n) -> p k n", k=k)

        def flat(slot, k, n):
            return raw[slot][:, 0:k * n].rearrange("p (k n) -> p k n", k=k)

        block = ctx.enter_context(nc.Block())

        @block.sync
        def _(sp_eng):
            xr = x.rearrange("b (t p) d -> (b p) t d", p=P)
            for t in range(TT):
                sp_eng.dma_start(x_tok[:, t, :], xr[:, t, :]).then_inc(x_loaded, 16)

            sp_eng.dma_start(ln_rows[0:32, :], ln_g.rearrange("l w (k p) -> (l w k) p", p=P)).then_inc(ln_loaded, 16)
            sp_eng.dma_start(ln_rows[32:64, :], ln_b.rearrange("l w (k p) -> (l w k) p", p=P)).then_inc(ln_loaded, 16)

            def slot_free(q, j):
                sp_eng.wait_ge(lo_ready, 4 * q + j - RAW + 1)

            def from_cols(w, col0, k=KD, n=P):
                def step(q, i, j, last):
                    if not isinstance(q, int) or q > 0:
                        slot_free(q, j)
                    sp_eng.dma_start(flat(j, k, n), cols(w, col0 + (RAW * i + j) * n, n)).then_inc(raw_loaded[j], 16)
                return step

            def v_step(w, col0):
                wv = w.rearrange("(g k p) n -> g p k n", p=P, g=2)

                def step(q, i, j, last):
                    slot_free(q, j)
                    sp_eng.dma_start(flat(j, 4, 256), wv[j % 2][:, :, bass.ds(col0 + (2 * i + j // 2) * 256, 256)]
                                     ).then_inc(raw_loaded[j], 16)
                return step

            def gu_step(q, i, j, last):
                slot_free(q, j)
                sp_eng.dma_start(flat(j, KD, P), cols(ffn_w_gu[0], (2 * i + j // 2) * P + (j % 2) * FF)
                                 ).then_inc(raw_loaded[j], 16)

            def down_step(q, i, j, last):
                wd = ffn_w_down[0].rearrange("(g k p) n -> g p k n", p=P, g=2)
                slot_free(q, j)
                sp_eng.dma_start(flat(j, KF // 2, P), wd[j % 2][:, :, bass.ds((2 * i + j // 2) * P, P)]
                                 ).then_inc(raw_loaded[j], 16)

            def load_small():
                sp_eng.dma_start(w_f[:, :, :], cols(kvf_w, 2 * D, H)).then_inc(small_loaded, 16)
                sp_eng.dma_start(w_r[:, :, :], cols(moe_w_router[0], 0, NE)).then_inc(small_loaded, 16)
                sp_eng.dma_start(b_f[:, :], kvf_b_f.rearrange("(a h) -> a h", a=1).to_broadcast([P, H])).then_inc(small_loaded, 16)

            def load_p(layer):
                if layer:
                    sp_eng.wait_ge(turned, KD + KP + 1)
                sp_eng.dma_start(p_tok[:, :, :], p[layer].rearrange("b (t p) d -> (b p) t d", p=P)).then_inc(p_loaded, 16)

            quads(sp_eng, "q0", from_cols(a_w_qkv[0], 0))
            load_small()
            load_p(0)
            quads(sp_eng, "k0", from_cols(a_w_qkv[0], D))
            quads(sp_eng, "v0", v_step(a_w_qkv[0], 2 * D))
            quads(sp_eng, "o0", from_cols(a_w_o[0], 0))
            quads(sp_eng, "gu", gu_step)
            quads(sp_eng, "down", down_step)
            quads(sp_eng, "proj0", from_cols(ple_w_proj[0], 0, KP, 256))
            quads(sp_eng, "gate0", from_cols(ple_w_gate[0], 0))
            load_p(1)
            quads(sp_eng, "q1", from_cols(b_w_q[0], 0))
            quads(sp_eng, "k1", from_cols(kvf_w, 0))
            quads(sp_eng, "v1", v_step(kvf_w, D))
            quads(sp_eng, "o1", from_cols(b_w_o[0], 0))
            q0 = BASE["moe"] // RAW
            with sp_eng.Fori(0, NE) as e:
                for c in range(8):
                    half, up, kh = c // 4, c // 2 % 2, c % 2
                    col = up * FE + half * FC
                    src = moe_w_gu[0][bass.ds(e, 1), kh * 4 * P:(kh + 1) * 4 * P, col:col + FC]
                    slot_free(q0 + 3 * e + c // RAW, c % RAW)
                    sp_eng.dma_start(flat(c % RAW, 4, FC), src.rearrange("e (k p) n -> p (e k) n", p=P)
                                     ).then_inc(raw_loaded[c % RAW], 16)
                for c in range(4):
                    full, r0, col = (3, 2)[c % 2], c % 2 * 3 * P, c // 2 * 512
                    slot_free(q0 + 3 * e + 2, c)
                    src = moe_w_down[0][bass.ds(e, 1), r0:r0 + full * P, col:col + 512]
                    sp_eng.dma_start(flat(c, 3, 512)[:, 0:full, :], src.rearrange("e (k p) n -> p (e k) n", p=P)
                                     ).then_inc(raw_loaded[c], 16)
                    if c % 2:
                        src = moe_w_down[0][bass.ds(e, 1), (KE - 1) * P:FE, col:col + 512]
                        sp_eng.dma_start(raw[c][0:FE_LAST, 1024:1536], src.rearrange("e p n -> (e p) n")
                                         ).then_inc(last_loaded[c // 2], 16)
            quads(sp_eng, "proj1", from_cols(ple_w_proj[1], 0, KP, 256))
            quads(sp_eng, "gate1", from_cols(ple_w_gate[1], 0))
            for t in range(TT):
                sp_eng.wait_ge(final_dve, t + 1)
                sp_eng.wait_ge(final_act, t + 1)
                sp_eng.dma_start(out.rearrange("b (t p) d -> (b p) t d", p=P)[:, t, :], o_tok[:, t, :]).then_inc(out_stored, 16)
            sp_eng.wait_ge(out_stored, 16 * TT)

        @block.gpsimd
        def _(pool):
            fills = [(ident, 0.0), (ones, 1.0), (mean_f, 1.0 / D), (neg_incl_f, -1.0), (cum, 1.0), (keep, 1.0),
                     (floor_a, 0.0), (clip_b, BIG)]
            for t, v in fills:
                last = pool.memset(t[:, :], v)
            last.then_inc(built, 1)
            pool.wait_ge(built, 1)
            cuts = [(ident, ALU.not_equal, 1.0, 1, -1),
                    (neg_incl_f, ALU.is_ge, 0.0, 1, -1),
                    (cum, ALU.is_ge, 0.0, -1, 1),
                    (keep, ALU.is_gt, 0.0, -1, 1),
                    (floor_a, ALU.is_gt, NEG, -1, 1),
                    (clip_b, ALU.is_ge, NEG, 1, -1)]
            for t, op, fill, mult, step in cuts:
                pool.affine_select(out=t[:, :], in_=t[:, :], pattern=[[step, P]], compare_op=op, fill=fill,
                                   base=0, channel_multiplier=mult).then_inc(built, 1)
            pool.iota(lanes[:, :], pattern=[[1, NE]], base=0, channel_multiplier=0,
                      allow_small_or_imprecise_dtypes=True).then_inc(built, 1)

        BUILT = 8
        CONSTS = 2

        @block.tensor
        def _(pe):
            def mm3(o, s_hi, s_lo, m_hi, m_lo, start, stop):
                pe.matmul(o, s_hi, m_hi, start=start, stop=False, skip_group_check=True)
                pe.matmul(o, s_hi, m_lo, start=False, stop=False, skip_group_check=True)
                return pe.matmul(o, s_lo, m_hi, start=False, stop=stop, skip_group_check=True)

            def weights(q, j):
                pe.wait_ge(lo_ready, 4 * q + j + 1)

            def free_of(value):
                if not isinstance(value, int) or value > 0:
                    pe.wait_ge(drained, value)

            def tiles(name, m_hi, m_lo, ahead=0):
                def step(q, i, j, last):
                    weights(q, j)
                    if not isinstance(i, int) or i or ahead:
                        free_of(DRAINED[name] + 4 * i + j - 3)
                    elif j == 0:
                        free_of(DRAINED[name])
                    for k in range(KD):
                        w = slice(k * P, (k + 1) * P)
                        mm = mm3(bank[j][:, :], w_hi[j % 2][:, w], w_lo[j % 2][:, w], m_hi[:, k, :], m_lo[:, k, :],
                                 k == 0, k == KD - 1)
                    mm.then_inc(chunk_done, 1)
                quads(pe, name, step)

            def values(name):
                def step(q, i, j, last):
                    weights(q, j)
                    if j % 2 == 0:
                        free_of(DRAINED[name] + (0 if i == 0 and j == 0 else 4 * i + j - 2))
                    for t in range(TT):
                        for k in range(4):
                            w, kk = slice(k * 256, (k + 1) * 256), j % 2 * 4 + k
                            mm = mm3(bank[j // 2 * 4 + t][:, 0:256], x_hi[:, kk, t * P:(t + 1) * P],
                                     x_lo[:, kk, t * P:(t + 1) * P], w_hi[j % 2][:, w], w_lo[j % 2][:, w],
                                     kk == 0, kk == KD - 1)
                    mm.then_inc(chunk_done, 1)
                quads(pe, name, step)

            def norm(n):
                pe.wait_ge(drained, DRAINED[("gu", "proj0", "turn", "proj1")[n]])
                for k in range(KD):
                    pe.matmul(bank[4][:, :], mean_r[:, :], x_hi[:, k, :], start=k == 0, stop=False)
                    mm = pe.matmul(bank[4][:, :], mean_r[:, :], x_lo[:, k, :], start=False, stop=k == KD - 1)
                mm.then_inc(mean_done, 1)
                for k in range(KD):
                    pe.wait_ge(squared, KD * n + k + 1)
                    pe.matmul(bank[5][:, :], mean_f[:, :], sq[k % 2][:, :], start=k == 0, stop=k == KD - 1
                              ).then_inc(var_done, 1)

            def embed(layer):
                pe.wait_ge(p_loaded, 16 * (layer + 1))
                for k in range(KP):
                    for t in range(TT):
                        mm = pe.transpose(bank[6 + k][:, t * P:(t + 1) * P], p_tok[:, t, k * P:(k + 1) * P], ident[:, :])
                    mm.then_inc(turned, 1)
                pe.wait_ge(turned_lo, KD + KP * (layer + 1))
                name = f"proj{layer}"

                def step(q, i, j, last):
                    weights(q, j)
                    free_of(DRAINED[name] + max(0, j - 1))
                    for s in range(2):
                        for k in range(KP):
                            w = slice(k * 256 + s * P, k * 256 + (s + 1) * P)
                            mm = mm3(bank[j % 2 * 2 + s][:, :], w_hi[j % 2][:, w], w_lo[j % 2][:, w],
                                     pt_hi[:, k, :], pt_lo[:, k, :], k == 0, k == KP - 1)
                    mm.then_inc(chunk_done, 1)
                quads(pe, name, step)

            pe.wait_ge(built, BUILT)
            pe.wait_ge(x_loaded, 16 * TT)
            for k in range(KD):
                if k >= 4:
                    pe.wait_ge(turned_out, k - 3)
                for t in range(TT):
                    mm = pe.transpose(bank[k % 4][:, t * P:(t + 1) * P], x_tok[:, t, k * P:(k + 1) * P], ident[:, :])
                mm.then_inc(turned, 1)

            pe.wait_ge(ln_loaded, 32)
            pe.transpose(bank[5][:, 0:64], ln_rows[:, :], ident[0:64, 0:64]).then_inc(turned, 1)

            pe.wait_ge(turned_lo, KD)
            pe.wait_ge(consts, CONSTS)
            pe.wait_ge(turned_out, KD)
            tiles("q0", x_hi, x_lo)
            tiles("k0", x_hi, x_lo, ahead=1)
            values("v0")

            def scores_a(h):
                for g, n in enumerate(reversed(range(TT))):
                    if h:
                        pe.wait_ge(a_ready, TT * (h - 1) + g + 1)
                    for d in range(DT):
                        f = DT * h + d
                        mm = mm3(bank[n][:, 0:WID[n]], k_hi[:, f, n * P:(n + 1) * P], k_lo[:, f, n * P:(n + 1) * P],
                                 q_hi[:, f, n * P:], q_lo[:, f, n * P:], d == 0, d == DT - 1)
                    mm.then_inc(z_done, 1)

            def tails_a(h):
                for g, n in enumerate(reversed(range(TT))):
                    if g == 0:
                        pe.wait_ge(sp_lo_ready, 2 * h + 1)
                    if g == TT - 1:
                        pe.wait_ge(sp_lo_ready, 2 * h + 2)
                    for part in (sp_hi, sp_lo):
                        mm = pe.matmul(bank[n][:, 0:WID[n]], neg_incl[:, :], part[:, OFF[n]:OFF[n] + WID[n]],
                                       start=False, stop=n == TT - 1 and part is sp_lo, skip_group_check=True)
                    for m in range(n + 1, TT):
                        for part in (sp_hi, sp_lo):
                            mm = pe.matmul(bank[n][:, (m - n) * P:WID[n]], neg_ones[:, :],
                                           part[:, OFF[m]:OFF[m] + WID[m]], start=False,
                                           stop=m == TT - 1 and part is sp_lo, skip_group_check=True)
                    mm.then_inc(tail_done, 1)

            def mix_a(h):
                pe.wait_ge(a_lo_ready, 2 * h + 2)
                if h:
                    pe.wait_ge(mix_lo, DT * h)
                for d in range(DT):
                    c = slice(h * DH + d * P, h * DH + (d + 1) * P)
                    for n in range(TT):
                        a = slice(OFF[n], OFF[n] + WID[n])
                        mm = mm3(bank[6 + d][:, n * P:], v_hi[:, n, c], v_lo[:, n, c], a_hi[:, a], a_lo[:, a],
                                 n == 0, n == TT - 1)
                    mm.then_inc(mixed, 1)

            pe.wait_ge(drained, DRAINED["o0"])
            scores_a(0)
            for h in range(H):
                tails_a(h)
                if h + 1 < H:
                    scores_a(h + 1)
                mix_a(h)
            pe.wait_ge(mix_lo, KD)
            tiles("o0", q_hi, q_lo)
            norm(0)
            pe.wait_ge(x_ready, KD)
            tiles("gu", x_hi, x_lo)

            def down_step(q, i, j, last):
                weights(q, j)
                if j % 2 == 0:
                    free_of(DRAINED["down"] + 4 * i + j - 2)
                for k in range(KF // 2):
                    w, kk = slice(k * P, (k + 1) * P), j % 2 * (KF // 2) + k
                    mm = mm3(bank[j // 2][:, :], w_hi[j % 2][:, w], w_lo[j % 2][:, w], h_hi[:, kk, :], h_lo[:, kk, :],
                             kk == 0, kk == KF - 1)
                mm.then_inc(chunk_done, 1)
            pe.wait_ge(drained, DRAINED["down"])
            quads(pe, "down", down_step)
            embed(0)
            norm(1)
            pe.wait_ge(x_ready, 2 * KD)
            tiles("gate0", x_hi, x_lo)
            pe.wait_ge(x_ready, 3 * KD)
            tiles("q1", x_hi, x_lo)
            tiles("k1", x_hi, x_lo, ahead=1)
            values("v1")
            pe.wait_ge(drained, DRAINED["o1"])
            pe.wait_ge(small_loaded, 48)
            for t in range(TT):
                for k in range(KD):
                    mm = pe.matmul(bank[0][:, t * H:(t + 1) * H], x_exact[:, k, t * P:(t + 1) * P], w_f[:, k, :],
                                   start=k == 0, stop=k == KD - 1)
            mm.then_inc(f_done, 1)
            pe.wait_ge(f_step, 3)
            for t in range(TT):
                for m in range(t + 1):
                    mm = pe.matmul(bank[1][:, t * H:(t + 1) * H], (cum if m == t else ones)[:, :], log_f[:, m, :],
                                   start=m == 0, stop=m == t)
            mm.then_inc(c_done, 1)
            for h in range(H):
                pe.wait_ge(diag_ready, h + 1)
                if h >= 2:
                    pe.wait_ge(row_copied, h - 1)
                for t in range(TT):
                    mm = pe.matmul(bank[2 + h % 2][:, t * P:(t + 1) * P], ones[:, :], c_diag[:, t, :], start=True, stop=True)
                mm.then_inc(row_done, 1)

            def scores_b(h):
                for m in range(TT):
                    if h:
                        pe.wait_ge(z2_step, 3 * (TT * (h - 1) + m) + 1)
                    else:
                        pe.wait_ge(row_copied, H)
                    for d in range(DT):
                        f = DT * h + d
                        mm = mm3(bank[m][:, 0:WB[m]], q_hi[:, f, m * P:(m + 1) * P], q_lo[:, f, m * P:(m + 1) * P],
                                 k_hi[:, f, 0:WB[m]], k_lo[:, f, 0:WB[m]], d == 0, d == DT - 1)
                    mm.then_inc(z2_done, 1)

            def turn_b(h):
                for m in range(TT):
                    s = TT * h + m
                    pe.wait_ge(w_ready, s + 1)
                    if s >= 2:
                        pe.wait_ge(wt_ready, s - 1)
                    for n in range(m + 1):
                        mm = pe.transpose(bank[4 + m % 2][:, n * P:(n + 1) * P],
                                          zb[:, OB[m] + n * P:OB[m] + (n + 1) * P], ident[:, :])
                    mm.then_inc(w_turned, 1)

            def mix_b(h):
                pe.wait_ge(wt_ready, TT * (h + 1))
                pe.wait_ge(mix_lo, KD + DT * h)
                for d in range(DT):
                    c = slice(h * DH + d * P, h * DH + (d + 1) * P)
                    for n in range(TT):
                        mm = mm3(bank[6 + d][:, n * P:], v_hi[:, n, c], v_lo[:, n, c], wt_hi[:, n, n * P:], wt_lo[:, n, n * P:],
                                 n == 0, n == TT - 1)
                    mm.then_inc(mixed, 1)

            scores_b(0)
            for h in range(H):
                if h + 1 < H:
                    scores_b(h + 1)
                turn_b(h)
                mix_b(h)
            pe.wait_ge(mix_lo, 2 * KD)
            tiles("o1", q_hi, q_lo)
            norm(2)
            pe.wait_ge(x_ready, 4 * KD)
            for t in range(TT):
                for k in range(KD):
                    mm = pe.matmul(bank[6][:, t * NE:(t + 1) * NE], x_exact[:, k, t * P:(t + 1) * P], w_r[:, k, :],
                                   start=k == 0, stop=k == KD - 1)
            mm.then_inc(router_done, 1)
            q0 = BASE["moe"] // RAW
            with pe.Fori(0, NE) as e:
                for c in range(8):
                    half, up, kh = c // 4, c // 2 % 2, c % 2
                    weights(q0 + 3 * e + c // RAW, c % RAW)
                    if c == 0:
                        pe.wait_ge(acc_ready, 8 * e + TT)
                    if c == 4:
                        pe.wait_ge(silu_ready, 8 * e + TT)
                    if c == 6:
                        pe.wait_ge(he_ready, 8 * e + TT)
                    for t in range(TT):
                        for k in range(4):
                            w, kk = slice(k * FC, (k + 1) * FC), kh * 4 + k
                            mm = mm3(bank[4 * up + t][:, 0:FC], x_hi[:, kk, t * P:(t + 1) * P],
                                     x_lo[:, kk, t * P:(t + 1) * P], w_hi[c % 2][:, w], w_lo[c % 2][:, w],
                                     kk == 0, kk == KD - 1)
                    mm.then_inc(chunk_done, 1)
                pe.wait_ge(he_ready, 8 * e + 2 * TT)
                for t in range(TT):
                    if t >= 2:
                        pe.wait_ge(het_ready, TT * e + t - 1)
                    for k in range(KE):
                        mm = pe.transpose(bank[t % 2 * 2 + k // 4][:, k % 4 * P:(k % 4 + 1) * P],
                                          he[:, t, k * P:(k + 1) * P], ident[:, :])
                    mm.then_inc(he_turned, 1)
                pe.wait_ge(het_ready, TT * e + TT)
                for c in range(4):
                    weights(q0 + 3 * e + 2, c)
                    for t in range(TT):
                        for k in range(3):
                            kk = c % 2 * 3 + k
                            r, w = (FE_LAST if kk == KE - 1 else P), slice(k * 512, (k + 1) * 512)
                            mm = mm3(bank[4 * (1 - c // 2) + t][:, :], het_hi[0:r, kk, t * P:(t + 1) * P],
                                     het_lo[0:r, kk, t * P:(t + 1) * P], w_hi[c % 2][0:r, w], w_lo[c % 2][0:r, w],
                                     kk == 0, kk == KE - 1)
                    mm.then_inc(chunk_done, 1)
            pe.wait_ge(acc_ready, TT + 8 * NE)
            for k in range(KD):
                if k >= 4:
                    pe.wait_ge(drained, DRAINED["turn"] + k - 3)
                for t in range(TT):
                    mm = pe.transpose(bank[k % 4][:, t * P:(t + 1) * P], acc[:, t, k * P:(k + 1) * P], ident[:, :])
                mm.then_inc(acc_turned, 1)
            embed(1)
            norm(3)
            pe.wait_ge(x_ready, 5 * KD)
            tiles("gate1", x_hi, x_lo)
            pe.wait_ge(drained, DRAINED["gate1"] + KD)
            pe.wait_ge(embedded, 2 * KD)
            for t in range(TT):
                for k in range(KD):
                    mm = pe.transpose(bank[2 * t + k // 4][:, k % 4 * P:(k % 4 + 1) * P], x_exact[:, k, t * P:(t + 1) * P],
                                      ident[:, :])
                mm.then_inc(final_turned, 1)

        @block.scalar
        def _(act):
            def split_hi(q, j, n, last64=None):
                act.wait_ge(raw_loaded[j], 16 * (q + 1))
                if not isinstance(q, int) or 4 * q + j >= SPLIT:
                    act.wait_ge(chunk_done, 4 * q + j - 1)
                if last64 is None:
                    act.activation(w_hi[j % 2][:, 0:n], raw[j][:, 0:n], ACT.Copy).then_inc(hi_ready, 1)
                else:
                    act.wait_ge(last_loaded[j // 2], last64)
                    act.activation(w_hi[j % 2][:, 0:1024], raw[j][:, 0:1024], ACT.Copy)
                    act.activation(w_hi[j % 2][0:FE_LAST, 1024:1536], raw[j][0:FE_LAST, 1024:1536], ACT.Copy
                                   ).then_inc(hi_ready, 1)

            def ahead(name, q, j, last):
                n = NEXT_SIZE[name] if last else SIZE[name]
                if n:
                    split_hi(q + (j + 1) // RAW, (j + 1) % RAW, n)

            def tiles_hi(name, dst, scale=1.0):
                def step(q, i, j, last):
                    ahead(name, q, j, last)
                    act.wait_ge(chunk_done, 4 * q + j + 1)
                    act.activation(dst[:, 4 * i + j, :], bank[j][:, :], ACT.Copy, scale=scale).then_inc(out_hi, 1)
                quads(act, name, step, peel=True)

            def values_hi(name):
                def step(q, i, j, last):
                    ahead(name, q, j, last)
                    if j % 2 == 0:
                        return
                    act.wait_ge(chunk_done, 4 * q + j + 1)
                    g = 2 * i + j // 2
                    for t in range(TT):
                        op = act.activation(v_hi[:, t, g * 256:(g + 1) * 256], bank[j // 2 * 4 + t][:, 0:256], ACT.Copy)
                    op.then_inc(out_hi, 2)
                quads(act, name, step, peel=True)

            def sum_hi(n, k):
                act.wait_ge(summed, KD * n + k + 1)
                act.activation(x_hi[:, k, :], x_exact[:, k, :], ACT.Copy).then_inc(y_hi_ready, 1)

            def residual_hi(name, n):
                def step(q, i, j, last):
                    ahead(name, q, j, last)
                    if name != "down":
                        sum_hi(n, 4 * i + j)
                    elif j % 2:
                        sum_hi(n, 2 * i + j // 2)
                quads(act, name, step, peel=True)

            def norm(n):
                for k in range(KD):
                    act.wait_ge(centred, KD * n + k + 1)
                    if k >= 2:
                        act.wait_ge(var_done, KD * n + k - 1)
                    act.activation(sq[k % 2][:, :], x_exact[:, k, :], ACT.Square).then_inc(squared, 1)
                act.wait_ge(var_done, KD * (n + 1))
                act.wait_ge(consts, CONSTS)
                act.activation(rstd[:, :], bank[5][:, :], ACT.Sqrt, bias=eps[:, 0:1]).then_inc(std_ready, 1)
                for k in range(KD):
                    g, b = ln_cols[:, n * KD + k:n * KD + k + 1], ln_cols[:, 32 + n * KD + k:33 + n * KD + k]
                    act.wait_ge(normed, KD * n + k + 1)
                    act.activation(x_hi[:, k, :], x_exact[:, k, :], ACT.Identity, bias=b, scale=g)
                    act.activation(x_exact[:, k, :], x_exact[:, k, :], ACT.Identity, bias=b, scale=g).then_inc(affine, 1)

            def embed(layer):
                name = f"proj{layer}"
                for k in range(KP):
                    act.wait_ge(turned, KD + 1 + KP * layer + k + 1)
                    act.activation(pt_hi[:, k, :], bank[6 + k][:, :], ACT.Copy).then_inc(turned_hi, 1)
                quads(act, name, lambda q, i, j, last: ahead(name, q, j, last))

            def gate(layer, n):
                name = f"gate{layer}"

                def step(q, i, j, last):
                    ahead(name, q, j, last)
                    act.wait_ge(chunk_done, 4 * q + j + 1)
                    act.activation(sig[:, 4 * i + j, :], bank[j][:, :], ACT.Sigmoid).then_inc(gated, 1)
                quads(act, name, step, peel=True)
                if layer == 0:
                    for k in range(KD):
                        act.wait_ge(embedded, k + 1)
                        act.activation(x_hi[:, k, :], x_exact[:, k, :], ACT.Copy).then_inc(affine, 1)

            split_hi(0, 0, SIZE["q0"])
            for k in range(KD):
                act.wait_ge(turned_out, k + 1)
                act.activation(x_hi[:, k, :], x_exact[:, k, :], ACT.Copy).then_inc(turned_hi, 1)
            tiles_hi("q0", q_hi, SCALE)
            tiles_hi("k0", k_hi)
            values_hi("v0")

            act.wait_ge(drained, DRAINED["o0"])
            for h in range(H):
                for g, group in enumerate(((3, 2, 1), (0,))):
                    lo, hi = OFF[group[-1]], OFF[group[0]] + WID[group[0]]
                    if h and g == 0:
                        act.wait_ge(a_lo_ready, 2 * h)
                    for n in group:
                        act.wait_ge(z_done, TT * h + TT - n)
                        op = act.activation(ln_a[:, OFF[n]:OFF[n] + WID[n]], bank[n][:, 0:WID[n]], ACT.Abs)
                    op.then_inc(absed, 1)
                    act.wait_ge(absed, 2 * h + g + 1)
                    act.activation(ln_a[:, lo:hi], ln_a[:, lo:hi], ACT.Exp, scale=-1.0).then_inc(exped, 1)
                    act.wait_ge(exped, 2 * h + g + 1)
                    act.activation(ln_a[:, lo:hi], ln_a[:, lo:hi], ACT.Ln, bias=1.0).then_inc(logged, 1)
                for g, (lo, hi) in enumerate(((OFF[1], TRI), (0, OFF[1]))):
                    act.wait_ge(sp_ready, 2 * h + g + 1)
                    act.activation(sp_hi[:, lo:hi], sp[:, lo:hi], ACT.Copy).then_inc(sp_hi_ready, 1)
                for g, n in enumerate(reversed(range(TT))):
                    act.wait_ge(diag_cut, TT * h + g + 1)
                    op = act.activation(ln_a[:, OFF[n]:OFF[n] + P], a_diag[:, n, :], ACT.Exp)
                    if n < TT - 1:
                        op = act.activation(ln_a[:, OFF[n] + P:OFF[n] + WID[n]], bank[n][:, P:WID[n]], ACT.Exp)
                    op.then_inc(a_ready, 1)
                for d in range(DT):
                    act.wait_ge(mixed, DT * h + d + 1)
                    act.activation(q_hi[:, DT * h + d, :], bank[6 + d][:, :], ACT.Copy).then_inc(mix_hi, 1)
            residual_hi("o0", 0)
            norm(0)

            def gu_step(q, i, j, last):
                ahead("gu", q, j, last)
                if j % 2 == 0:
                    return
                m = 2 * i + j // 2
                act.wait_ge(chunk_done, 4 * q + j + 1)
                act.activation(h_tmp[j // 2][:, :], bank[j - 1][:, :], ACT.Silu).then_inc(gated, 1)
                act.wait_ge(hidden, m + 1)
                act.activation(h_hi[:, m, :], h_tmp[j // 2][:, :], ACT.Copy).then_inc(out_hi, 2)
            quads(act, "gu", gu_step, peel=True)
            residual_hi("down", 1)
            embed(0)
            norm(1)
            gate(0, 1)
            tiles_hi("q1", q_hi, SCALE)
            tiles_hi("k1", k_hi)
            values_hi("v1")

            act.wait_ge(f_step, 1)
            act.activation(f_abs[:, :, :], f_pre[:, :, :], ACT.Abs).then_inc(f_act, 1)
            act.wait_ge(f_act, 1)
            act.activation(f_abs[:, :, :], f_abs[:, :, :], ACT.Exp, scale=-1.0).then_inc(f_act, 1)
            act.wait_ge(f_act, 2)
            act.activation(f_abs[:, :, :], f_abs[:, :, :], ACT.Ln, bias=1.0).then_inc(f_act, 1)
            act.wait_ge(drained, DRAINED["o1"])
            for h in range(H):
                act.wait_ge(row_done, h + 1)
                act.activation(c_row[:, h, :], bank[2 + h % 2][:, :], ACT.Copy).then_inc(row_copied, 1)

            def exps_b(h):
                for m in range(TT):
                    s = TT * h + m
                    act.wait_ge(z2_step, 3 * s + 3)
                    z = zb[:, OB[m]:OB[m] + WB[m]]
                    act.activation(z, z, ACT.Exp, bias=neg_max[:, m:m + 1], accum_out=row_sum[:, m:m + 1]
                                   ).then_inc(e_ready, 1)

            def turned_b(h):
                for m in range(TT):
                    s = TT * h + m
                    act.wait_ge(w_turned, s + 1)
                    if m == 0 and h:
                        act.wait_ge(mixed, KD + DT * h)
                    src = bank[4 + m % 2][:, 0:WB[m]].rearrange("p (n t) -> p n t", t=P)
                    act.activation(wt_hi[:, 0:m + 1, m * P:(m + 1) * P], src, ACT.Copy).then_inc(wt_hi_ready, 1)

            for h in range(H):
                exps_b(h)
                turned_b(h)
                for d in range(DT):
                    act.wait_ge(mixed, KD + DT * h + d + 1)
                    act.activation(q_hi[:, DT * h + d, :], bank[6 + d][:, :], ACT.Copy).then_inc(mix_hi, 1)
            residual_hi("o1", 2)
            norm(2)
            act.wait_ge(route_step, 3)
            act.activation(g_exp[:, :], g_diff[:, :], ACT.Exp).then_inc(gate_exp, 1)

            q0 = BASE["moe"] // RAW

            def expert(e, final):
                for c in range(8):
                    half, up, kh = c // 4, c // 2 % 2, c % 2
                    split_hi(q0 + 3 * e + (c + 1) // RAW, (c + 1) % RAW, 4 * FC if c < 7 else 1536)
                    if up == 0 and kh == 1:
                        act.wait_ge(chunk_done, 4 * q0 + 12 * e + c + 1)
                        for t in range(TT):
                            act.activation(he[:, t, half * FC:(half + 1) * FC], bank[t][:, 0:FC], ACT.Silu
                                           ).then_inc(silu_ready, 1)
                for t in range(TT):
                    act.wait_ge(he_turned, TT * e + t + 1)
                    act.activation(het_hi[:, 0:4, t * P:(t + 1) * P],
                                   bank[t % 2 * 2][:, :].rearrange("p (k t) -> p k t", t=P), ACT.Copy)
                    act.activation(het_hi[:, 4:KE, t * P:(t + 1) * P],
                                   bank[t % 2 * 2 + 1][:, 0:2 * P].rearrange("p (k t) -> p k t", t=P), ACT.Copy
                                   ).then_inc(het_hi_ready, 1)
                for c in range(4):
                    if c < 3:
                        split_hi(q0 + 3 * e + 2, c + 1, 1536, 16 * (e + 1) if c % 2 == 0 else None)
                    elif not final:
                        split_hi(q0 + 3 * e + 3, 0, 4 * FC)
                    else:
                        split_hi(q0 + 3 * e + 3, 0, NEXT_SIZE["moe"])

            with act.Fori(0, NE - 1) as e:
                expert(e, False)
            expert(NE - 1, True)
            for k in range(KD):
                sum_hi(3, k)
            embed(1)
            norm(3)
            gate(1, 3)
            for t in range(TT):
                act.wait_ge(final_turned, t + 1)
                act.activation(o_tok[:, t, 0:512], bank[2 * t][:, :], ACT.Copy).then_inc(final_act, 1)

        @block.vector
        def _(dve):
            def minus(dst, a, b):
                return dve.tensor_tensor(dst, a, b, ALU.subtract)

            def split_lo(q, j, n, last64=False):
                dve.wait_ge(hi_ready, 4 * q + j + 1)
                if last64:
                    minus(w_lo[j % 2][:, 0:1024], raw[j][:, 0:1024], w_hi[j % 2][:, 0:1024].bitcast(F32))
                    minus(w_lo[j % 2][0:FE_LAST, 1024:1536], raw[j][0:FE_LAST, 1024:1536],
                          w_hi[j % 2][0:FE_LAST, 1024:1536].bitcast(F32)).then_inc(lo_ready, 1)
                else:
                    minus(w_lo[j % 2][:, 0:n], raw[j][:, 0:n], w_hi[j % 2][:, 0:n].bitcast(F32)).then_inc(lo_ready, 1)

            def ahead(name, q, j, last):
                n = NEXT_SIZE[name] if last else SIZE[name]
                if n:
                    split_lo(q + (j + 1) // RAW, (j + 1) % RAW, n)

            def low(dst, psum, hi, scale=1.0):
                return dve.scalar_tensor_tensor(out=dst, in0=psum, scalar=scale, in1=hi.bitcast(F32),
                                                op0=ALU.mult, op1=ALU.subtract)

            def tiles_lo(name, hi, lo, scale=1.0):
                def step(q, i, j, last):
                    ahead(name, q, j, last)
                    dve.wait_ge(out_hi, OUT_HI[name] + 4 * i + j + 1)
                    low(lo[:, 4 * i + j, :], bank[j][:, :], hi[:, 4 * i + j, :], scale).then_inc(drained, 1)
                quads(dve, name, step, peel=True)

            def values_lo(name):
                def step(q, i, j, last):
                    ahead(name, q, j, last)
                    if j % 2 == 0:
                        return
                    g = 2 * i + j // 2
                    c = slice(g * 256, (g + 1) * 256)
                    dve.wait_ge(out_hi, OUT_HI[name] + 2 * (g + 1))
                    for t in range(TT):
                        op = low(v_lo[:, t, c], bank[j // 2 * 4 + t][:, 0:256], v_hi[:, t, c])
                    op.then_inc(drained, 2)
                quads(dve, name, step, peel=True)

            def add_residual(n, k, psum):
                dve.scalar_tensor_tensor(out=x_exact[:, k, :], in0=x_exact[:, k, :], scalar=ALPHA, in1=psum,
                                         op0=ALU.mult, op1=ALU.add).then_inc(summed, 1)
                dve.wait_ge(y_hi_ready, KD * n + k + 1)
                return minus(x_lo[:, k, :], x_exact[:, k, :], x_hi[:, k, :].bitcast(F32))

            def residual(name, n):
                def step(q, i, j, last):
                    ahead(name, q, j, last)
                    if name != "down":
                        dve.wait_ge(chunk_done, 4 * q + j + 1)
                        add_residual(n, 4 * i + j, bank[j][:, :]).then_inc(drained, 1)
                    elif j % 2:
                        dve.wait_ge(chunk_done, 4 * q + j + 1)
                        add_residual(n, 2 * i + j // 2, bank[j // 2][:, :]).then_inc(drained, 2)
                quads(dve, name, step, peel=True)

            def norm(n):
                dve.wait_ge(mean_done, n + 1)
                for k in range(KD):
                    minus(x_exact[:, k, :], x_exact[:, k, :], bank[4][:, :]).then_inc(centred, 1)
                dve.wait_ge(std_ready, n + 1)
                dve.reciprocal(rstd[:, :], rstd[:, :]).then_inc(rstd_ready, 1)
                dve.wait_ge(rstd_ready, n + 1)
                dve.wait_ge(squared, KD * (n + 1))
                for k in range(KD):
                    dve.tensor_tensor(x_exact[:, k, :], x_exact[:, k, :], rstd[:, :], ALU.mult).then_inc(normed, 1)
                done = [0, KD, 3 * KD, 4 * KD][n]
                for k in range(KD):
                    dve.wait_ge(affine, done + k + 1)
                    minus(x_lo[:, k, :], x_exact[:, k, :], x_hi[:, k, :].bitcast(F32)).then_inc(x_ready, 1)

            def embed(layer):
                name = f"proj{layer}"
                for k in range(KP):
                    dve.wait_ge(turned_hi, KD + KP * layer + k + 1)
                    low(pt_lo[:, k, :], bank[6 + k][:, :], pt_hi[:, k, :]).then_inc(turned_lo, 1)

                def step(q, i, j, last):
                    ahead(name, q, j, last)
                    dve.wait_ge(chunk_done, 4 * q + j + 1)
                    for s in range(2):
                        op = dve.tensor_copy(proj[:, 2 * j + s, :], bank[j % 2 * 2 + s][:, :])
                    op.then_inc(drained, 1)
                quads(dve, name, step)

            def gate(layer):
                name = f"gate{layer}"

                def step(q, i, j, last):
                    ahead(name, q, j, last)
                    k = 4 * i + j
                    dve.wait_ge(gated, GATED[name] + k + 1)
                    dve.tensor_tensor(proj[:, k, :], proj[:, k, :], sig[:, k, :], ALU.mult).then_inc(drained, 1)
                    dve.wait_ge(drained, DRAINED[name] + k + 1)
                    dve.tensor_tensor(x_exact[:, k, :], x_exact[:, k, :], proj[:, k, :], ALU.add).then_inc(embedded, 1)
                quads(dve, name, step)
                if layer == 0:
                    for k in range(KD):
                        dve.wait_ge(affine, 2 * KD + k + 1)
                        minus(x_lo[:, k, :], x_exact[:, k, :], x_hi[:, k, :].bitcast(F32)).then_inc(x_ready, 1)

            dve.wait_ge(built, BUILT)
            dve.memset(eps[:, :], EPS)
            dve.tensor_scalar(neg_ones[:, :], ones[:, :], -1.0, None, ALU.mult)
            dve.tensor_copy(mean_r[:, :], mean_f[:, :])
            dve.tensor_copy(neg_incl[:, :], neg_incl_f[:, :]).then_inc(consts, 1)
            split_lo(0, 0, SIZE["q0"])
            for k in range(KD):
                dve.wait_ge(turned, k + 1)
                dve.tensor_copy(x_exact[:, k, :], bank[k % 4][:, :]).then_inc(turned_out, 1)
            for k in range(KD):
                dve.wait_ge(turned_hi, k + 1)
                minus(x_lo[:, k, :], x_exact[:, k, :], x_hi[:, k, :].bitcast(F32)).then_inc(turned_lo, 1)
            dve.wait_ge(turned, KD + 1)
            dve.tensor_copy(ln_cols[:, :], bank[5][:, 0:64]).then_inc(consts, 1)
            tiles_lo("q0", q_hi, q_lo, SCALE)
            tiles_lo("k0", k_hi, k_lo)
            values_lo("v0")

            for h in range(H):
                for g, group in enumerate(((3, 2, 1), (0,))):
                    lo, hi = OFF[group[-1]], OFF[group[0]] + WID[group[0]]
                    dve.wait_ge(logged, 2 * h + g + 1)
                    for n in group:
                        o = slice(OFF[n], OFF[n] + WID[n])
                        op = dve.scalar_tensor_tensor(out=sp[:, o], in0=bank[n][:, 0:WID[n]], scalar=0.0, in1=ln_a[:, o],
                                                      op0=ALU.max, op1=ALU.add)
                    op.then_inc(sp_raw, 1)
                    dve.wait_ge(sp_raw, 2 * h + g + 1)
                    for n in group:
                        o = slice(OFF[n], OFF[n] + P)
                        op = dve.tensor_tensor(sp[:, o], sp[:, o], keep[:, :], ALU.mult)
                    op.then_inc(sp_ready, 1)
                for g, (lo, hi) in enumerate(((OFF[1], TRI), (0, OFF[1]))):
                    dve.wait_ge(sp_hi_ready, 2 * h + g + 1)
                    minus(sp_lo[:, lo:hi], sp[:, lo:hi], sp_hi[:, lo:hi].bitcast(F32)).then_inc(sp_lo_ready, 1)
                for g, n in enumerate(reversed(range(TT))):
                    dve.wait_ge(tail_done, TT * h + g + 1)
                    dve.tensor_tensor(a_diag[:, n, :], bank[n][:, 0:P], floor_a[:, :], ALU.min).then_inc(diag_cut, 1)
                if h:
                    dve.wait_ge(mixed, DT * h)
                for g, (lo, hi) in enumerate(((OFF[1], TRI), (0, OFF[1]))):
                    dve.wait_ge(a_ready, TT * h + (TT - 1, TT)[g])
                    dve.tensor_copy(a_hi[:, lo:hi], ln_a[:, lo:hi]).then_inc(a_hi_ready, 1)
                    dve.wait_ge(a_hi_ready, 2 * h + g + 1)
                    minus(a_lo[:, lo:hi], ln_a[:, lo:hi], a_hi[:, lo:hi].bitcast(F32)).then_inc(a_lo_ready, 1)
                for d in range(DT):
                    dve.wait_ge(mix_hi, DT * h + d + 1)
                    low(q_lo[:, DT * h + d, :], bank[6 + d][:, :], q_hi[:, DT * h + d, :]).then_inc(mix_lo, 1)
            residual("o0", 0)
            norm(0)

            def gu_step(q, i, j, last):
                ahead("gu", q, j, last)
                if j % 2 == 0:
                    return
                m, t = 2 * i + j // 2, h_tmp[j // 2]
                dve.wait_ge(gated, m + 1)
                dve.tensor_tensor(t[:, :], t[:, :], bank[j][:, :], ALU.mult).then_inc(hidden, 1)
                dve.wait_ge(out_hi, OUT_HI["gu"] + 2 * (m + 1))
                minus(h_lo[:, m, :], t[:, :], h_hi[:, m, :].bitcast(F32)).then_inc(drained, 2)
            quads(dve, "gu", gu_step, peel=True)
            residual("down", 1)
            embed(0)
            norm(1)
            gate(0)
            tiles_lo("q1", q_hi, q_lo, SCALE)
            tiles_lo("k1", k_hi, k_lo)
            values_lo("v1")

            dve.wait_ge(f_done, 1)
            dve.wait_ge(small_loaded, 48)
            for t in range(TT):
                op = dve.tensor_tensor(f_pre[:, t, :], bank[0][:, t * H:(t + 1) * H], b_f[:, :], ALU.add)
            op.then_inc(f_step, 1)
            dve.wait_ge(f_act, 1)
            dve.tensor_scalar(f_pre[:, :, :], f_pre[:, :, :], 0.0, None, ALU.min).then_inc(f_step, 1)
            dve.wait_ge(f_step, 2)
            dve.wait_ge(f_act, 3)
            minus(log_f[:, :, :], f_pre[:, :, :], f_abs[:, :, :]).then_inc(f_step, 1)
            dve.wait_ge(c_done, 1)
            dve.tensor_copy(c_col[:, :, :], bank[1][:, 0:TT * H].rearrange("p (t h) -> p t h", h=H)).then_inc(c_copied, 1)
            dve.wait_ge(c_copied, 1)
            for h in range(H):
                if h:
                    dve.wait_ge(row_done, h)
                for t in range(TT):
                    op = dve.tensor_scalar(c_diag[:, t, :], ident[:, :], c_col[:, t, h:h + 1], None, ALU.mult)
                op.then_inc(diag_ready, 1)
            dve.wait_ge(row_copied, H)

            def scores_b(h):
                for m in range(TT):
                    s = TT * h + m
                    z, d = zb[:, OB[m]:OB[m] + WB[m]], zb[:, OB[m] + m * P:OB[m] + WB[m]]
                    dve.wait_ge(z2_done, s + 1)
                    if h:
                        dve.wait_ge(w_turned, TT * (h - 1) + m + 1)
                    dve.scalar_tensor_tensor(out=z, in0=bank[m][:, 0:WB[m]], scalar=c_col[:, m, h:h + 1],
                                             in1=c_row[:, h, 0:WB[m]], op0=ALU.add, op1=ALU.subtract).then_inc(z2_step, 1)
                    dve.wait_ge(z2_step, 3 * s + 1)
                    dve.tensor_tensor(d, d, clip_b[:, :], ALU.min).then_inc(z2_step, 1)
                    dve.wait_ge(z2_step, 3 * s + 2)
                    dve.tensor_reduce(neg_max[:, m:m + 1], z, AX.X, ALU.max, negate=True).then_inc(z2_step, 1)

            def weights_b(h):
                for m in range(TT):
                    s = TT * h + m
                    z = zb[:, OB[m]:OB[m] + WB[m]]
                    dve.wait_ge(e_ready, s + 1)
                    dve.reciprocal(row_inv[:, m:m + 1], row_sum[:, m:m + 1]).then_inc(inv_ready, 1)
                    dve.wait_ge(inv_ready, s + 1)
                    dve.tensor_scalar(z, z, row_inv[:, m:m + 1], None, ALU.mult).then_inc(w_ready, 1)

            for h in range(H):
                scores_b(h)
                weights_b(h)
                for m in range(TT):
                    s = TT * h + m
                    dve.wait_ge(wt_hi_ready, s + 1)
                    src = bank[4 + m % 2][:, 0:WB[m]].rearrange("p (n t) -> p n t", t=P)
                    low(wt_lo[:, 0:m + 1, m * P:(m + 1) * P], src, wt_hi[:, 0:m + 1, m * P:(m + 1) * P]).then_inc(wt_ready, 1)
                for d in range(DT):
                    dve.wait_ge(mix_hi, KD + DT * h + d + 1)
                    low(q_lo[:, DT * h + d, :], bank[6 + d][:, :], q_hi[:, DT * h + d, :]).then_inc(mix_lo, 1)
            residual("o1", 2)
            norm(2)

            dve.wait_ge(router_done, 1)
            dve.tensor_copy(logits[:, :, :], bank[6][:, 0:TT * NE].rearrange("p (t e) -> p t e", e=NE)).then_inc(route_step, 1)
            dve.wait_ge(route_step, 1)
            for t in range(TT):
                op = dve.max(top[:, t, :], logits[:, t, :])
            op.then_inc(route_step, 1)
            dve.wait_ge(route_step, 2)
            minus(g_diff[:, :], top[:, :, 1], top[:, :, 0]).then_inc(route_step, 1)
            for t in range(TT):
                op = dve.max_index(top_at[:, t, :], top[:, t, :], logits[:, t, :])
            op.then_inc(route_step, 1)
            dve.wait_ge(route_step, 4)
            dve.tensor_copy(top_f[:, :, :], top_at[:, :, 0:2]).then_inc(route_step, 1)
            dve.wait_ge(gate_exp, 1)
            dve.tensor_scalar(g_sum[:, :], g_exp[:, :], 1.0, None, ALU.add).then_inc(route_step, 1)
            dve.wait_ge(route_step, 6)
            dve.reciprocal(g_one[:, :], g_sum[:, :]).then_inc(route_step, 1)
            dve.wait_ge(route_step, 7)
            dve.tensor_tensor(g_two[:, :], g_exp[:, :], g_one[:, :], ALU.mult).then_inc(route_step, 1)
            dve.wait_ge(route_step, 8)
            for t in range(TT):
                dve.tensor_scalar(gates_a[:, t, :], lanes[:, :], top_f[:, t, 0:1], g_one[:, t:t + 1], ALU.is_equal, ALU.mult)
                op = dve.tensor_scalar(gates_b[:, t, :], lanes[:, :], top_f[:, t, 1:2], g_two[:, t:t + 1],
                                       ALU.is_equal, ALU.mult)
            op.then_inc(route_step, 1)
            dve.wait_ge(route_step, 9)
            dve.tensor_tensor(gates[:, :, :], gates_a[:, :, :], gates_b[:, :, :], ALU.add).then_inc(gates_ready, 1)
            dve.wait_ge(gates_ready, 1)

            q0 = BASE["moe"] // RAW
            for t in range(TT):
                dve.memset(he[:, t, FE:], 0.0)
                dve.memset(acc[:, t, :], 0.0).then_inc(acc_ready, 1)

            def expert(e, final):
                for c in range(8):
                    half, up, kh = c // 4, c // 2 % 2, c % 2
                    split_lo(q0 + 3 * e + (c + 1) // RAW, (c + 1) % RAW, 4 * FC if c < 7 else 1536)
                    if up == 1 and kh == 1:
                        dve.wait_ge(chunk_done, 4 * q0 + 12 * e + c + 1)
                        for t in range(TT):
                            o = he[:, t, half * FC:(half + 1) * FC]
                            dve.wait_ge(silu_ready, 8 * e + half * TT + t + 1)
                            dve.tensor_tensor(o, o, bank[4 + t][:, 0:FC], ALU.mult).then_inc(he_ready, 1)
                for t in range(TT):
                    dve.wait_ge(het_hi_ready, TT * e + t + 1)
                    b = bank[t % 2 * 2]
                    s = slice(t * P, (t + 1) * P)
                    low(het_lo[:, 0:4, s], b[:, :].rearrange("p (k t) -> p k t", t=P), het_hi[:, 0:4, s])
                    b = bank[t % 2 * 2 + 1]
                    low(het_lo[:, 4:KE, s], b[:, 0:2 * P].rearrange("p (k t) -> p k t", t=P), het_hi[:, 4:KE, s]
                        ).then_inc(het_ready, 1)
                for c in range(4):
                    if c < 3:
                        split_lo(q0 + 3 * e + 2, c + 1, 1536, c % 2 == 0)
                    else:
                        split_lo(q0 + 3 * e + 3, 0, NEXT_SIZE["moe"] if final else 4 * FC)
                    if c % 2:
                        dve.wait_ge(chunk_done, 4 * q0 + 12 * e + 8 + c + 1)
                        dve.wait_ge(acc_ready, 8 * e + TT)
                        for t in range(TT):
                            o = acc[:, t, c // 2 * 512:(c // 2 + 1) * 512]
                            dve.scalar_tensor_tensor(out=o, in0=bank[4 * (1 - c // 2) + t][:, :],
                                                     scalar=gates[:, t, bass.ds(e, 1)], in1=o, op0=ALU.mult, op1=ALU.add
                                                     ).then_inc(acc_ready, 1)

            with dve.Fori(0, NE - 1) as e:
                expert(e, False)
            expert(NE - 1, True)
            for k in range(KD):
                dve.wait_ge(acc_turned, k + 1)
                add_residual(3, k, bank[k % 4][:, :]).then_inc(drained, 1)
            embed(1)
            norm(3)
            gate(1)
            for t in range(TT):
                dve.wait_ge(final_turned, t + 1)
                dve.tensor_copy(o_tok[:, t, 512:1024], bank[2 * t + 1][:, :]).then_inc(final_dve, 1)


_INS = ["x", "p", "a_w_qkv", "a_w_o", "kvf_w", "kvf_b_f", "b_w_q", "b_w_o", "ffn_w_gu", "ffn_w_down",
        "moe_w_router", "moe_w_gu", "moe_w_down", "ple_w_proj", "ple_w_gate", "ln_g", "ln_b"]


def kernel(**inputs):
    import numpy as np
    import concourse.bacc as bacc
    from concourse.bass_utils import run_bass_kernel_spmd

    nc = bacc.Bacc("TRN2", target_bir_lowering=False, num_devices=1)
    arrays, args = {}, []
    for name in _INS:
        a = np.ascontiguousarray(inputs[name])
        arrays[name] = a
        args.append(nc.dram_tensor(name, a.shape, mybir.dt.from_np(a.dtype), kind="ExternalInput").ap())
    args.append(nc.dram_tensor("result", (1, SEQ, D), F32, kind="ExternalOutput").ap())
    build(nc, *args)
    return run_bass_kernel_spmd(nc, [arrays], core_ids=[0]).results[0]["result"]
```

```python
from contextlib import ExitStack

import concourse.bass as bass
from concourse import mybir

F32 = mybir.dt.float32
R32 = mybir.dt.float32r
U32 = mybir.dt.uint32
I32 = mybir.dt.int32
ACT = mybir.ActivationFunctionType
ALU = mybir.AluOpType
AX = mybir.AxisListType

P = 128
SEQ = 512
D = 1024
KD = D // P
TT = SEQ // P
H = 4
DH = D // H
DT = DH // P
FF = 2816
KF = FF // P
NE = 8
FE = 704
FC = FE // 2
KE = -(-FE // P)
FE_LAST = FE - (KE - 1) * P
PD = 256
KP = PD // P
DEPTH = 2
ALPHA = (2.0 * DEPTH) ** 0.25
SCALE = 1.0 / float(DH) ** 0.5
EPS = 1e-5
NEG = -1e30
BIG = 3e38

RAW = 4
SPLIT = 2
CH = 1536

WID = [SEQ - n * P for n in range(TT)]
OFF = [sum(WID[:n]) for n in range(TT)]
TRI = sum(WID)

PHASES = [
    ("q0", 8, KD * P), ("k0", 8, KD * P), ("v0", 8, 4 * 256), ("o0", 8, KD * P),
    ("gu", 2 * KF, KD * P), ("down", 16, KF // 2 * P), ("proj0", 4, KP * 256), ("gate0", 8, KD * P),
    ("q1", 8, KD * P), ("k1", 8, KD * P), ("v1", 8, 4 * 256), ("o1", 8, KD * P),
    ("proj1", 4, KP * 256), ("moe", NE * 12, 4 * FC), ("gate1", 8, KD * P),
]
BASE, SIZE, COUNT, NEXT_SIZE = {}, {}, {}, {}
_at = 0
for _n, (_name, _count, _size) in enumerate(PHASES):
    BASE[_name], SIZE[_name], COUNT[_name] = _at, _size, _count
    NEXT_SIZE[_name] = PHASES[_n + 1][2] if _n + 1 < len(PHASES) else 0
    _at += _count
CHUNKS = _at
assert all(b % RAW == 0 for b in BASE.values())

SLOT_TILES = (NE + 1) * TT


def by_tiles(eng, count, body):
    with eng.If(count < 2):
        body(1)
    with eng.Else():
        with eng.If(count < 3):
            body(2)
        with eng.Else():
            with eng.If(count < 4):
                body(3)
            with eng.Else():
                body(4)


def share(t, n):
    return 1 if t < n - 1 else TT - n + 1


DRAINED, _n = {}, 0
for _name in ("q0", "k0", "v0", "o0", "gu", "down", "proj0", "gate0", "q1", "k1", "v1", "o1", "proj1", "turn", "gate1"):
    DRAINED[_name] = _n
    _n += COUNT.get(_name, KD)
OUT_HI, _n = {}, 0
for _name in ("q0", "k0", "v0", "gu", "q1", "k1", "v1"):
    OUT_HI[_name] = _n
    _n += COUNT[_name]
GATED = {"gu": 0, "gate0": KF, "gate1": KF + KD}


def quads(eng, name, step, peel=False):
    first, rounds = BASE[name] // RAW, COUNT[name] // RAW
    looped = rounds - 1 if peel else rounds
    if looped > 2:
        with eng.Fori(0, looped) as i:
            for j in range(RAW):
                step(first + i, i, j, False)
        done = looped
    else:
        done = 0
    for i in range(done, rounds):
        for j in range(RAW):
            step(first + i, i, j, i == rounds - 1 and j == RAW - 1)


def build(nc, x, p, a_w_qkv, a_w_o, kvf_w, kvf_b_f, b_w_q, b_w_o, ffn_w_gu, ffn_w_down,
          moe_w_router, moe_w_gu, moe_w_down, ple_w_proj, ple_w_gate, ln_g, ln_b, out):
    with ExitStack() as ctx:
        base = (nc.sbuf_base + 63) // 64 * 64
        place = [base]

        def at(name, shape, dt, offset):
            return nc.alloc_sbuf_tensor_at(name, shape, dt, offset=offset)

        def sb(name, shape, dt=F32):
            n = 4
            for s in shape[1:]:
                n *= s
            t = at(name, shape, dt, place[0])
            place[0] += (n + 31) // 32 * 32
            return t

        def sem(name):
            return ctx.enter_context(nc.semaphore(name))

        x_exact = sb("x_exact", [P, KD, SEQ])
        work0 = place[0]
        x_hi = sb("x_hi", [P, KD, SEQ], R32)
        x_lo = sb("x_lo", [P, KD, SEQ], R32)
        raw = [sb(f"raw{i}", [P, CH]) for i in range(RAW)]
        w_hi = [sb(f"w_hi{i}", [P, CH], R32) for i in range(SPLIT)]
        w_lo = [sb(f"w_lo{i}", [P, CH], R32) for i in range(SPLIT)]
        ident = sb("ident", [P, P])
        ones = sb("ones", [P, P])
        mean_f = sb("mean_f", [P, P])
        mean_r = sb("mean_r", [P, P], R32)
        neg_ones = sb("neg_ones", [P, P], R32)
        neg_incl = sb("neg_incl", [P, P], R32)
        cum = sb("cum", [P, P])
        keep = sb("keep", [P, P])
        floor_a = sb("floor_a", [P, P])
        clip_b = sb("clip_b", [P, P])
        ln_rows = sb("ln_rows", [64, P])
        ln_cols = sb("ln_cols", [P, 64])
        w_f = sb("w_f", [P, KD, H])
        w_r = sb("w_r", [P, KD, NE])
        b_f = sb("b_f", [P, H])
        p_tok = sb("p_tok", [P, TT, PD])
        h_tmp = [sb(f"h_tmp{i}", [P, SEQ]) for i in range(2)]
        eps = sb("eps", [P, 1])
        log_f = sb("log_f", [P, TT, H])
        f_abs = sb("f_abs", [P, TT, H])
        f_pre = sb("f_pre", [P, TT, H])
        c_col = sb("c_col", [P, TT, H])
        neg_max = sb("neg_max", [P, TT])
        row_sum = sb("row_sum", [P, TT])
        row_inv = sb("row_inv", [P, TT])
        logits = sb("logits", [P, TT, NE])
        top = sb("top", [P, TT, NE])
        top_at = sb("top_at", [P, TT, NE], U32)
        top_f = sb("top_f", [P, TT, 2])
        g_diff = sb("g_diff", [P, TT])
        g_exp = sb("g_exp", [P, TT])
        g_sum = sb("g_sum", [P, TT])
        g_one = sb("g_one", [P, TT])
        g_two = sb("g_two", [P, TT])
        lanes = sb("lanes", [P, NE])
        lane_slots = sb("lane_slots", [P, NE])
        slot_f = sb("slot_f", [P, 2, TT])
        slot_i = sb("slot_i", [P, 2, TT], I32)
        tiles_f = [sb(f"tiles_f{i}", [P, NE + 1]) for i in range(2)]
        tiles_i = sb("tiles_i", [P, NE + 1], I32)
        place_f = sb("place_f", [P, 2, TT])
        gather_i = sb("gather_i", [P, TT], I32)
        store_i = sb("store_i", [P, TT], I32)
        place_i = sb("place_i", [P, SLOT_TILES], I32)
        token_i = sb("token_i", [P, SLOT_TILES], I32)
        G = (place[0] + 63) // 64 * 64
        KB = 1024
        assert G + 96 * KB <= nc.sbuf_usable_end, (G, nc.sbuf_usable_end)

        x_tok = at("x_tok", [P, TT, D], F32, G)
        neg_incl_f = at("neg_incl_f", [P, P], F32, G + 92 * KB)
        q_hi = at("q_hi", [P, KD, SEQ], R32, G)
        q_lo = at("q_lo", [P, KD, SEQ], R32, G + 16 * KB)
        k_hi = at("k_hi", [P, KD, SEQ], R32, G + 32 * KB)
        k_lo = at("k_lo", [P, KD, SEQ], R32, G + 48 * KB)
        v_hi = at("v_hi", [P, TT, D], R32, G + 64 * KB)
        v_lo = at("v_lo", [P, TT, D], R32, G + 80 * KB)
        h_hi = at("h_hi", [P, KF, SEQ], R32, G)
        h_lo = at("h_lo", [P, KF, SEQ], R32, G + 44 * KB)
        proj = at("proj", [P, KD, SEQ], F32, G)
        sig = at("sig", [P, KD, SEQ], F32, G + 16 * KB)
        pt_hi = at("pt_hi", [P, KP, SEQ], R32, G + 88 * KB)
        pt_lo = at("pt_lo", [P, KP, SEQ], R32, G + 92 * KB)
        sq = [at(f"sq{i}", [P, SEQ], F32, G + (64 + 2 * i) * KB) for i in range(2)]
        rstd = at("rstd", [P, SEQ], F32, G + 68 * KB)
        he = at("he", [P, TT, KE * P], F32, G + 16 * KB)
        het_hi = at("het_hi", [P, KE, SEQ], R32, G + 28 * KB)
        het_lo = at("het_lo", [P, KE, SEQ], R32, G + 40 * KB)
        xg = at("xg", [P, TT, D], F32, G + 52 * KB)
        x_rows = at("x_rows", [P, TT, D], F32, G + 68 * KB)
        y_tok = at("y_tok", [P, TT, D], F32, G + 68 * KB)
        sel = at("sel", [P, 2, TT, NE], F32, G + 84 * KB)
        sel_any = at("sel_any", [P, TT, NE], F32, G + 84 * KB + 256)
        slot_all = at("slot_all", [P, TT, NE], F32, G + 84 * KB + 384)
        list_rows = at("list_rows", [SLOT_TILES, P], F32, G + 84 * KB + 512)
        place_c = at("place_c", [P, SLOT_TILES], F32, G + 85 * KB + 256)
        past = [at(f"past{i}", [P, SLOT_TILES], F32, G + 85 * KB + 512 + 256 * i) for i in range(2)]
        y_one = at("y_one", [P, TT, D], F32, G + 16 * KB)
        y_two = at("y_two", [P, TT, D], F32, G + 32 * KB)
        o_tok = at("o_tok", [P, TT, D], F32, G)

        wk = lambda name, shape, dt, o: at(name, shape, dt, work0 + o)
        ln_a = wk("ln_a", [P, TRI], F32, 0)
        sp = wk("sp", [P, TRI], F32, 5 * KB)
        sp_hi = wk("sp_hi", [P, TRI], R32, 10 * KB)
        sp_lo = wk("sp_lo", [P, TRI], R32, 15 * KB)
        a_hi = wk("a_hi", [P, TRI], R32, 20 * KB)
        a_lo = wk("a_lo", [P, TRI], R32, 25 * KB)
        a_diag = wk("a_diag", [P, TT, P], F32, 30 * KB)
        zb = wk("zb", [P, TRI], F32, 0)
        wt_hi = wk("wt_hi", [P, TT, SEQ], R32, 5 * KB)
        wt_lo = wk("wt_lo", [P, TT, SEQ], R32, 13 * KB)
        c_row = wk("c_row", [P, H, SEQ], F32, 21 * KB)
        c_diag = wk("c_diag", [P, TT, P], F32, 29 * KB)
        WB = [(m + 1) * P for m in range(TT)]
        OB = [sum(WB[:m]) for m in range(TT)]

        bank = [ctx.enter_context(nc.psum_tensor(f"bank{i}", [P, 512], F32)) for i in range(8)]

        place_of = nc.dram_tensor("place_of", (SLOT_TILES * P, 1), F32, kind="Internal").ap()
        x_dram = nc.dram_tensor("x_dram", (SEQ, D), F32, kind="Internal").ap()
        y_dram = nc.dram_tensor("y_dram", (2 * SEQ + P, D), F32, kind="Internal").ap()

        raw_loaded = [sem(f"raw_loaded{i}") for i in range(RAW)]
        last_loaded = [sem(f"last_loaded{i}") for i in range(2)]
        small_loaded = sem("small_loaded")
        ln_loaded = sem("ln_loaded")
        x_loaded = sem("x_loaded")
        p_loaded = sem("p_loaded")
        out_stored = sem("out_stored")
        hi_ready = sem("hi_ready")
        lo_ready = sem("lo_ready")
        chunk_done = sem("chunk_done")
        drained = sem("drained")
        out_hi = sem("out_hi")
        gated = sem("gated")
        hidden = sem("hidden")
        built = sem("built")
        consts = sem("consts")
        turned = sem("turned")
        turned_out = sem("turned_out")
        turned_hi = sem("turned_hi")
        turned_lo = sem("turned_lo")
        summed = sem("summed")
        y_hi_ready = sem("y_hi_ready")
        mean_done = sem("mean_done")
        centred = sem("centred")
        squared = sem("squared")
        var_done = sem("var_done")
        std_ready = sem("std_ready")
        rstd_ready = sem("rstd_ready")
        normed = sem("normed")
        affine = sem("affine")
        x_ready = sem("x_ready")
        embedded = sem("embedded")
        ple_step = sem("ple_step")
        z_done = sem("z_done")
        absed = sem("absed")
        exped = sem("exped")
        logged = sem("logged")
        sp_raw = sem("sp_raw")
        sp_ready = sem("sp_ready")
        sp_hi_ready = sem("sp_hi_ready")
        sp_lo_ready = sem("sp_lo_ready")
        tail_done = sem("tail_done")
        diag_cut = sem("diag_cut")
        a_ready = sem("a_ready")
        a_hi_ready = sem("a_hi_ready")
        a_lo_ready = sem("a_lo_ready")
        mixed = sem("mixed")
        mix_hi = sem("mix_hi")
        mix_lo = sem("mix_lo")
        f_done = sem("f_done")
        f_step = sem("f_step")
        f_act = sem("f_act")
        c_done = sem("c_done")
        c_copied = sem("c_copied")
        diag_ready = sem("diag_ready")
        row_done = sem("row_done")
        row_copied = sem("row_copied")
        z2_done = sem("z2_done")
        z2_step = sem("z2_step")
        e_ready = sem("e_ready")
        inv_ready = sem("inv_ready")
        w_ready = sem("w_ready")
        w_turned = sem("w_turned")
        wt_hi_ready = sem("wt_hi_ready")
        wt_ready = sem("wt_ready")
        router_done = sem("router_done")
        route_step = sem("route_step")
        gate_exp = sem("gate_exp")
        gate_step = sem("gate_step")
        slot_step = sem("slot_step")
        ranked = sem("ranked")
        slots_ready = sem("slots_ready")
        tiles_ready = sem("tiles_ready")
        rows_turned = sem("rows_turned")
        rows_copied = sem("rows_copied")
        list_cleared = sem("list_cleared")
        listed = sem("listed")
        list_loaded = sem("list_loaded")
        list_turned = sem("list_turned")
        list_step = sem("list_step")
        list_ready = sem("list_ready")
        indexed = sem("indexed")
        xg_loaded = sem("xg_loaded")
        xg_turned = sem("xg_turned")
        xg_hi_ready = sem("xg_hi_ready")
        xg_ready = sem("xg_ready")
        silu_ready = sem("silu_ready")
        he_ready = sem("he_ready")
        he_turned = sem("he_turned")
        het_hi_ready = sem("het_hi_ready")
        het_ready = sem("het_ready")
        banks_out = sem("banks_out")
        y_stored = sem("y_stored")
        y_loaded = [sem(f"y_loaded{t}") for t in range(TT)]
        y_step = sem("y_step")
        combined = sem("combined")
        acc_turned = sem("acc_turned")
        final_turned = sem("final_turned")
        final_dve = sem("final_dve")
        final_act = sem("final_act")

        def cols(w, c, n=P):
            return w.rearrange("(k p) n -> p k n", p=P)[:, :, bass.ds(c, n)]

        def view(slot, k):
            return raw[slot][:, :].rearrange("p (k n) -> p k n", k=k)

        def flat(slot, k, n):
            return raw[slot][:, 0:k * n].rearrange("p (k n) -> p k n", k=k)

        BUILT = 8
        CONSTS = 2
        block = ctx.enter_context(nc.Block())

        @block.sync
        def _(sp_eng):
            xr = x.rearrange("b (t p) d -> (b p) t d", p=P)
            for t in range(TT):
                sp_eng.dma_start(x_tok[:, t, :], xr[:, t, :]).then_inc(x_loaded, 16)

            sp_eng.dma_start(ln_rows[0:32, :], ln_g.rearrange("l w (k p) -> (l w k) p", p=P)).then_inc(ln_loaded, 16)
            sp_eng.dma_start(ln_rows[32:64, :], ln_b.rearrange("l w (k p) -> (l w k) p", p=P)).then_inc(ln_loaded, 16)

            def slot_free(q, j):
                sp_eng.wait_ge(lo_ready, 4 * q + j - RAW + 1)

            def from_cols(w, col0, k=KD, n=P):
                def step(q, i, j, last):
                    if not isinstance(q, int) or q > 0:
                        slot_free(q, j)
                    sp_eng.dma_start(flat(j, k, n), cols(w, col0 + (RAW * i + j) * n, n)).then_inc(raw_loaded[j], 16)
                return step

            def v_step(w, col0):
                wv = w.rearrange("(g k p) n -> g p k n", p=P, g=2)

                def step(q, i, j, last):
                    slot_free(q, j)
                    sp_eng.dma_start(flat(j, 4, 256), wv[j % 2][:, :, bass.ds(col0 + (2 * i + j // 2) * 256, 256)]
                                     ).then_inc(raw_loaded[j], 16)
                return step

            def gu_step(q, i, j, last):
                slot_free(q, j)
                sp_eng.dma_start(flat(j, KD, P), cols(ffn_w_gu[0], (2 * i + j // 2) * P + (j % 2) * FF)
                                 ).then_inc(raw_loaded[j], 16)

            def down_step(q, i, j, last):
                wd = ffn_w_down[0].rearrange("(g k p) n -> g p k n", p=P, g=2)
                slot_free(q, j)
                sp_eng.dma_start(flat(j, KF // 2, P), wd[j % 2][:, :, bass.ds((2 * i + j // 2) * P, P)]
                                 ).then_inc(raw_loaded[j], 16)

            def load_small():
                sp_eng.dma_start(w_f[:, :, :], cols(kvf_w, 2 * D, H)).then_inc(small_loaded, 16)
                sp_eng.dma_start(w_r[:, :, :], cols(moe_w_router[0], 0, NE)).then_inc(small_loaded, 16)
                sp_eng.dma_start(b_f[:, :], kvf_b_f.rearrange("(a h) -> a h", a=1).to_broadcast([P, H])).then_inc(small_loaded, 16)

            def load_p(layer):
                if layer:
                    sp_eng.wait_ge(turned, KD + KP + 1)
                sp_eng.dma_start(p_tok[:, :, :], p[layer].rearrange("b (t p) d -> (b p) t d", p=P)).then_inc(p_loaded, 16)

            quads(sp_eng, "q0", from_cols(a_w_qkv[0], 0))
            load_small()
            load_p(0)
            quads(sp_eng, "k0", from_cols(a_w_qkv[0], D))
            quads(sp_eng, "v0", v_step(a_w_qkv[0], 2 * D))
            quads(sp_eng, "o0", from_cols(a_w_o[0], 0))
            quads(sp_eng, "gu", gu_step)
            quads(sp_eng, "down", down_step)
            quads(sp_eng, "proj0", from_cols(ple_w_proj[0], 0, KP, 256))
            quads(sp_eng, "gate0", from_cols(ple_w_gate[0], 0))
            load_p(1)
            quads(sp_eng, "q1", from_cols(b_w_q[0], 0))
            quads(sp_eng, "k1", from_cols(kvf_w, 0))
            quads(sp_eng, "v1", v_step(kvf_w, D))
            quads(sp_eng, "o1", from_cols(b_w_o[0], 0))
            quads(sp_eng, "proj1", from_cols(ple_w_proj[1], 0, KP, 256))
            q0 = BASE["moe"] // RAW
            with sp_eng.Fori(0, NE) as e:
                for c in range(8):
                    half, up, kh = c // 4, c // 2 % 2, c % 2
                    col = up * FE + half * FC
                    src = moe_w_gu[0][bass.ds(e, 1), kh * 4 * P:(kh + 1) * 4 * P, col:col + FC]
                    slot_free(q0 + 3 * e + c // RAW, c % RAW)
                    sp_eng.dma_start(flat(c % RAW, 4, FC), src.rearrange("e (k p) n -> p (e k) n", p=P)
                                     ).then_inc(raw_loaded[c % RAW], 16)
                for c in range(4):
                    full, r0, col = (3, 2)[c % 2], c % 2 * 3 * P, c // 2 * 512
                    slot_free(q0 + 3 * e + 2, c)
                    src = moe_w_down[0][bass.ds(e, 1), r0:r0 + full * P, col:col + 512]
                    sp_eng.dma_start(flat(c, 3, 512)[:, 0:full, :], src.rearrange("e (k p) n -> p (e k) n", p=P)
                                     ).then_inc(raw_loaded[c], 16)
                    if c % 2:
                        src = moe_w_down[0][bass.ds(e, 1), (KE - 1) * P:FE, col:col + 512]
                        sp_eng.dma_start(raw[c][0:FE_LAST, 1024:1536], src.rearrange("e p n -> (e p) n")
                                         ).then_inc(last_loaded[c // 2], 16)
            quads(sp_eng, "gate1", from_cols(ple_w_gate[1], 0))
            for t in range(TT):
                sp_eng.wait_ge(final_dve, t + 1)
                sp_eng.wait_ge(final_act, t + 1)
                sp_eng.dma_start(out.rearrange("b (t p) d -> (b p) t d", p=P)[:, t, :], o_tok[:, t, :]).then_inc(out_stored, 16)
            sp_eng.wait_ge(out_stored, 16 * TT)

        @block.gpsimd
        def _(pool):
            fills = [(ident, 0.0), (ones, 1.0), (mean_f, 1.0 / D), (neg_incl_f, -1.0), (cum, 1.0), (keep, 1.0),
                     (floor_a, 0.0), (clip_b, BIG)]
            for t, v in fills:
                last = pool.memset(t[:, :], v)
            last.then_inc(built, 1)
            pool.wait_ge(built, 1)
            cuts = [(ident, ALU.not_equal, 1.0, 1, -1),
                    (neg_incl_f, ALU.is_ge, 0.0, 1, -1),
                    (cum, ALU.is_ge, 0.0, -1, 1),
                    (keep, ALU.is_gt, 0.0, -1, 1),
                    (floor_a, ALU.is_gt, NEG, -1, 1),
                    (clip_b, ALU.is_ge, NEG, 1, -1)]
            for t, op, fill, mult, step in cuts:
                pool.affine_select(out=t[:, :], in_=t[:, :], pattern=[[step, P]], compare_op=op, fill=fill,
                                   base=0, channel_multiplier=mult).then_inc(built, 1)
            pool.iota(lanes[:, :], pattern=[[1, NE]], base=0, channel_multiplier=0,
                      allow_small_or_imprecise_dtypes=True)
            pool.iota(lane_slots[:, :], pattern=[[SEQ, NE]], base=0, channel_multiplier=0,
                      allow_small_or_imprecise_dtypes=True)
            pool.iota(place_f[:, :, :], pattern=[[SEQ, 2], [P, TT]], base=0, channel_multiplier=1,
                      allow_small_or_imprecise_dtypes=True).then_inc(built, 1)
            pool.wait_ge(mix_lo, 2 * KD)
            pool.iota(list_rows[:, :], pattern=[[1, P]], base=2 * SEQ, channel_multiplier=0,
                      allow_small_or_imprecise_dtypes=True).then_inc(built, 1)
            pool.wait_ge(built, BUILT + 1)
            by_slot = place_of.rearrange("(c p) o -> c (p o)", p=P)
            pool.dma_start(by_slot, list_rows[:, :]).then_inc(list_cleared, 16)

            pool.wait_ge(rows_copied, TT)
            pool.dma_start(x_dram.rearrange("(t p) d -> p t d", p=P), x_rows[:, :, :]).then_inc(y_stored, 16)
            pool.wait_ge(list_cleared, 16)
            pool.wait_ge(slots_ready, 1)
            for c in range(2):
                for t in range(TT):
                    pool.indirect_dma_start(place_of, bass.IndirectOffsetOnAxis(ap=slot_i[:, c, t:t + 1], axis=0),
                                            place_f[:, c, t:t + 1], None).then_inc(listed, 16)
            pool.wait_ge(listed, 16 * 2 * TT)
            pool.dma_start(list_rows[:, :], by_slot).then_inc(list_loaded, 16)
            pool.wait_ge(list_ready, 1)
            pool.wait_ge(y_stored, 16)
            pool.wait_ge(tiles_ready, 1)

            def gather(e, indexed_to):
                pool.tensor_copy(gather_i[:, :], token_i[:, bass.ds(TT * e, TT)]).then_inc(indexed, 1)
                pool.wait_ge(indexed, indexed_to)

                def body(n):
                    for t in range(n):
                        pool.indirect_dma_start(
                            xg[:, t, :], None, x_dram,
                            bass.IndirectOffsetOnAxis(ap=gather_i[:, t:t + 1], axis=0)
                        ).then_inc(xg_loaded, 16 * share(t, n))
                by_tiles(pool, pool.value_load(tiles_i[0:1, bass.ds(e, 1)], min_val=1, max_val=TT), body)

            gather(0, 1)
            with pool.Fori(0, NE) as e:
                pool.wait_ge(xg_turned, TT * e + TT)
                gather(e + 1, 2 * e + 2)

                def store(n):
                    for t in range(n):
                        pool.indirect_dma_start(y_dram, bass.IndirectOffsetOnAxis(ap=store_i[:, t:t + 1], axis=0),
                                                y_tok[:, t, :], None).then_inc(y_stored, 16 * share(t, n))
                pool.wait_ge(y_stored, 16 * TT * e + 16)
                pool.tensor_copy(store_i[:, :], place_i[:, bass.ds(TT * e, TT)]).then_inc(indexed, 1)
                pool.wait_ge(indexed, 2 * e + 3)
                pool.wait_ge(banks_out, 8 * e + 16)
                by_tiles(pool, pool.value_load(tiles_i[0:1, bass.ds(e, 1)], min_val=1, max_val=TT), store)
            pool.wait_ge(y_stored, 16 * TT * NE + 16)
            for t in range(TT):
                for c, y in enumerate((y_one, y_two)):
                    r0 = c * SEQ + t * P
                    pool.dma_start(y[:, t, :], y_dram[r0:r0 + P, :]).then_inc(y_loaded[t], 16)

        @block.tensor
        def _(pe):
            def mm3(o, s_hi, s_lo, m_hi, m_lo, start, stop):
                pe.matmul(o, s_hi, m_hi, start=start, stop=False, skip_group_check=True)
                pe.matmul(o, s_hi, m_lo, start=False, stop=False, skip_group_check=True)
                return pe.matmul(o, s_lo, m_hi, start=False, stop=stop, skip_group_check=True)

            def weights(q, j):
                pe.wait_ge(lo_ready, 4 * q + j + 1)

            def free_of(value):
                if not isinstance(value, int) or value > 0:
                    pe.wait_ge(drained, value)

            def tiles(name, m_hi, m_lo, ahead=0):
                def step(q, i, j, last):
                    weights(q, j)
                    if not isinstance(i, int) or i or ahead:
                        free_of(DRAINED[name] + 4 * i + j - 3)
                    elif j == 0:
                        free_of(DRAINED[name])
                    for k in range(KD):
                        w = slice(k * P, (k + 1) * P)
                        mm = mm3(bank[j][:, :], w_hi[j % 2][:, w], w_lo[j % 2][:, w], m_hi[:, k, :], m_lo[:, k, :],
                                 k == 0, k == KD - 1)
                    mm.then_inc(chunk_done, 1)
                quads(pe, name, step)

            def values(name):
                def step(q, i, j, last):
                    weights(q, j)
                    if j % 2 == 0:
                        free_of(DRAINED[name] + (0 if i == 0 and j == 0 else 4 * i + j - 2))
                    for t in range(TT):
                        for k in range(4):
                            w, kk = slice(k * 256, (k + 1) * 256), j % 2 * 4 + k
                            mm = mm3(bank[j // 2 * 4 + t][:, 0:256], x_hi[:, kk, t * P:(t + 1) * P],
                                     x_lo[:, kk, t * P:(t + 1) * P], w_hi[j % 2][:, w], w_lo[j % 2][:, w],
                                     kk == 0, kk == KD - 1)
                    mm.then_inc(chunk_done, 1)
                quads(pe, name, step)

            def norm(n):
                pe.wait_ge(drained, DRAINED[("gu", "proj0", "proj1", "gate1")[n]])
                for k in range(KD):
                    pe.matmul(bank[4][:, :], mean_r[:, :], x_hi[:, k, :], start=k == 0, stop=False)
                    mm = pe.matmul(bank[4][:, :], mean_r[:, :], x_lo[:, k, :], start=False, stop=k == KD - 1)
                mm.then_inc(mean_done, 1)
                for k in range(KD):
                    pe.wait_ge(squared, KD * n + k + 1)
                    pe.matmul(bank[5][:, :], mean_f[:, :], sq[k % 2][:, :], start=k == 0, stop=k == KD - 1
                              ).then_inc(var_done, 1)

            def embed(layer):
                pe.wait_ge(p_loaded, 16 * (layer + 1))
                for k in range(KP):
                    for t in range(TT):
                        mm = pe.transpose(bank[6 + k][:, t * P:(t + 1) * P], p_tok[:, t, k * P:(k + 1) * P], ident[:, :])
                    mm.then_inc(turned, 1)
                pe.wait_ge(turned_lo, KD + KP * (layer + 1))
                name = f"proj{layer}"

                def step(q, i, j, last):
                    weights(q, j)
                    free_of(DRAINED[name] + max(0, j - 1))
                    for s in range(2):
                        for k in range(KP):
                            w = slice(k * 256 + s * P, k * 256 + (s + 1) * P)
                            mm = mm3(bank[j % 2 * 2 + s][:, :], w_hi[j % 2][:, w], w_lo[j % 2][:, w],
                                     pt_hi[:, k, :], pt_lo[:, k, :], k == 0, k == KP - 1)
                    mm.then_inc(chunk_done, 1)
                quads(pe, name, step)

            pe.wait_ge(built, BUILT)
            pe.wait_ge(x_loaded, 16 * TT)
            for k in range(KD):
                if k >= 4:
                    pe.wait_ge(turned_out, k - 3)
                for t in range(TT):
                    mm = pe.transpose(bank[k % 4][:, t * P:(t + 1) * P], x_tok[:, t, k * P:(k + 1) * P], ident[:, :])
                mm.then_inc(turned, 1)

            pe.wait_ge(ln_loaded, 32)
            pe.transpose(bank[5][:, 0:64], ln_rows[:, :], ident[0:64, 0:64]).then_inc(turned, 1)

            pe.wait_ge(turned_lo, KD)
            pe.wait_ge(consts, CONSTS)
            pe.wait_ge(turned_out, KD)
            tiles("q0", x_hi, x_lo)
            tiles("k0", x_hi, x_lo, ahead=1)
            values("v0")

            def scores_a(h):
                for g, n in enumerate(reversed(range(TT))):
                    if h:
                        pe.wait_ge(a_ready, TT * (h - 1) + g + 1)
                    for d in range(DT):
                        f = DT * h + d
                        mm = mm3(bank[n][:, 0:WID[n]], k_hi[:, f, n * P:(n + 1) * P], k_lo[:, f, n * P:(n + 1) * P],
                                 q_hi[:, f, n * P:], q_lo[:, f, n * P:], d == 0, d == DT - 1)
                    mm.then_inc(z_done, 1)

            def tails_a(h):
                for g, n in enumerate(reversed(range(TT))):
                    if g == 0:
                        pe.wait_ge(sp_lo_ready, 2 * h + 1)
                    if g == TT - 1:
                        pe.wait_ge(sp_lo_ready, 2 * h + 2)
                    for part in (sp_hi, sp_lo):
                        mm = pe.matmul(bank[n][:, 0:WID[n]], neg_incl[:, :], part[:, OFF[n]:OFF[n] + WID[n]],
                                       start=False, stop=n == TT - 1 and part is sp_lo, skip_group_check=True)
                    for m in range(n + 1, TT):
                        for part in (sp_hi, sp_lo):
                            mm = pe.matmul(bank[n][:, (m - n) * P:WID[n]], neg_ones[:, :],
                                           part[:, OFF[m]:OFF[m] + WID[m]], start=False,
                                           stop=m == TT - 1 and part is sp_lo, skip_group_check=True)
                    mm.then_inc(tail_done, 1)

            def mix_a(h):
                pe.wait_ge(a_lo_ready, 2 * h + 2)
                if h:
                    pe.wait_ge(mix_lo, DT * h)
                for d in range(DT):
                    c = slice(h * DH + d * P, h * DH + (d + 1) * P)
                    for n in range(TT):
                        a = slice(OFF[n], OFF[n] + WID[n])
                        mm = mm3(bank[6 + d][:, n * P:], v_hi[:, n, c], v_lo[:, n, c], a_hi[:, a], a_lo[:, a],
                                 n == 0, n == TT - 1)
                    mm.then_inc(mixed, 1)

            pe.wait_ge(drained, DRAINED["o0"])
            scores_a(0)
            for h in range(H):
                tails_a(h)
                if h + 1 < H:
                    scores_a(h + 1)
                mix_a(h)
            pe.wait_ge(mix_lo, KD)
            tiles("o0", q_hi, q_lo)
            norm(0)
            pe.wait_ge(x_ready, KD)
            tiles("gu", x_hi, x_lo)

            def down_step(q, i, j, last):
                weights(q, j)
                if j % 2 == 0:
                    free_of(DRAINED["down"] + 4 * i + j - 2)
                for k in range(KF // 2):
                    w, kk = slice(k * P, (k + 1) * P), j % 2 * (KF // 2) + k
                    mm = mm3(bank[j // 2][:, :], w_hi[j % 2][:, w], w_lo[j % 2][:, w], h_hi[:, kk, :], h_lo[:, kk, :],
                             kk == 0, kk == KF - 1)
                mm.then_inc(chunk_done, 1)
            pe.wait_ge(drained, DRAINED["down"])
            quads(pe, "down", down_step)
            embed(0)
            norm(1)
            pe.wait_ge(x_ready, 2 * KD)
            tiles("gate0", x_hi, x_lo)
            pe.wait_ge(x_ready, 3 * KD)
            tiles("q1", x_hi, x_lo)
            tiles("k1", x_hi, x_lo, ahead=1)
            values("v1")
            pe.wait_ge(drained, DRAINED["o1"])
            pe.wait_ge(small_loaded, 48)
            for t in range(TT):
                for k in range(KD):
                    mm = pe.matmul(bank[0][:, t * H:(t + 1) * H], x_exact[:, k, t * P:(t + 1) * P], w_f[:, k, :],
                                   start=k == 0, stop=k == KD - 1)
            mm.then_inc(f_done, 1)
            pe.wait_ge(f_step, 3)
            for t in range(TT):
                for m in range(t + 1):
                    mm = pe.matmul(bank[1][:, t * H:(t + 1) * H], (cum if m == t else ones)[:, :], log_f[:, m, :],
                                   start=m == 0, stop=m == t)
            mm.then_inc(c_done, 1)
            for h in range(H):
                pe.wait_ge(diag_ready, h + 1)
                if h >= 2:
                    pe.wait_ge(row_copied, h - 1)
                for t in range(TT):
                    mm = pe.matmul(bank[2 + h % 2][:, t * P:(t + 1) * P], ones[:, :], c_diag[:, t, :], start=True, stop=True)
                mm.then_inc(row_done, 1)

            def scores_b(h):
                for m in range(TT):
                    if h:
                        pe.wait_ge(z2_step, 3 * (TT * (h - 1) + m) + 1)
                    else:
                        pe.wait_ge(row_copied, H)
                    for d in range(DT):
                        f = DT * h + d
                        mm = mm3(bank[m][:, 0:WB[m]], q_hi[:, f, m * P:(m + 1) * P], q_lo[:, f, m * P:(m + 1) * P],
                                 k_hi[:, f, 0:WB[m]], k_lo[:, f, 0:WB[m]], d == 0, d == DT - 1)
                    mm.then_inc(z2_done, 1)

            def turn_b(h):
                for m in range(TT):
                    s = TT * h + m
                    pe.wait_ge(w_ready, s + 1)
                    if s >= 2:
                        pe.wait_ge(wt_ready, s - 1)
                    for n in range(m + 1):
                        mm = pe.transpose(bank[4 + m % 2][:, n * P:(n + 1) * P],
                                          zb[:, OB[m] + n * P:OB[m] + (n + 1) * P], ident[:, :])
                    mm.then_inc(w_turned, 1)

            def mix_b(h):
                pe.wait_ge(wt_ready, TT * (h + 1))
                pe.wait_ge(mix_lo, KD + DT * h)
                for d in range(DT):
                    c = slice(h * DH + d * P, h * DH + (d + 1) * P)
                    for n in range(TT):
                        mm = mm3(bank[6 + d][:, n * P:], v_hi[:, n, c], v_lo[:, n, c], wt_hi[:, n, n * P:], wt_lo[:, n, n * P:],
                                 n == 0, n == TT - 1)
                    mm.then_inc(mixed, 1)

            scores_b(0)
            for h in range(H):
                if h + 1 < H:
                    scores_b(h + 1)
                turn_b(h)
                mix_b(h)
            pe.wait_ge(mix_lo, 2 * KD)
            tiles("o1", q_hi, q_lo)
            norm(2)
            pe.wait_ge(x_ready, 4 * KD)
            for t in range(TT):
                for k in range(KD):
                    mm = pe.matmul(bank[6][:, t * NE:(t + 1) * NE], x_exact[:, k, t * P:(t + 1) * P], w_r[:, k, :],
                                   start=k == 0, stop=k == KD - 1)
            mm.then_inc(router_done, 1)
            for t in range(TT):
                if t >= 2:
                    pe.wait_ge(rows_copied, t - 1)
                for k in range(KD):
                    mm = pe.transpose(bank[t % 2 * 2 + k // 4][:, k % 4 * P:(k % 4 + 1) * P],
                                      x_exact[:, k, t * P:(t + 1) * P], ident[:, :])
                mm.then_inc(rows_turned, 1)
            pe.wait_ge(route_step, 7)
            for t in range(TT):
                for m in range(t + 1):
                    pe.matmul(bank[7][:, t * NE:(t + 1) * NE], (keep if m == t else ones)[:, :], sel_any[:, m, :],
                              start=m == 0, stop=m == t)
            for m in range(TT):
                mm = pe.matmul(bank[7][:, TT * NE:(TT + 1) * NE], ones[:, :], sel_any[:, m, :],
                               start=m == 0, stop=m == TT - 1)
            mm.then_inc(ranked, 1)
            pe.wait_ge(slots_ready, 1)
            pe.wait_ge(rows_copied, TT)
            embed(1)
            pe.wait_ge(list_loaded, 16)
            pe.transpose(bank[6][:, 0:SLOT_TILES], list_rows[:, :], ident[0:SLOT_TILES, 0:SLOT_TILES]
                         ).then_inc(list_turned, 1)
            pe.wait_ge(tiles_ready, 1)
            pe.wait_ge(drained, DRAINED["turn"])

            def count(e):
                return pe.value_load(tiles_i[0:1, bass.ds(e, 1)], min_val=1, max_val=TT)

            def turn_x(e):
                def body(n):
                    pe.wait_ge(xg_loaded, 16 * TT * e + 16 * TT)
                    for t in range(n):
                        if t >= 2:
                            pe.wait_ge(xg_ready, TT * e + t - 1)
                        for k in range(KD):
                            mm = pe.transpose(bank[4 + t % 2 * 2 + k // 4][:, k % 4 * P:(k % 4 + 1) * P],
                                              xg[:, t, k * P:(k + 1) * P], ident[:, :])
                        mm.then_inc(xg_turned, share(t, n))
                by_tiles(pe, count(e), body)

            q0 = BASE["moe"] // RAW

            def first_product(e):
                def body(n):
                    for c in range(8):
                        half, up, kh = c // 4, c // 2 % 2, c % 2
                        weights(q0 + 3 * e + c // RAW, c % RAW)
                        if c == 0:
                            pe.wait_ge(xg_ready, TT * e + TT)
                            pe.wait_ge(banks_out, 8 * e + 4)
                        if c == 2:
                            pe.wait_ge(banks_out, 8 * e + 8)
                        if c == 4:
                            pe.wait_ge(silu_ready, 8 * e + TT)
                        if c == 6:
                            pe.wait_ge(he_ready, 8 * e + TT)
                        for t in range(n):
                            for k in range(4):
                                w, kk = slice(k * FC, (k + 1) * FC), kh * 4 + k
                                mm = mm3(bank[4 * up + t][:, 0:FC], x_hi[:, kk, t * P:(t + 1) * P],
                                         x_lo[:, kk, t * P:(t + 1) * P], w_hi[c % 2][:, w], w_lo[c % 2][:, w],
                                         kk == 0, kk == KD - 1)
                        mm.then_inc(chunk_done, 1)
                    for t in range(n):
                        pe.wait_ge(he_ready, 8 * e + TT + t + 1)
                        if t >= 2:
                            pe.wait_ge(het_ready, TT * e + t - 1)
                        for k in range(KE):
                            mm = pe.transpose(bank[t % 2 * 2 + k // 4][:, k % 4 * P:(k % 4 + 1) * P],
                                              he[:, t, k * P:(k + 1) * P], ident[:, :])
                        mm.then_inc(he_turned, share(t, n))
                    pe.wait_ge(he_ready, 8 * e + 2 * TT)
                by_tiles(pe, count(e), body)

            def second_product(e):
                def body(n):
                    pe.wait_ge(het_ready, TT * e + TT)
                    for c in range(4):
                        weights(q0 + 3 * e + 2, c)
                        if c == 2:
                            pe.wait_ge(xg_ready, TT * e + 2 * TT)
                        for t in range(n):
                            for k in range(3):
                                kk = c % 2 * 3 + k
                                r, w = (FE_LAST if kk == KE - 1 else P), slice(k * 512, (k + 1) * 512)
                                mm = mm3(bank[4 * (c // 2) + t][:, :], het_hi[0:r, kk, t * P:(t + 1) * P],
                                         het_lo[0:r, kk, t * P:(t + 1) * P], w_hi[c % 2][0:r, w], w_lo[c % 2][0:r, w],
                                         kk == 0, kk == KE - 1)
                        mm.then_inc(chunk_done, 1)
                by_tiles(pe, count(e), body)

            pe.wait_ge(list_ready, 1)
            turn_x(0)
            with pe.Fori(0, NE) as e:
                first_product(e)
                turn_x(e + 1)
                second_product(e)
            pe.wait_ge(banks_out, 8 + 8 * NE)
            pe.wait_ge(combined, TT)
            for k in range(KD):
                if k >= 4:
                    pe.wait_ge(drained, DRAINED["turn"] + k - 3)
                for t in range(TT):
                    mm = pe.transpose(bank[k % 4][:, t * P:(t + 1) * P], y_one[:, t, k * P:(k + 1) * P], ident[:, :])
                mm.then_inc(acc_turned, 1)
            norm(3)
            pe.wait_ge(x_ready, 5 * KD)
            tiles("gate1", x_hi, x_lo)
            pe.wait_ge(drained, DRAINED["gate1"] + KD)
            pe.wait_ge(embedded, 2 * KD)
            for t in range(TT):
                for k in range(KD):
                    mm = pe.transpose(bank[2 * t + k // 4][:, k % 4 * P:(k % 4 + 1) * P], x_exact[:, k, t * P:(t + 1) * P],
                                      ident[:, :])
                mm.then_inc(final_turned, 1)

        @block.scalar
        def _(act):
            def split_hi(q, j, n, last64=None):
                act.wait_ge(raw_loaded[j], 16 * (q + 1))
                if not isinstance(q, int) or 4 * q + j >= SPLIT:
                    act.wait_ge(chunk_done, 4 * q + j - 1)
                if last64 is None:
                    act.copy(w_hi[j % 2][:, 0:n], raw[j][:, 0:n]).then_inc(hi_ready, 1)
                else:
                    act.wait_ge(last_loaded[j // 2], last64)
                    act.copy(w_hi[j % 2][:, 0:1024], raw[j][:, 0:1024])
                    act.copy(w_hi[j % 2][0:FE_LAST, 1024:1536], raw[j][0:FE_LAST, 1024:1536]).then_inc(hi_ready, 1)

            def ahead(name, q, j, last):
                n = NEXT_SIZE[name] if last else SIZE[name]
                if n:
                    split_hi(q + (j + 1) // RAW, (j + 1) % RAW, n)

            def tiles_hi(name, dst, scale=1.0):
                def step(q, i, j, last):
                    ahead(name, q, j, last)
                    act.wait_ge(chunk_done, 4 * q + j + 1)
                    act.activation(dst[:, 4 * i + j, :], bank[j][:, :], ACT.Copy, scale=scale).then_inc(out_hi, 1)
                quads(act, name, step, peel=True)

            def values_hi(name):
                def step(q, i, j, last):
                    ahead(name, q, j, last)
                    if j % 2 == 0:
                        return
                    act.wait_ge(chunk_done, 4 * q + j + 1)
                    g = 2 * i + j // 2
                    for t in range(TT):
                        op = act.copy(v_hi[:, t, g * 256:(g + 1) * 256], bank[j // 2 * 4 + t][:, 0:256])
                    op.then_inc(out_hi, 2)
                quads(act, name, step, peel=True)

            def sum_hi(n, k):
                act.wait_ge(summed, KD * n + k + 1)
                act.copy(x_hi[:, k, :], x_exact[:, k, :]).then_inc(y_hi_ready, 1)

            def residual_hi(name, n):
                def step(q, i, j, last):
                    ahead(name, q, j, last)
                    if name != "down":
                        sum_hi(n, 4 * i + j)
                    elif j % 2:
                        sum_hi(n, 2 * i + j // 2)
                quads(act, name, step, peel=True)

            def norm(n):
                for k in range(KD):
                    act.wait_ge(centred, KD * n + k + 1)
                    if k >= 2:
                        act.wait_ge(var_done, KD * n + k - 1)
                    act.activation(sq[k % 2][:, :], x_exact[:, k, :], ACT.Square).then_inc(squared, 1)
                act.wait_ge(var_done, KD * (n + 1))
                act.wait_ge(consts, CONSTS)
                act.activation(rstd[:, :], bank[5][:, :], ACT.Sqrt, bias=eps[:, 0:1]).then_inc(std_ready, 1)
                for k in range(KD):
                    g, b = ln_cols[:, n * KD + k:n * KD + k + 1], ln_cols[:, 32 + n * KD + k:33 + n * KD + k]
                    act.wait_ge(normed, KD * n + k + 1)
                    act.activation(x_hi[:, k, :], x_exact[:, k, :], ACT.Identity, bias=b, scale=g)
                    act.activation(x_exact[:, k, :], x_exact[:, k, :], ACT.Identity, bias=b, scale=g).then_inc(affine, 1)

            def embed(layer):
                name = f"proj{layer}"
                for k in range(KP):
                    act.wait_ge(turned, KD + 1 + KP * layer + k + 1)
                    act.copy(pt_hi[:, k, :], bank[6 + k][:, :]).then_inc(turned_hi, 1)
                quads(act, name, lambda q, i, j, last: ahead(name, q, j, last))

            def gate(layer, n):
                name = f"gate{layer}"

                def step(q, i, j, last):
                    ahead(name, q, j, last)
                    act.wait_ge(chunk_done, 4 * q + j + 1)
                    act.activation(sig[:, 4 * i + j, :], bank[j][:, :], ACT.Sigmoid).then_inc(gated, 1)
                quads(act, name, step, peel=True)
                if layer == 0:
                    for k in range(KD):
                        act.wait_ge(embedded, k + 1)
                        act.copy(x_hi[:, k, :], x_exact[:, k, :]).then_inc(affine, 1)

            split_hi(0, 0, SIZE["q0"])
            for k in range(KD):
                act.wait_ge(turned_out, k + 1)
                act.copy(x_hi[:, k, :], x_exact[:, k, :]).then_inc(turned_hi, 1)
            tiles_hi("q0", q_hi, SCALE)
            tiles_hi("k0", k_hi)
            values_hi("v0")

            act.preload_act_table_set("natural_log_exp_and_others")
            act.wait_ge(drained, DRAINED["o0"])
            for h in range(H):
                for g, group in enumerate(((3, 2, 1), (0,))):
                    lo, hi = OFF[group[-1]], OFF[group[0]] + WID[group[0]]
                    if h and g == 0:
                        act.wait_ge(a_lo_ready, 2 * h)
                    for n in group:
                        act.wait_ge(z_done, TT * h + TT - n)
                        op = act.activation(ln_a[:, OFF[n]:OFF[n] + WID[n]], bank[n][:, 0:WID[n]], ACT.Abs)
                    op.then_inc(absed, 1)
                    act.wait_ge(absed, 2 * h + g + 1)
                    act.activation(ln_a[:, lo:hi], ln_a[:, lo:hi], ACT.Exp, scale=-1.0).then_inc(exped, 1)
                    act.wait_ge(exped, 2 * h + g + 1)
                    act.activation(ln_a[:, lo:hi], ln_a[:, lo:hi], ACT.Ln, bias=1.0).then_inc(logged, 1)
                for g, (lo, hi) in enumerate(((OFF[1], TRI), (0, OFF[1]))):
                    act.wait_ge(sp_ready, 2 * h + g + 1)
                    act.copy(sp_hi[:, lo:hi], sp[:, lo:hi]).then_inc(sp_hi_ready, 1)
                for g, n in enumerate(reversed(range(TT))):
                    act.wait_ge(diag_cut, TT * h + g + 1)
                    op = act.activation(ln_a[:, OFF[n]:OFF[n] + P], a_diag[:, n, :], ACT.Exp)
                    if n < TT - 1:
                        op = act.activation(ln_a[:, OFF[n] + P:OFF[n] + WID[n]], bank[n][:, P:WID[n]], ACT.Exp)
                    op.then_inc(a_ready, 1)
                for d in range(DT):
                    act.wait_ge(mixed, DT * h + d + 1)
                    act.copy(q_hi[:, DT * h + d, :], bank[6 + d][:, :]).then_inc(mix_hi, 1)
            residual_hi("o0", 0)
            norm(0)

            def gu_step(q, i, j, last):
                ahead("gu", q, j, last)
                if j % 2 == 0:
                    return
                m = 2 * i + j // 2
                act.wait_ge(chunk_done, 4 * q + j + 1)
                act.activation(h_tmp[j // 2][:, :], bank[j - 1][:, :], ACT.Silu).then_inc(gated, 1)
                act.wait_ge(hidden, m + 1)
                act.copy(h_hi[:, m, :], h_tmp[j // 2][:, :]).then_inc(out_hi, 2)
            quads(act, "gu", gu_step, peel=True)
            residual_hi("down", 1)
            embed(0)
            norm(1)
            gate(0, 1)
            tiles_hi("q1", q_hi, SCALE)
            tiles_hi("k1", k_hi)
            values_hi("v1")

            act.preload_act_table_set("natural_log_exp_and_others")
            act.wait_ge(f_step, 1)
            act.activation(f_abs[:, :, :], f_pre[:, :, :], ACT.Abs).then_inc(f_act, 1)
            act.wait_ge(f_act, 1)
            act.activation(f_abs[:, :, :], f_abs[:, :, :], ACT.Exp, scale=-1.0).then_inc(f_act, 1)
            act.wait_ge(f_act, 2)
            act.activation(f_abs[:, :, :], f_abs[:, :, :], ACT.Ln, bias=1.0).then_inc(f_act, 1)
            act.wait_ge(drained, DRAINED["o1"])
            for h in range(H):
                act.wait_ge(row_done, h + 1)
                act.copy(c_row[:, h, :], bank[2 + h % 2][:, :]).then_inc(row_copied, 1)

            def exps_b(h):
                for m in range(TT):
                    s = TT * h + m
                    act.wait_ge(z2_step, 3 * s + 3)
                    z = zb[:, OB[m]:OB[m] + WB[m]]
                    act.activation(z, z, ACT.Exp, bias=neg_max[:, m:m + 1], accum_out=row_sum[:, m:m + 1]
                                   ).then_inc(e_ready, 1)

            def turned_b(h):
                for m in range(TT):
                    s = TT * h + m
                    act.wait_ge(w_turned, s + 1)
                    if m == 0 and h:
                        act.wait_ge(mixed, KD + DT * h)
                    src = bank[4 + m % 2][:, 0:WB[m]].rearrange("p (n t) -> p n t", t=P)
                    act.copy(wt_hi[:, 0:m + 1, m * P:(m + 1) * P], src).then_inc(wt_hi_ready, 1)

            for h in range(H):
                exps_b(h)
                turned_b(h)
                for d in range(DT):
                    act.wait_ge(mixed, KD + DT * h + d + 1)
                    act.copy(q_hi[:, DT * h + d, :], bank[6 + d][:, :]).then_inc(mix_hi, 1)
            residual_hi("o1", 2)
            norm(2)
            for t in range(TT):
                act.wait_ge(rows_turned, t + 1)
                act.copy(x_rows[:, t, 0:512], bank[t % 2 * 2][:, :])
                act.copy(x_rows[:, t, 512:1024], bank[t % 2 * 2 + 1][:, :]).then_inc(rows_copied, 1)
            act.wait_ge(route_step, 3)
            act.activation(g_exp[:, :], g_diff[:, :], ACT.Exp).then_inc(gate_exp, 1)

            embed(1)
            q0 = BASE["moe"] // RAW
            act.wait_ge(tiles_ready, 1)

            def count(e):
                return act.value_load(tiles_i[0:1, bass.ds(e, 1)], min_val=1, max_val=TT)

            def x_high(e):
                def body(n):
                    for t in range(n):
                        act.wait_ge(xg_turned, TT * e + t + 1)
                        for b in range(2):
                            op = act.copy(x_hi[:, 4 * b:4 * b + 4, t * P:(t + 1) * P],
                                                bank[4 + t % 2 * 2 + b][:, :].rearrange("p (k t) -> p k t", t=P))
                        op.then_inc(xg_hi_ready, share(t, n))
                by_tiles(act, count(e), body)


            def first_product(e):
                def body(n):
                    for c in range(8):
                        half, up, kh = c // 4, c // 2 % 2, c % 2
                        split_hi(q0 + 3 * e + (c + 1) // RAW, (c + 1) % RAW, 4 * FC if c < 7 else 1536)
                        if up == 0 and kh == 1:
                            act.wait_ge(chunk_done, 4 * q0 + 12 * e + c + 1)
                            for t in range(n):
                                act.activation(he[:, t, half * FC:(half + 1) * FC], bank[t][:, 0:FC], ACT.Silu
                                               ).then_inc(silu_ready, share(t, n))
                    for t in range(n):
                        act.wait_ge(he_turned, TT * e + t + 1)
                        act.copy(het_hi[:, 0:4, t * P:(t + 1) * P],
                                       bank[t % 2 * 2][:, :].rearrange("p (k t) -> p k t", t=P))
                        act.copy(het_hi[:, 4:KE, t * P:(t + 1) * P],
                                       bank[t % 2 * 2 + 1][:, 0:2 * P].rearrange("p (k t) -> p k t", t=P)).then_inc(het_hi_ready, share(t, n))
                by_tiles(act, count(e), body)

            def second_product(e):
                def body(n):
                    for c in range(4):
                        if c < 3:
                            split_hi(q0 + 3 * e + 2, c + 1, 1536, 16 * e + 16 if c % 2 == 0 else None)
                        else:
                            split_hi(q0 + 3 * e + 3, 0, 4 * FC)
                        if c % 2:
                            act.wait_ge(chunk_done, 4 * q0 + 12 * e + 8 + c + 1)
                            if c == 1:
                                act.wait_ge(y_stored, 16 * TT * e + 16)
                            for t in range(n):
                                act.copy(y_tok[:, t, c // 2 * 512:(c // 2 + 1) * 512],
                                               bank[4 * (c // 2) + t][:, :]).then_inc(banks_out, share(t, n))
                by_tiles(act, count(e), body)

            x_high(0)
            act.nop().then_inc(banks_out, 8)
            with act.Fori(0, NE) as e:
                first_product(e)
                x_high(e + 1)
                second_product(e)
            for k in range(KD):
                sum_hi(3, k)
            norm(3)
            gate(1, 3)
            for t in range(TT):
                act.wait_ge(final_turned, t + 1)
                act.copy(o_tok[:, t, 0:512], bank[2 * t][:, :]).then_inc(final_act, 1)

        @block.vector
        def _(dve):
            def minus(dst, a, b):
                return dve.tensor_tensor(dst, a, b, ALU.subtract)

            def split_lo(q, j, n, last64=False):
                dve.wait_ge(hi_ready, 4 * q + j + 1)
                if last64:
                    minus(w_lo[j % 2][:, 0:1024], raw[j][:, 0:1024], w_hi[j % 2][:, 0:1024].bitcast(F32))
                    minus(w_lo[j % 2][0:FE_LAST, 1024:1536], raw[j][0:FE_LAST, 1024:1536],
                          w_hi[j % 2][0:FE_LAST, 1024:1536].bitcast(F32)).then_inc(lo_ready, 1)
                else:
                    minus(w_lo[j % 2][:, 0:n], raw[j][:, 0:n], w_hi[j % 2][:, 0:n].bitcast(F32)).then_inc(lo_ready, 1)

            def ahead(name, q, j, last):
                n = NEXT_SIZE[name] if last else SIZE[name]
                if n:
                    split_lo(q + (j + 1) // RAW, (j + 1) % RAW, n)

            def low(dst, psum, hi, scale=1.0):
                return dve.scalar_tensor_tensor(out=dst, in0=psum, scalar=scale, in1=hi.bitcast(F32),
                                                op0=ALU.mult, op1=ALU.subtract)

            def tiles_lo(name, hi, lo, scale=1.0):
                def step(q, i, j, last):
                    ahead(name, q, j, last)
                    dve.wait_ge(out_hi, OUT_HI[name] + 4 * i + j + 1)
                    low(lo[:, 4 * i + j, :], bank[j][:, :], hi[:, 4 * i + j, :], scale).then_inc(drained, 1)
                quads(dve, name, step, peel=True)

            def values_lo(name):
                def step(q, i, j, last):
                    ahead(name, q, j, last)
                    if j % 2 == 0:
                        return
                    g = 2 * i + j // 2
                    c = slice(g * 256, (g + 1) * 256)
                    dve.wait_ge(out_hi, OUT_HI[name] + 2 * (g + 1))
                    for t in range(TT):
                        op = low(v_lo[:, t, c], bank[j // 2 * 4 + t][:, 0:256], v_hi[:, t, c])
                    op.then_inc(drained, 2)
                quads(dve, name, step, peel=True)

            def add_residual(n, k, psum):
                dve.scalar_tensor_tensor(out=x_exact[:, k, :], in0=x_exact[:, k, :], scalar=ALPHA, in1=psum,
                                         op0=ALU.mult, op1=ALU.add).then_inc(summed, 1)
                dve.wait_ge(y_hi_ready, KD * n + k + 1)
                return minus(x_lo[:, k, :], x_exact[:, k, :], x_hi[:, k, :].bitcast(F32))

            def residual(name, n):
                def step(q, i, j, last):
                    ahead(name, q, j, last)
                    if name != "down":
                        dve.wait_ge(chunk_done, 4 * q + j + 1)
                        add_residual(n, 4 * i + j, bank[j][:, :]).then_inc(drained, 1)
                    elif j % 2:
                        dve.wait_ge(chunk_done, 4 * q + j + 1)
                        add_residual(n, 2 * i + j // 2, bank[j // 2][:, :]).then_inc(drained, 2)
                quads(dve, name, step, peel=True)

            def norm(n):
                dve.wait_ge(mean_done, n + 1)
                for k in range(KD):
                    minus(x_exact[:, k, :], x_exact[:, k, :], bank[4][:, :]).then_inc(centred, 1)
                dve.wait_ge(std_ready, n + 1)
                dve.reciprocal(rstd[:, :], rstd[:, :]).then_inc(rstd_ready, 1)
                dve.wait_ge(rstd_ready, n + 1)
                dve.wait_ge(squared, KD * (n + 1))
                for k in range(KD):
                    dve.tensor_tensor(x_exact[:, k, :], x_exact[:, k, :], rstd[:, :], ALU.mult).then_inc(normed, 1)
                done = [0, KD, 3 * KD, 4 * KD][n]
                for k in range(KD):
                    dve.wait_ge(affine, done + k + 1)
                    minus(x_lo[:, k, :], x_exact[:, k, :], x_hi[:, k, :].bitcast(F32)).then_inc(x_ready, 1)

            def embed(layer):
                name = f"proj{layer}"
                for k in range(KP):
                    dve.wait_ge(turned_hi, KD + KP * layer + k + 1)
                    low(pt_lo[:, k, :], bank[6 + k][:, :], pt_hi[:, k, :]).then_inc(turned_lo, 1)

                def step(q, i, j, last):
                    ahead(name, q, j, last)
                    dve.wait_ge(chunk_done, 4 * q + j + 1)
                    for s in range(2):
                        op = dve.tensor_copy(proj[:, 2 * j + s, :], bank[j % 2 * 2 + s][:, :])
                    op.then_inc(drained, 1)
                quads(dve, name, step)

            def gate(layer):
                name = f"gate{layer}"

                def step(q, i, j, last):
                    ahead(name, q, j, last)
                    k = 4 * i + j
                    dve.wait_ge(gated, GATED[name] + k + 1)
                    dve.tensor_tensor(proj[:, k, :], proj[:, k, :], sig[:, k, :], ALU.mult).then_inc(drained, 1)
                    dve.wait_ge(drained, DRAINED[name] + k + 1)
                    dve.tensor_tensor(x_exact[:, k, :], x_exact[:, k, :], proj[:, k, :], ALU.add).then_inc(embedded, 1)
                quads(dve, name, step)
                if layer == 0:
                    for k in range(KD):
                        dve.wait_ge(affine, 2 * KD + k + 1)
                        minus(x_lo[:, k, :], x_exact[:, k, :], x_hi[:, k, :].bitcast(F32)).then_inc(x_ready, 1)

            dve.wait_ge(built, BUILT)
            dve.memset(eps[:, :], EPS)
            dve.tensor_scalar(neg_ones[:, :], ones[:, :], -1.0, None, ALU.mult)
            dve.tensor_copy(mean_r[:, :], mean_f[:, :])
            dve.tensor_copy(neg_incl[:, :], neg_incl_f[:, :]).then_inc(consts, 1)
            split_lo(0, 0, SIZE["q0"])
            for k in range(KD):
                dve.wait_ge(turned, k + 1)
                dve.tensor_copy(x_exact[:, k, :], bank[k % 4][:, :]).then_inc(turned_out, 1)
            for k in range(KD):
                dve.wait_ge(turned_hi, k + 1)
                minus(x_lo[:, k, :], x_exact[:, k, :], x_hi[:, k, :].bitcast(F32)).then_inc(turned_lo, 1)
            dve.wait_ge(turned, KD + 1)
            dve.tensor_copy(ln_cols[:, :], bank[5][:, 0:64]).then_inc(consts, 1)
            tiles_lo("q0", q_hi, q_lo, SCALE)
            tiles_lo("k0", k_hi, k_lo)
            values_lo("v0")

            for h in range(H):
                for g, group in enumerate(((3, 2, 1), (0,))):
                    lo, hi = OFF[group[-1]], OFF[group[0]] + WID[group[0]]
                    dve.wait_ge(logged, 2 * h + g + 1)
                    for n in group:
                        o = slice(OFF[n], OFF[n] + WID[n])
                        op = dve.scalar_tensor_tensor(out=sp[:, o], in0=bank[n][:, 0:WID[n]], scalar=0.0, in1=ln_a[:, o],
                                                      op0=ALU.max, op1=ALU.add)
                    op.then_inc(sp_raw, 1)
                    dve.wait_ge(sp_raw, 2 * h + g + 1)
                    for n in group:
                        o = slice(OFF[n], OFF[n] + P)
                        op = dve.tensor_tensor(sp[:, o], sp[:, o], keep[:, :], ALU.mult)
                    op.then_inc(sp_ready, 1)
                for g, (lo, hi) in enumerate(((OFF[1], TRI), (0, OFF[1]))):
                    dve.wait_ge(sp_hi_ready, 2 * h + g + 1)
                    minus(sp_lo[:, lo:hi], sp[:, lo:hi], sp_hi[:, lo:hi].bitcast(F32)).then_inc(sp_lo_ready, 1)
                for g, n in enumerate(reversed(range(TT))):
                    dve.wait_ge(tail_done, TT * h + g + 1)
                    dve.tensor_tensor(a_diag[:, n, :], bank[n][:, 0:P], floor_a[:, :], ALU.min).then_inc(diag_cut, 1)
                if h:
                    dve.wait_ge(mixed, DT * h)
                for g, (lo, hi) in enumerate(((OFF[1], TRI), (0, OFF[1]))):
                    dve.wait_ge(a_ready, TT * h + (TT - 1, TT)[g])
                    dve.tensor_copy(a_hi[:, lo:hi], ln_a[:, lo:hi]).then_inc(a_hi_ready, 1)
                    dve.wait_ge(a_hi_ready, 2 * h + g + 1)
                    minus(a_lo[:, lo:hi], ln_a[:, lo:hi], a_hi[:, lo:hi].bitcast(F32)).then_inc(a_lo_ready, 1)
                for d in range(DT):
                    dve.wait_ge(mix_hi, DT * h + d + 1)
                    low(q_lo[:, DT * h + d, :], bank[6 + d][:, :], q_hi[:, DT * h + d, :]).then_inc(mix_lo, 1)
            residual("o0", 0)
            norm(0)

            def gu_step(q, i, j, last):
                ahead("gu", q, j, last)
                if j % 2 == 0:
                    return
                m, t = 2 * i + j // 2, h_tmp[j // 2]
                dve.wait_ge(gated, m + 1)
                dve.tensor_tensor(t[:, :], t[:, :], bank[j][:, :], ALU.mult).then_inc(hidden, 1)
                dve.wait_ge(out_hi, OUT_HI["gu"] + 2 * (m + 1))
                minus(h_lo[:, m, :], t[:, :], h_hi[:, m, :].bitcast(F32)).then_inc(drained, 2)
            quads(dve, "gu", gu_step, peel=True)
            residual("down", 1)
            embed(0)
            norm(1)
            gate(0)
            tiles_lo("q1", q_hi, q_lo, SCALE)
            tiles_lo("k1", k_hi, k_lo)
            values_lo("v1")

            dve.wait_ge(f_done, 1)
            dve.wait_ge(small_loaded, 48)
            for t in range(TT):
                op = dve.tensor_tensor(f_pre[:, t, :], bank[0][:, t * H:(t + 1) * H], b_f[:, :], ALU.add)
            op.then_inc(f_step, 1)
            dve.wait_ge(f_act, 1)
            dve.tensor_scalar(f_pre[:, :, :], f_pre[:, :, :], 0.0, None, ALU.min).then_inc(f_step, 1)
            dve.wait_ge(f_step, 2)
            dve.wait_ge(f_act, 3)
            minus(log_f[:, :, :], f_pre[:, :, :], f_abs[:, :, :]).then_inc(f_step, 1)
            dve.wait_ge(c_done, 1)
            dve.tensor_copy(c_col[:, :, :], bank[1][:, 0:TT * H].rearrange("p (t h) -> p t h", h=H)).then_inc(c_copied, 1)
            dve.wait_ge(c_copied, 1)
            for h in range(H):
                if h:
                    dve.wait_ge(row_done, h)
                for t in range(TT):
                    op = dve.tensor_scalar(c_diag[:, t, :], ident[:, :], c_col[:, t, h:h + 1], None, ALU.mult)
                op.then_inc(diag_ready, 1)
            dve.wait_ge(row_copied, H)

            def scores_b(h):
                for m in range(TT):
                    s = TT * h + m
                    z, d = zb[:, OB[m]:OB[m] + WB[m]], zb[:, OB[m] + m * P:OB[m] + WB[m]]
                    dve.wait_ge(z2_done, s + 1)
                    if h:
                        dve.wait_ge(w_turned, TT * (h - 1) + m + 1)
                    dve.scalar_tensor_tensor(out=z, in0=bank[m][:, 0:WB[m]], scalar=c_col[:, m, h:h + 1],
                                             in1=c_row[:, h, 0:WB[m]], op0=ALU.add, op1=ALU.subtract).then_inc(z2_step, 1)
                    dve.wait_ge(z2_step, 3 * s + 1)
                    dve.tensor_tensor(d, d, clip_b[:, :], ALU.min).then_inc(z2_step, 1)
                    dve.wait_ge(z2_step, 3 * s + 2)
                    dve.tensor_reduce(neg_max[:, m:m + 1], z, AX.X, ALU.max, negate=True).then_inc(z2_step, 1)

            def weights_b(h):
                for m in range(TT):
                    s = TT * h + m
                    z = zb[:, OB[m]:OB[m] + WB[m]]
                    dve.wait_ge(e_ready, s + 1)
                    dve.reciprocal(row_inv[:, m:m + 1], row_sum[:, m:m + 1]).then_inc(inv_ready, 1)
                    dve.wait_ge(inv_ready, s + 1)
                    dve.tensor_scalar(z, z, row_inv[:, m:m + 1], None, ALU.mult).then_inc(w_ready, 1)

            for h in range(H):
                scores_b(h)
                weights_b(h)
                for m in range(TT):
                    s = TT * h + m
                    dve.wait_ge(wt_hi_ready, s + 1)
                    src = bank[4 + m % 2][:, 0:WB[m]].rearrange("p (n t) -> p n t", t=P)
                    low(wt_lo[:, 0:m + 1, m * P:(m + 1) * P], src, wt_hi[:, 0:m + 1, m * P:(m + 1) * P]).then_inc(wt_ready, 1)
                for d in range(DT):
                    dve.wait_ge(mix_hi, KD + DT * h + d + 1)
                    low(q_lo[:, DT * h + d, :], bank[6 + d][:, :], q_hi[:, DT * h + d, :]).then_inc(mix_lo, 1)
            residual("o1", 2)
            norm(2)

            dve.wait_ge(router_done, 1)
            dve.tensor_copy(logits[:, :, :], bank[6][:, 0:TT * NE].rearrange("p (t e) -> p t e", e=NE)).then_inc(route_step, 1)
            dve.wait_ge(route_step, 1)
            for t in range(TT):
                op = dve.max(top[:, t, :], logits[:, t, :])
            op.then_inc(route_step, 1)
            dve.wait_ge(route_step, 2)
            minus(g_diff[:, :], top[:, :, 1], top[:, :, 0]).then_inc(route_step, 1)
            for t in range(TT):
                op = dve.max_index(top_at[:, t, :], top[:, t, :], logits[:, t, :])
            op.then_inc(route_step, 1)
            dve.wait_ge(route_step, 4)
            dve.tensor_copy(top_f[:, :, :], top_at[:, :, 0:2]).then_inc(route_step, 1)
            dve.wait_ge(route_step, 5)
            for c in range(2):
                for t in range(TT):
                    op = dve.tensor_scalar(sel[:, c, t, :], lanes[:, :], top_f[:, t, c:c + 1], None, ALU.is_equal)
            op.then_inc(route_step, 1)
            dve.wait_ge(route_step, 6)
            dve.tensor_tensor(sel_any[:, :, :], sel[:, 0, :, :], sel[:, 1, :, :], ALU.add).then_inc(route_step, 1)
            dve.wait_ge(gate_exp, 1)
            dve.tensor_scalar(g_sum[:, :], g_exp[:, :], 1.0, None, ALU.add).then_inc(gate_step, 1)
            dve.wait_ge(gate_step, 1)
            dve.reciprocal(g_one[:, :], g_sum[:, :]).then_inc(gate_step, 1)
            dve.wait_ge(gate_step, 2)
            dve.tensor_tensor(g_two[:, :], g_exp[:, :], g_one[:, :], ALU.mult).then_inc(gate_step, 1)
            dve.wait_ge(ranked, 1)
            for t in range(TT):
                op = dve.tensor_tensor(slot_all[:, t, :], bank[7][:, t * NE:(t + 1) * NE], lane_slots[:, :], ALU.add)
            op.then_inc(slot_step, 1)
            counts = bank[7][:, TT * NE:(TT + 1) * NE]
            for b in tiles_f:
                dve.memset(b[:, NE:], 1.0)
            dve.tensor_scalar(tiles_f[0][:, 0:NE], counts, float(P), 1.0, ALU.is_gt, ALU.add).then_inc(slot_step, 1)
            dve.wait_ge(slot_step, 2)
            for c in range(2):
                dve.tensor_tensor(sel[:, c, :, :], sel[:, c, :, :], slot_all[:, :, :], ALU.mult)
            dve.scalar_tensor_tensor(out=tiles_f[1][:, 0:NE], in0=counts, scalar=2.0 * P, in1=tiles_f[0][:, 0:NE],
                                     op0=ALU.is_gt, op1=ALU.add).then_inc(slot_step, 1)
            dve.wait_ge(slot_step, 3)
            for c in range(2):
                dve.tensor_reduce(slot_f[:, c, :], sel[:, c, :, :], AX.X, ALU.add)
            dve.scalar_tensor_tensor(out=tiles_f[0][:, 0:NE], in0=counts, scalar=3.0 * P, in1=tiles_f[1][:, 0:NE],
                                     op0=ALU.is_gt, op1=ALU.add).then_inc(slot_step, 1)
            dve.wait_ge(slot_step, 4)
            dve.tensor_copy(slot_i[:, :, :], slot_f[:, :, :]).then_inc(slots_ready, 1)
            dve.tensor_copy(tiles_i[:, :], tiles_f[0][:, :]).then_inc(tiles_ready, 1)
            embed(1)
            dve.wait_ge(list_turned, 1)
            dve.tensor_copy(place_c[:, :], bank[6][:, 0:SLOT_TILES]).then_inc(list_step, 1)
            dve.wait_ge(list_step, 1)
            dve.tensor_copy(place_i[:, :], place_c[:, :])
            for i in range(2):
                op = dve.tensor_scalar(past[i][:, :], place_c[:, :], float(SEQ * (i + 1)), -float(SEQ), ALU.is_ge, ALU.mult)
            op.then_inc(list_step, 1)
            dve.wait_ge(list_step, 2)
            dve.tensor_tensor(past[0][:, :], past[0][:, :], past[1][:, :], ALU.add).then_inc(list_step, 1)
            dve.wait_ge(list_step, 3)
            dve.tensor_tensor(token_i[:, :], past[0][:, :], place_c[:, :], ALU.add).then_inc(list_ready, 1)

            q0 = BASE["moe"] // RAW
            for t in range(TT):
                dve.memset(he[:, t, FE:], 0.0)

            def count(e):
                return dve.value_load(tiles_i[0:1, bass.ds(e, 1)], min_val=1, max_val=TT)

            def x_low(e):
                def body(n):
                    for t in range(n):
                        dve.wait_ge(xg_hi_ready, TT * e + t + 1)
                        for b in range(2):
                            k, s = slice(4 * b, 4 * b + 4), slice(t * P, (t + 1) * P)
                            op = low(x_lo[:, k, s], bank[4 + t % 2 * 2 + b][:, :].rearrange("p (k t) -> p k t", t=P),
                                     x_hi[:, k, s])
                        op.then_inc(xg_ready, share(t, n))
                by_tiles(dve, count(e), body)

            def first_product(e):
                def body(n):
                    for c in range(8):
                        half, up, kh = c // 4, c // 2 % 2, c % 2
                        split_lo(q0 + 3 * e + (c + 1) // RAW, (c + 1) % RAW, 4 * FC if c < 7 else 1536)
                        if up == 1 and kh == 1:
                            dve.wait_ge(chunk_done, 4 * q0 + 12 * e + c + 1)
                            for t in range(n):
                                o = he[:, t, half * FC:(half + 1) * FC]
                                dve.wait_ge(silu_ready, 8 * e + half * TT + t + 1)
                                dve.tensor_tensor(o, o, bank[4 + t][:, 0:FC], ALU.mult).then_inc(he_ready, share(t, n))
                    for t in range(n):
                        dve.wait_ge(het_hi_ready, TT * e + t + 1)
                        s = slice(t * P, (t + 1) * P)
                        low(het_lo[:, 0:4, s], bank[t % 2 * 2][:, :].rearrange("p (k t) -> p k t", t=P), het_hi[:, 0:4, s])
                        low(het_lo[:, 4:KE, s], bank[t % 2 * 2 + 1][:, 0:2 * P].rearrange("p (k t) -> p k t", t=P),
                            het_hi[:, 4:KE, s]).then_inc(het_ready, share(t, n))
                by_tiles(dve, count(e), body)

            def second_product(e):
                for c in range(4):
                    if c < 3:
                        split_lo(q0 + 3 * e + 2, c + 1, 1536, c % 2 == 0)
                    else:
                        split_lo(q0 + 3 * e + 3, 0, 4 * FC)

            x_low(0)
            with dve.Fori(0, NE) as e:
                first_product(e)
                x_low(e + 1)
                second_product(e)
            for t in range(TT):
                dve.wait_ge(y_loaded[t], 32)
                dve.tensor_scalar(y_one[:, t, :], y_one[:, t, :], g_one[:, t:t + 1], None, ALU.mult).then_inc(y_step, 1)
                dve.wait_ge(y_step, t + 1)
                dve.scalar_tensor_tensor(out=y_one[:, t, :], in0=y_two[:, t, :], scalar=g_two[:, t:t + 1],
                                         in1=y_one[:, t, :], op0=ALU.mult, op1=ALU.add).then_inc(combined, 1)
            for k in range(KD):
                dve.wait_ge(acc_turned, k + 1)
                add_residual(3, k, bank[k % 4][:, :]).then_inc(drained, 1)
            norm(3)
            gate(1)
            for t in range(TT):
                dve.wait_ge(final_turned, t + 1)
                dve.tensor_copy(o_tok[:, t, 512:1024], bank[2 * t + 1][:, :]).then_inc(final_dve, 1)


_INS = ["x", "p", "a_w_qkv", "a_w_o", "kvf_w", "kvf_b_f", "b_w_q", "b_w_o", "ffn_w_gu", "ffn_w_down",
        "moe_w_router", "moe_w_gu", "moe_w_down", "ple_w_proj", "ple_w_gate", "ln_g", "ln_b"]


def kernel(**inputs):
    import numpy as np
    import concourse.bacc as bacc
    from concourse.bass_utils import run_bass_kernel_spmd

    nc = bacc.Bacc("TRN2", target_bir_lowering=False, num_devices=1)
    arrays, args = {}, []
    for name in _INS:
        a = np.ascontiguousarray(inputs[name])
        arrays[name] = a
        args.append(nc.dram_tensor(name, a.shape, mybir.dt.from_np(a.dtype), kind="ExternalInput").ap())
    args.append(nc.dram_tensor("result", (1, SEQ, D), F32, kind="ExternalOutput").ap())
    build(nc, *args)
    return run_bass_kernel_spmd(nc, [arrays], core_ids=[0]).results[0]["result"]
```

```python
from contextlib import ExitStack

import concourse.bass as bass
from concourse import mybir

F32 = mybir.dt.float32
R32 = mybir.dt.float32r
U32 = mybir.dt.uint32
I32 = mybir.dt.int32
ACT = mybir.ActivationFunctionType
ALU = mybir.AluOpType
AX = mybir.AxisListType

P = 128
SEQ = 512
D = 1024
KD = D // P
TT = SEQ // P
H = 4
DH = D // H
DT = DH // P
FF = 2816
KF = FF // P
NE = 8
FE = 704
FC = (3 * P, FE - 3 * P)
KE = -(-FE // P)
FE_LAST = FE - (KE - 1) * P
PD = 256
KP = PD // P
DEPTH = 2
ALPHA = (2.0 * DEPTH) ** 0.25
SCALE = 1.0 / float(DH) ** 0.5
EPS = 1e-5
NEG = -1e30
BIG = 3e38

RAW = 4
SPLIT = 2
DEEP = 4
CH = 1536

WID = [SEQ - n * P for n in range(TT)]
OFF = [sum(WID[:n]) for n in range(TT)]
TRI = sum(WID)

PHASES = [
    ("q0", 8, KD * P), ("k0", 8, KD * P), ("v0", 8, 4 * 256), ("o0", 8, KD * P),
    ("gu", 2 * KF, KD * P), ("down", 16, KF // 2 * P), ("proj0", 4, KP * 256), ("gate0", 8, KD * P),
    ("q1", 8, KD * P), ("k1", 8, KD * P), ("v1", 8, 4 * 256), ("o1", 8, KD * P),
    ("proj1", 4, KP * 256), ("moe", NE * 12, 4 * FC[0]), ("gate1", 8, KD * P),
]
BASE, SIZE, COUNT, NEXT_SIZE = {}, {}, {}, {}
_at = 0
for _n, (_name, _count, _size) in enumerate(PHASES):
    BASE[_name], SIZE[_name], COUNT[_name] = _at, _size, _count
    NEXT_SIZE[_name] = PHASES[_n + 1][2] if _n + 1 < len(PHASES) else 0
    _at += _count
CHUNKS = _at
assert all(b % RAW == 0 for b in BASE.values())

PROJ_BANKS = [(0, 2, 6, 4), (0, 2, 0, 2)]

SLOT_TILES = (NE + 1) * TT


def by_tiles(eng, count, body):
    with eng.If(count < 2):
        body(1)
    with eng.Else():
        with eng.If(count < 3):
            body(2)
        with eng.Else():
            with eng.If(count < 4):
                body(3)
            with eng.Else():
                body(4)


def share(t, n):
    return 1 if t < n - 1 else TT - n + 1


DRAINED, _n = {}, 0
for _name in ("q0", "k0", "v0", "o0", "gu", "down", "proj0", "gate0", "q1", "k1", "v1", "o1", "proj1", "turn", "gate1"):
    DRAINED[_name] = _n
    _n += 0 if _name == "proj0" else COUNT.get(_name, KD)
OUT_HI, _n = {}, 0
for _name in ("q0", "k0", "v0", "gu", "q1", "k1", "v1"):
    OUT_HI[_name] = _n
    _n += COUNT[_name]
EARLY = ("q0", "gu", "gate0", "q1")
LAG = 3
GATED = {"gu": 0, "gate0": KF, "gate1": KF + KD}


def ahead_of(name, j, q):
    if name in EARLY and isinstance(q, int) and RAW * q + j < BASE[name] + 2:
        return [j + 2] if j == 0 else []
    return [j + 1]


def quads(eng, name, step, peel=False):
    first, rounds = BASE[name] // RAW, COUNT[name] // RAW
    start = 1 if name in EARLY else 0
    end = rounds - 1 if peel else rounds

    def straight(i0, i1):
        for i in range(i0, i1):
            for j in range(RAW):
                step(first + i, i, j, i == rounds - 1 and j == RAW - 1)
    if end - start > 2:
        straight(0, start)
        with eng.Fori(start, end) as i:
            for j in range(RAW):
                step(first + i, i, j, False)
        straight(end, rounds)
    else:
        straight(0, rounds)


def build(nc, x, p, a_w_qkv, a_w_o, kvf_w, kvf_b_f, b_w_q, b_w_o, ffn_w_gu, ffn_w_down,
          moe_w_router, moe_w_gu, moe_w_down, ple_w_proj, ple_w_gate, ln_g, ln_b, out):
    with ExitStack() as ctx:
        base = (nc.sbuf_base + 63) // 64 * 64
        place = [base]

        def at(name, shape, dt, offset):
            return nc.alloc_sbuf_tensor_at(name, shape, dt, offset=offset)

        def sb(name, shape, dt=F32):
            n = 4
            for s in shape[1:]:
                n *= s
            t = at(name, shape, dt, place[0])
            place[0] += (n + 31) // 32 * 32
            return t

        def sem(name):
            return ctx.enter_context(nc.semaphore(name))

        x_exact = sb("x_exact", [P, KD, SEQ])
        work0 = place[0]
        x_hi = sb("x_hi", [P, KD, SEQ], R32)
        x_lo = sb("x_lo", [P, KD, SEQ], R32)
        raw = [sb(f"raw{i}", [P, CH]) for i in range(RAW)]
        w_hi = [sb(f"w_hi{i}", [P, CH], R32) for i in range(SPLIT)]
        w_lo = [sb(f"w_lo{i}", [P, CH], R32) for i in range(SPLIT)]
        ident = sb("ident", [P, P])
        ones = sb("ones", [P, P])
        mean_f = sb("mean_f", [P, P])
        mean_r = sb("mean_r", [P, P], R32)
        neg_ones = sb("neg_ones", [P, P], R32)
        neg_incl = sb("neg_incl", [P, P], R32)
        cum = sb("cum", [P, P])
        keep = sb("keep", [P, P])
        floor_a = sb("floor_a", [P, P])
        clip_b = sb("clip_b", [P, P])
        ln_rows = sb("ln_rows", [64, P])
        ln_cols = sb("ln_cols", [P, 64])
        w_f = sb("w_f", [P, KD, H])
        w_r = sb("w_r", [P, KD, NE])
        b_f = sb("b_f", [P, H])
        p_tok = sb("p_tok", [P, TT, PD])
        f_row = at("f_row", [H, SEQ], F32, place[0])
        h_tmp = [sb(f"h_tmp{i}", [P, SEQ]) for i in range(2)]
        eps = sb("eps", [P, 1])
        log_f = sb("log_f", [P, TT, H])
        f_abs = sb("f_abs", [P, TT, H])
        f_pre = sb("f_pre", [P, TT, H])
        c_col = sb("c_col", [P, TT, H])
        neg_max = sb("neg_max", [P, TT])
        row_sum = sb("row_sum", [P, TT])
        row_inv = sb("row_inv", [P, TT])
        logits = sb("logits", [P, TT, NE])
        top = sb("top", [P, TT, NE])
        top_at = sb("top_at", [P, TT, NE], U32)
        top_f = sb("top_f", [P, TT, 2])
        g_diff = sb("g_diff", [P, TT])
        g_exp = sb("g_exp", [P, TT])
        g_sum = sb("g_sum", [P, TT])
        g_one = sb("g_one", [P, TT])
        g_two = sb("g_two", [P, TT])
        lanes = sb("lanes", [P, NE])
        lane_slots = sb("lane_slots", [P, NE])
        slot_f = sb("slot_f", [P, 2, TT])
        slot_i = sb("slot_i", [P, 2, TT], I32)
        tiles_f = [sb(f"tiles_f{i}", [P, NE + 1]) for i in range(2)]
        tiles_i = sb("tiles_i", [P, NE + 1], I32)
        place_f = sb("place_f", [P, 2, TT])
        gather_i = sb("gather_i", [P, TT], I32)
        store_i = sb("store_i", [P, TT], I32)
        place_i = sb("place_i", [P, SLOT_TILES], I32)
        token_i = sb("token_i", [P, SLOT_TILES], I32)
        G = (place[0] + 63) // 64 * 64
        KB = 1024
        assert G + 96 * KB <= nc.sbuf_usable_end, (G, nc.sbuf_usable_end)

        x_tok = at("x_tok", [P, TT, D], F32, G)
        neg_incl_f = at("neg_incl_f", [P, P], F32, G + 90 * KB)
        q_hi = at("q_hi", [P, KD, SEQ], R32, G)
        q_lo = at("q_lo", [P, KD, SEQ], R32, G + 16 * KB)
        k_hi = at("k_hi", [P, KD, SEQ], R32, G + 32 * KB)
        k_lo = at("k_lo", [P, KD, SEQ], R32, G + 48 * KB)
        v_hi = at("v_hi", [P, TT, D], R32, G + 64 * KB)
        v_lo = at("v_lo", [P, TT, D], R32, G + 80 * KB)
        h_hi = at("h_hi", [P, KF, SEQ], R32, G)
        h_lo = at("h_lo", [P, KF, SEQ], R32, G + 44 * KB)
        proj = at("proj", [P, KD, SEQ], F32, G)
        sig = at("sig", [P, KD, SEQ], F32, G + 16 * KB)
        pt_hi = [at(f"pt_hi{l}", [P, KP, SEQ], R32, G + (88, 28)[l] * KB) for l in range(2)]
        pt_lo = [at(f"pt_lo{l}", [P, KP, SEQ], R32, G + (92, 32)[l] * KB) for l in range(2)]
        sq = [at(f"sq{i}", [P, SEQ], F32, G + (58 + 2 * i) * KB) for i in range(2)]
        rstd = at("rstd", [P, SEQ], F32, G + 62 * KB)
        he = at("he", [P, TT, KE * P], F32, G + 16 * KB)
        het_hi = at("het_hi", [P, KE, SEQ], R32, G + 28 * KB)
        het_lo = at("het_lo", [P, KE, SEQ], R32, G + 40 * KB)
        xg = at("xg", [P, TT, D], F32, G + 52 * KB)
        x_rows = at("x_rows", [P, TT, D], F32, G + 68 * KB)
        y_tok = at("y_tok", [P, TT, D], F32, G + 52 * KB)
        sel = at("sel", [P, 2, TT, NE], F32, G + 92 * KB)
        sel_any = at("sel_any", [P, TT, NE], F32, G + 92 * KB + 256)
        slot_all = at("slot_all", [P, TT, NE], F32, G + 92 * KB + 384)
        list_rows = at("list_rows", [SLOT_TILES, P], F32, G + 92 * KB + 512)
        logits_e = at("logits_e", [NE, SEQ], F32, G + 94 * KB)
        place_c = at("place_c", [P, SLOT_TILES], F32, G + 93 * KB + 256)
        past = [at(f"past{i}", [P, SLOT_TILES], F32, G + 93 * KB + 512 + 256 * i) for i in range(2)]
        w_hi += [at(f"w_hi{i}", [P, CH], R32, G + (68 + 12 * (i - SPLIT)) * KB) for i in range(SPLIT, DEEP)]
        w_lo += [at(f"w_lo{i}", [P, CH], R32, G + (74 + 12 * (i - SPLIT)) * KB) for i in range(SPLIT, DEEP)]
        y_one = at("y_one", [P, TT, D], F32, G + 16 * KB)
        y_two = at("y_two", [P, TT, D], F32, G + 32 * KB)
        o_tok = at("o_tok", [P, TT, D], F32, G)

        wk = lambda name, shape, dt, o: at(name, shape, dt, work0 + o)
        ln_a = wk("ln_a", [P, TRI], F32, 0)
        sp = wk("sp", [P, TRI], F32, 5 * KB)
        sp_hi = wk("sp_hi", [P, TRI], R32, 10 * KB)
        sp_lo = wk("sp_lo", [P, TRI], R32, 15 * KB)
        a_hi = wk("a_hi", [P, TRI], R32, 20 * KB)
        a_lo = wk("a_lo", [P, TRI], R32, 25 * KB)
        a_diag = wk("a_diag", [P, TT, P], F32, 30 * KB)
        zb = wk("zb", [P, TRI], F32, 0)
        wt_hi = wk("wt_hi", [P, TT, SEQ], R32, 5 * KB)
        wt_lo = wk("wt_lo", [P, TT, SEQ], R32, 13 * KB)
        c_row = wk("c_row", [P, H, SEQ], F32, 21 * KB)
        c_diag = wk("c_diag", [P, TT, P], F32, 29 * KB)
        WB = [(m + 1) * P for m in range(TT)]
        OB = [sum(WB[:m]) for m in range(TT)]

        bank = [ctx.enter_context(nc.psum_tensor(f"bank{i}", [P, 512], F32)) for i in range(8)]

        place_of = nc.dram_tensor("place_of", (SLOT_TILES * P, 1), F32, kind="Internal").ap()
        x_dram = nc.dram_tensor("x_dram", (SEQ, D), F32, kind="Internal").ap()
        y_dram = nc.dram_tensor("y_dram", (2 * SEQ + P, D), F32, kind="Internal").ap()

        raw_loaded = [sem(f"raw_loaded{i}") for i in range(RAW)]
        last_loaded = [sem(f"last_loaded{i}") for i in range(2)]
        small_loaded = sem("small_loaded")
        ln_loaded = sem("ln_loaded")
        x_loaded = [sem(f"x_loaded{i}") for i in range(4)]
        p_loaded = sem("p_loaded")
        out_stored = sem("out_stored")
        hi_ready = sem("hi_ready")
        lo_ready = sem("lo_ready")
        chunk_done = sem("chunk_done")
        drained = sem("drained")
        out_hi = sem("out_hi")
        gated = sem("gated")
        hidden = sem("hidden")
        built = sem("built")
        consts = sem("consts")
        turned = sem("turned")
        turned_out = sem("turned_out")
        turned_hi = sem("turned_hi")
        turned_lo = sem("turned_lo")
        summed = sem("summed")
        y_hi_ready = sem("y_hi_ready")
        mean_done = sem("mean_done")
        centred = sem("centred")
        squared = sem("squared")
        var_done = sem("var_done")
        std_ready = sem("std_ready")
        rstd_ready = sem("rstd_ready")
        normed = sem("normed")
        affine = sem("affine")
        x_ready = sem("x_ready")
        embedded = sem("embedded")
        proj_out = sem("proj_out")
        ple_step = sem("ple_step")
        z_done = sem("z_done")
        absed = sem("absed")
        exped = sem("exped")
        logged = sem("logged")
        sp_raw = sem("sp_raw")
        sp_ready = sem("sp_ready")
        sp_hi_ready = sem("sp_hi_ready")
        sp_lo_ready = sem("sp_lo_ready")
        tail_done = sem("tail_done")
        diag_cut = sem("diag_cut")
        a_ready = sem("a_ready")
        a_hi_ready = sem("a_hi_ready")
        a_lo_ready = sem("a_lo_ready")
        mixed = sem("mixed")
        mix_hi = sem("mix_hi")
        mix_lo = sem("mix_lo")
        f_done = sem("f_done")
        f_turned = sem("f_turned")
        f_step = sem("f_step")
        f_act = sem("f_act")
        c_done = sem("c_done")
        c_copied = sem("c_copied")
        diag_ready = sem("diag_ready")
        row_done = sem("row_done")
        row_copied = sem("row_copied")
        z2_done = sem("z2_done")
        z2_step = sem("z2_step")
        e_ready = sem("e_ready")
        inv_ready = sem("inv_ready")
        w_ready = sem("w_ready")
        w_turned = sem("w_turned")
        wt_hi_ready = sem("wt_hi_ready")
        wt_ready = sem("wt_ready")
        router_done = sem("router_done")
        logits_turned = sem("logits_turned")
        route_step = sem("route_step")
        gate_exp = sem("gate_exp")
        gate_step = sem("gate_step")
        slot_step = sem("slot_step")
        ranked = sem("ranked")
        slots_ready = sem("slots_ready")
        tiles_ready = sem("tiles_ready")
        rows_turned = sem("rows_turned")
        rows_copied = sem("rows_copied")
        list_cleared = sem("list_cleared")
        listed = sem("listed")
        list_loaded = sem("list_loaded")
        list_turned = sem("list_turned")
        list_step = sem("list_step")
        list_ready = sem("list_ready")
        indexed = sem("indexed")
        xg_loaded = sem("xg_loaded")
        first_turned = sem("first_turned")
        xg_turned = sem("xg_turned")
        xg_hi_ready = sem("xg_hi_ready")
        xg_ready = sem("xg_ready")
        silu_ready = sem("silu_ready")
        he_ready = sem("he_ready")
        he_turned = sem("he_turned")
        het_hi_ready = sem("het_hi_ready")
        het_ready = sem("het_ready")
        banks_out = sem("banks_out")
        rows_stored = sem("rows_stored")
        y_stored = sem("y_stored")
        y_loaded = [sem(f"y_loaded{t}") for t in range(4)]
        y_step = sem("y_step")
        combined = sem("combined")
        acc_turned = sem("acc_turned")
        final_turned = sem("final_turned")
        final_dve = sem("final_dve")
        final_act = sem("final_act")

        def cols(w, c, n=P):
            return w.rearrange("(k p) n -> p k n", p=P)[:, :, bass.ds(c, n)]

        def view(slot, k):
            return raw[slot][:, :].rearrange("p (k n) -> p k n", k=k)

        def flat(slot, k, n):
            return raw[slot][:, 0:k * n].rearrange("p (k n) -> p k n", k=k)

        BUILT = 8
        CONSTS = 2
        block = ctx.enter_context(nc.Block())

        @block.sync
        def _(sp_eng):
            def slot_free(q, j):
                sp_eng.wait_ge(lo_ready, 4 * q + j - RAW + 1)

            def from_cols(w, col0, k=KD, n=P):
                def step(q, i, j, last):
                    if not isinstance(q, int) or q > 0:
                        slot_free(q, j)
                    sp_eng.dma_start(flat(j, k, n), cols(w, col0 + (RAW * i + j) * n, n)).then_inc(raw_loaded[j], 16)
                return step

            xr = x.rearrange("b (t p) d -> (b p) t d", p=P)
            load_q = from_cols(a_w_qkv[0], 0)
            for part in range(4):
                f = slice(part * 256, (part + 1) * 256)
                sp_eng.dma_start(x_tok[:, :, f], xr[:, :, f]).then_inc(x_loaded[part], 16)
                if part < 2:
                    load_q(0, 0, part, False)
            sp_eng.dma_start(ln_rows[0:32, :], ln_g.rearrange("l w (k p) -> (l w k) p", p=P)).then_inc(ln_loaded, 16)
            sp_eng.dma_start(ln_rows[32:64, :], ln_b.rearrange("l w (k p) -> (l w k) p", p=P)).then_inc(ln_loaded, 16)

            def v_step(w, col0):
                wv = w.rearrange("(g k p) n -> g p k n", p=P, g=2)

                def step(q, i, j, last):
                    slot_free(q, j)
                    sp_eng.dma_start(flat(j, 4, 256), wv[j % 2][:, :, bass.ds(col0 + (2 * i + j // 2) * 256, 256)]
                                     ).then_inc(raw_loaded[j], 16)
                return step

            def gu_step(q, i, j, last):
                slot_free(q, j)
                sp_eng.dma_start(flat(j, KD, P), cols(ffn_w_gu[0], (2 * i + j // 2) * P + (j % 2) * FF)
                                 ).then_inc(raw_loaded[j], 16)

            def down_step(q, i, j, last):
                wd = ffn_w_down[0].rearrange("(g k p) n -> g p k n", p=P, g=2)
                slot_free(q, j)
                sp_eng.dma_start(flat(j, KF // 2, P), wd[j % 2][:, :, bass.ds((2 * i + j // 2) * P, P)]
                                 ).then_inc(raw_loaded[j], 16)

            def load_small():
                sp_eng.dma_start(w_f[:, :, :], cols(kvf_w, 2 * D, H)).then_inc(small_loaded, 16)
                sp_eng.dma_start(w_r[:, :, :], cols(moe_w_router[0], 0, NE)).then_inc(small_loaded, 16)
                sp_eng.dma_start(b_f[:, :], kvf_b_f.rearrange("(a h) -> a h", a=1).to_broadcast([P, H])).then_inc(small_loaded, 16)

            def load_p(layer):
                if layer:
                    sp_eng.wait_ge(turned, KD + KP + 1)
                sp_eng.dma_start(p_tok[:, :, :], p[layer].rearrange("b (t p) d -> (b p) t d", p=P)).then_inc(p_loaded, 16)

            def q0_step(q, i, j, last):
                if 4 * i + j >= 2:
                    load_q(q, i, j, last)
            quads(sp_eng, "q0", q0_step)
            load_small()
            load_p(0)
            quads(sp_eng, "k0", from_cols(a_w_qkv[0], D))
            quads(sp_eng, "v0", v_step(a_w_qkv[0], 2 * D))
            quads(sp_eng, "o0", from_cols(a_w_o[0], 0))
            quads(sp_eng, "gu", gu_step)
            quads(sp_eng, "down", down_step)
            quads(sp_eng, "proj0", from_cols(ple_w_proj[0], 0, KP, 256))
            quads(sp_eng, "gate0", from_cols(ple_w_gate[0], 0))
            load_p(1)
            quads(sp_eng, "q1", from_cols(b_w_q[0], 0))
            quads(sp_eng, "k1", from_cols(kvf_w, 0))
            quads(sp_eng, "v1", v_step(kvf_w, D))
            quads(sp_eng, "o1", from_cols(b_w_o[0], 0))
            quads(sp_eng, "proj1", from_cols(ple_w_proj[1], 0, KP, 256))
            q0 = BASE["moe"] // RAW
            with sp_eng.Fori(0, NE) as e:
                for c in range(8):
                    half, up, kh = c // 4, c // 2 % 2, c % 2
                    col = up * FE + half * FC[0]
                    src = moe_w_gu[0][bass.ds(e, 1), kh * 4 * P:(kh + 1) * 4 * P, col:col + FC[half]]
                    slot_free(q0 + 3 * e + c // RAW, c % RAW)
                    sp_eng.dma_start(flat(c % RAW, 4, FC[half]), src.rearrange("e (k p) n -> p (e k) n", p=P)
                                     ).then_inc(raw_loaded[c % RAW], 16)
                for c in range(4):
                    full, r0, col = (3, 2)[c % 2], c % 2 * 3 * P, c // 2 * 512
                    slot_free(q0 + 3 * e + 2, c)
                    src = moe_w_down[0][bass.ds(e, 1), r0:r0 + full * P, col:col + 512]
                    sp_eng.dma_start(flat(c, 3, 512)[:, 0:full, :], src.rearrange("e (k p) n -> p (e k) n", p=P)
                                     ).then_inc(raw_loaded[c], 16)
                    if c % 2:
                        src = moe_w_down[0][bass.ds(e, 1), (KE - 1) * P:FE, col:col + 512]
                        sp_eng.dma_start(raw[c][0:FE_LAST, 1024:1536], src.rearrange("e p n -> (e p) n")
                                         ).then_inc(last_loaded[c // 2], 16)
            quads(sp_eng, "gate1", from_cols(ple_w_gate[1], 0))
            for t in range(TT):
                sp_eng.wait_ge(final_dve, t + 1)
                sp_eng.wait_ge(final_act, t + 1)
                sp_eng.dma_start(out.rearrange("b (t p) d -> (b p) t d", p=P)[:, t, :], o_tok[:, t, :]).then_inc(out_stored, 16)
            sp_eng.wait_ge(out_stored, 16 * TT)

        @block.gpsimd
        def _(pool):
            fills = [(ident, 0.0), (ones, 1.0), (mean_f, 1.0 / D), (neg_incl_f, -1.0), (cum, 1.0), (keep, 1.0),
                     (floor_a, 0.0), (clip_b, BIG)]
            for t, v in fills:
                last = pool.memset(t[:, :], v)
            last.then_inc(built, 1)
            pool.wait_ge(built, 1)
            cuts = [(ident, ALU.not_equal, 1.0, 1, -1),
                    (neg_incl_f, ALU.is_ge, 0.0, 1, -1),
                    (cum, ALU.is_ge, 0.0, -1, 1),
                    (keep, ALU.is_gt, 0.0, -1, 1),
                    (floor_a, ALU.is_gt, NEG, -1, 1),
                    (clip_b, ALU.is_ge, NEG, 1, -1)]
            for t, op, fill, mult, step in cuts:
                pool.affine_select(out=t[:, :], in_=t[:, :], pattern=[[step, P]], compare_op=op, fill=fill,
                                   base=0, channel_multiplier=mult).then_inc(built, 1)
            pool.iota(lanes[:, :], pattern=[[1, NE]], base=0, channel_multiplier=0,
                      allow_small_or_imprecise_dtypes=True)
            pool.iota(lane_slots[:, :], pattern=[[SEQ, NE]], base=0, channel_multiplier=0,
                      allow_small_or_imprecise_dtypes=True)
            pool.iota(place_f[:, :, :], pattern=[[SEQ, 2], [P, TT]], base=0, channel_multiplier=1,
                      allow_small_or_imprecise_dtypes=True).then_inc(built, 1)
            pool.wait_ge(mix_lo, 2 * KD)
            pool.iota(list_rows[:, :], pattern=[[1, P]], base=2 * SEQ, channel_multiplier=0,
                      allow_small_or_imprecise_dtypes=True).then_inc(built, 1)
            pool.wait_ge(built, BUILT + 1)
            by_slot = place_of.rearrange("(c p) o -> c (p o)", p=P)
            pool.dma_start(by_slot, list_rows[:, :]).then_inc(list_cleared, 16)

            pool.wait_ge(list_cleared, 16)
            pool.wait_ge(slots_ready, 1)
            for c in range(2):
                for t in range(TT):
                    pool.indirect_dma_start(place_of, bass.IndirectOffsetOnAxis(ap=slot_i[:, c, t:t + 1], axis=0),
                                            place_f[:, c, t:t + 1], None).then_inc(listed, 16)
            pool.wait_ge(listed, 16 * 2 * TT)
            pool.dma_start(list_rows[:, :], by_slot).then_inc(list_loaded, 16)
            pool.wait_ge(list_ready, 1)
            pool.wait_ge(rows_stored, 16)
            pool.wait_ge(tiles_ready, 1)

            def gather(e, indexed_to):
                pool.tensor_copy(gather_i[:, :], token_i[:, bass.ds(TT * e, TT)]).then_inc(indexed, 1)
                pool.wait_ge(indexed, indexed_to)

                def body(n):
                    for t in range(n):
                        pool.indirect_dma_start(
                            xg[:, t, :], None, x_dram,
                            bass.IndirectOffsetOnAxis(ap=gather_i[:, t:t + 1], axis=0)
                        ).then_inc(xg_loaded, 16 * share(t, n))
                by_tiles(pool, pool.value_load(tiles_i[0:1, bass.ds(e, 1)], min_val=1, max_val=TT), body)

            gather(0, 1)
            with pool.Fori(0, NE) as e:
                pool.wait_ge(xg_turned, TT * e + TT)
                gather(e + 1, 2 * e + 2)

                def store(n):
                    for t in range(n):
                        pool.indirect_dma_start(y_dram, bass.IndirectOffsetOnAxis(ap=store_i[:, t:t + 1], axis=0),
                                                y_tok[:, t, :], None).then_inc(y_stored, 16 * share(t, n))
                pool.tensor_copy(store_i[:, :], place_i[:, bass.ds(TT * e, TT)]).then_inc(indexed, 1)
                pool.wait_ge(indexed, 2 * e + 3)
                pool.wait_ge(banks_out, 8 * e + 16)
                by_tiles(pool, pool.value_load(tiles_i[0:1, bass.ds(e, 1)], min_val=1, max_val=TT), store)
                pool.wait_ge(y_stored, 16 * TT * e + 16 * TT)
            for part in range(4):
                f = slice(part * 256, (part + 1) * 256)
                for c, y in enumerate((y_one, y_two)):
                    rows = y_dram[c * SEQ:(c + 1) * SEQ, f].rearrange("(t p) d -> p t d", p=P)
                    pool.dma_start(y[:, :, f], rows).then_inc(y_loaded[part], 16)

        @block.tensor
        def _(pe):
            def mm3(o, s_hi, s_lo, m_hi, m_lo, start, stop):
                pe.matmul(o, s_hi, m_hi, start=start, stop=False, skip_group_check=True)
                pe.matmul(o, s_hi, m_lo, start=False, stop=False, skip_group_check=True)
                return pe.matmul(o, s_lo, m_hi, start=False, stop=stop, skip_group_check=True)

            def weights(q, j):
                pe.wait_ge(lo_ready, 4 * q + j + 1)

            def free_of(value):
                if not isinstance(value, int) or value > 0:
                    pe.wait_ge(drained, value)

            def tiles(name, m_hi, m_lo, ahead=0, slots=SPLIT, arriving=None):
                def step(q, i, j, last):
                    if arriving is not None and isinstance(i, int) and i == 0 and j < 2:
                        if j:
                            return
                        weights(q, 1)
                        free_of(DRAINED[name])
                        if name == "gate0":
                            pe.wait_ge(proj_out, 1)
                        for k in range(KD + LAG):
                            if k < KD:
                                pe.wait_ge(turned_lo if name == "q0" else x_ready, arriving + k + 1)
                            for c, kk in ((0, k), (1, k - LAG)):
                                if 0 <= kk < KD:
                                    w = slice(kk * P, (kk + 1) * P)
                                    mm = mm3(bank[c][:, :], w_hi[c][:, w], w_lo[c][:, w], m_hi[:, kk, :], m_lo[:, kk, :],
                                             kk == 0, kk == KD - 1)
                                    if kk == KD - 1:
                                        mm.then_inc(chunk_done, 1)
                        return
                    weights(q, j)
                    if name == "gate0" and i == 0 and j == 2:
                        pe.wait_ge(proj_out, 2)
                    if not isinstance(i, int) or i or ahead:
                        free_of(DRAINED[name] + 4 * i + j - 3)
                    elif j == 0:
                        free_of(DRAINED[name])
                    for k in range(KD):
                        w = slice(k * P, (k + 1) * P)
                        mm = mm3(bank[j][:, :], w_hi[j % slots][:, w], w_lo[j % slots][:, w], m_hi[:, k, :], m_lo[:, k, :],
                                 k == 0, k == KD - 1)
                    mm.then_inc(chunk_done, 1)
                quads(pe, name, step)

            def values(name):
                def step(q, i, j, last):
                    weights(q, j)
                    if j % 2 == 0:
                        free_of(DRAINED[name] + (0 if i == 0 and j == 0 else 4 * i + j - 2))
                    for t in range(TT):
                        for k in range(4):
                            w, kk = slice(k * 256, (k + 1) * 256), j % 2 * 4 + k
                            mm = mm3(bank[j // 2 * 4 + t][:, 0:256], x_hi[:, kk, t * P:(t + 1) * P],
                                     x_lo[:, kk, t * P:(t + 1) * P], w_hi[j % 2][:, w], w_lo[j % 2][:, w],
                                     kk == 0, kk == KD - 1)
                    mm.then_inc(chunk_done, 1)
                quads(pe, name, step)

            def mean(n, k):
                name, per = (("o0", 1), ("down", 2), ("o1", 1), ("turn", 1))[n]
                pe.wait_ge(drained, DRAINED[name] + per * (k + 1))
                pe.matmul(bank[4][:, :], mean_r[:, :], x_hi[:, k, :], start=k == 0, stop=False)
                mm = pe.matmul(bank[4][:, :], mean_r[:, :], x_lo[:, k, :], start=False, stop=k == KD - 1)
                if k == KD - 1:
                    mm.then_inc(mean_done, 1)

            def variance(n):
                for k in range(KD):
                    pe.wait_ge(squared, KD * n + k + 1)
                    pe.matmul(bank[5][:, :], mean_f[:, :], sq[k % 2][:, :], start=k == 0, stop=k == KD - 1
                              ).then_inc(var_done, 1)

            def turn_p(layer):
                pe.wait_ge(p_loaded, 16 * (layer + 1))
                for k in range(KP):
                    for t in range(TT):
                        mm = pe.transpose(bank[6 + k][:, t * P:(t + 1) * P], p_tok[:, t, k * P:(k + 1) * P], ident[:, :])
                    mm.then_inc(turned, 1)

            def embed(layer, before_last=lambda: None):
                pe.wait_ge(turned_lo, KD + KP * (layer + 1))
                name = f"proj{layer}"

                def step(q, i, j, last):
                    if last:
                        before_last()
                    weights(q, j)
                    free_of(DRAINED[name] + (0 if layer == 0 else max(0, j - 1)))
                    if layer == 0 and j == 3:
                        pe.wait_ge(centred, 2 * KD)
                        pe.wait_ge(std_ready, 2)
                    for s in range(2):
                        for k in range(KP):
                            w = slice(k * 256 + s * P, k * 256 + (s + 1) * P)
                            mm = mm3(bank[PROJ_BANKS[layer][j] + s][:, :], w_hi[j % 2][:, w], w_lo[j % 2][:, w],
                                     pt_hi[layer][:, k, :], pt_lo[layer][:, k, :], k == 0, k == KP - 1)
                    mm.then_inc(chunk_done, 1)
                quads(pe, name, step)

            pe.wait_ge(built, BUILT)
            for k in range(KD):
                if k % 2 == 0:
                    pe.wait_ge(x_loaded[k // 2], 16)
                if k >= 4:
                    pe.wait_ge(turned_out, k - 3)
                for t in range(TT):
                    mm = pe.transpose(bank[4 + k % 4][:, t * P:(t + 1) * P], x_tok[:, t, k * P:(k + 1) * P], ident[:, :])
                mm.then_inc(turned, 1)

            pe.wait_ge(ln_loaded, 32)
            pe.transpose(bank[2][:, 0:64], ln_rows[:, :], ident[0:64, 0:64]).then_inc(turned, 1)

            tiles("q0", x_hi, x_lo, arriving=0)
            tiles("k0", x_hi, x_lo, ahead=1)
            values("v0")

            def scores_a(h):
                for g, n in enumerate(reversed(range(TT))):
                    if h:
                        pe.wait_ge(a_ready, TT * (h - 1) + g + 1)
                    for d in range(DT):
                        f = DT * h + d
                        mm = mm3(bank[n][:, 0:WID[n]], k_hi[:, f, n * P:(n + 1) * P], k_lo[:, f, n * P:(n + 1) * P],
                                 q_hi[:, f, n * P:], q_lo[:, f, n * P:], d == 0, d == DT - 1)
                    mm.then_inc(z_done, 1)

            def tails_a(h):
                for g, n in enumerate(reversed(range(TT))):
                    if g == 0:
                        pe.wait_ge(sp_lo_ready, 2 * h + 1)
                    if g == TT - 1:
                        pe.wait_ge(sp_lo_ready, 2 * h + 2)
                    for part in (sp_hi, sp_lo):
                        mm = pe.matmul(bank[n][:, 0:WID[n]], neg_incl[:, :], part[:, OFF[n]:OFF[n] + WID[n]],
                                       start=False, stop=n == TT - 1 and part is sp_lo, skip_group_check=True)
                    for m in range(n + 1, TT):
                        for part in (sp_hi, sp_lo):
                            mm = pe.matmul(bank[n][:, (m - n) * P:WID[n]], neg_ones[:, :],
                                           part[:, OFF[m]:OFF[m] + WID[m]], start=False,
                                           stop=m == TT - 1 and part is sp_lo, skip_group_check=True)
                    mm.then_inc(tail_done, 1)

            def mix_a(h):
                pe.wait_ge(a_lo_ready, 2 * h + 2)
                if h:
                    pe.wait_ge(mix_lo, DT * h)
                for d in range(DT):
                    c = slice(h * DH + d * P, h * DH + (d + 1) * P)
                    for n in range(TT):
                        a = slice(OFF[n], OFF[n] + WID[n])
                        mm = mm3(bank[6 + d][:, n * P:], v_hi[:, n, c], v_lo[:, n, c], a_hi[:, a], a_lo[:, a],
                                 n == 0, n == TT - 1)
                    mm.then_inc(mixed, 1)

            pe.wait_ge(drained, DRAINED["o0"] - 2)
            scores_a(0)
            for h in range(H):
                tails_a(h)
                if h + 1 < H:
                    scores_a(h + 1)
                mix_a(h)
            pe.wait_ge(mix_lo, KD)
            tiles("o0", q_hi, q_lo)
            for k in range(KD):
                mean(0, k)
            variance(0)
            tiles("gu", x_hi, x_lo, arriving=0)

            def down_step(q, i, j, last):
                weights(q, j)
                if j % 2 == 0:
                    free_of(DRAINED["down"] + 4 * i + j - 2)
                for k in range(KF // 2):
                    w, kk = slice(k * P, (k + 1) * P), j % 2 * (KF // 2) + k
                    mm = mm3(bank[j // 2][:, :], w_hi[j % 2][:, w], w_lo[j % 2][:, w], h_hi[:, kk, :], h_lo[:, kk, :],
                             kk == 0, kk == KF - 1)
                mm.then_inc(chunk_done, 1)
            pe.wait_ge(drained, DRAINED["down"])
            quads(pe, "down", down_step)
            turn_p(0)
            for k in range(KD):
                mean(1, k)
            variance(1)
            embed(0)
            tiles("gate0", x_hi, x_lo, arriving=KD)
            tiles("q1", x_hi, x_lo, arriving=2 * KD)
            pe.wait_ge(small_loaded, 48)
            pe.wait_ge(embedded, KD)
            for k in range(KD):
                mm = pe.matmul(bank[4][0:H, :], w_f[:, k, :], x_exact[:, k, :], start=k == 0, stop=k == KD - 1)
            mm.then_inc(f_done, 1)
            tiles("k1", x_hi, x_lo, ahead=1)
            pe.wait_ge(f_step, 1)
            for t in range(TT):
                mm = pe.transpose(bank[5][:, t * H:(t + 1) * H], f_row[:, t * P:(t + 1) * P], ident[0:H, 0:H])
            mm.then_inc(f_turned, 1)
            pe.wait_ge(f_step, 2)
            values("v1")
            pe.wait_ge(drained, DRAINED["o1"] - 2)
            pe.wait_ge(f_step, 4)
            for t in range(TT):
                for m in range(t + 1):
                    mm = pe.matmul(bank[0][:, t * H:(t + 1) * H], (cum if m == t else ones)[:, :], log_f[:, m, :],
                                   start=m == 0, stop=m == t)
            mm.then_inc(c_done, 1)

            def gate_rows():
                for h in range(H):
                    pe.wait_ge(diag_ready, h + 1)
                    if h >= 2:
                        pe.wait_ge(row_copied, h - 1)
                    for t in range(TT):
                        mm = pe.matmul(bank[4 + h % 2][:, t * P:(t + 1) * P], ones[:, :], c_diag[:, t, :], start=True, stop=True)
                    mm.then_inc(row_done, 1)

            def scores_b(h):
                for m in range(TT):
                    if h:
                        pe.wait_ge(z2_step, 3 * (TT * (h - 1) + m) + 1)
                    for d in range(DT):
                        f = DT * h + d
                        mm = mm3(bank[m][:, 0:WB[m]], q_hi[:, f, m * P:(m + 1) * P], q_lo[:, f, m * P:(m + 1) * P],
                                 k_hi[:, f, 0:WB[m]], k_lo[:, f, 0:WB[m]], d == 0, d == DT - 1)
                    mm.then_inc(z2_done, 1)

            def turn_b(h):
                for m in range(TT):
                    s = TT * h + m
                    pe.wait_ge(w_ready, s + 1)
                    if s >= 2:
                        pe.wait_ge(wt_ready, s - 1)
                    else:
                        pe.wait_ge(row_copied, H)
                    for n in range(m + 1):
                        mm = pe.transpose(bank[4 + m % 2][:, n * P:(n + 1) * P],
                                          zb[:, OB[m] + n * P:OB[m] + (n + 1) * P], ident[:, :])
                    mm.then_inc(w_turned, 1)

            def mix_b(h):
                pe.wait_ge(wt_ready, TT * (h + 1))
                pe.wait_ge(mix_lo, KD + DT * h)
                for d in range(DT):
                    c = slice(h * DH + d * P, h * DH + (d + 1) * P)
                    for n in range(TT):
                        mm = mm3(bank[6 + d][:, n * P:], v_hi[:, n, c], v_lo[:, n, c], wt_hi[:, n, n * P:], wt_lo[:, n, n * P:],
                                 n == 0, n == TT - 1)
                    mm.then_inc(mixed, 1)

            pe.wait_ge(c_copied, 1)
            scores_b(0)
            pe.wait_ge(drained, DRAINED["o1"])
            gate_rows()
            for h in range(H):
                if h + 1 < H:
                    scores_b(h + 1)
                turn_b(h)
                mix_b(h)
            pe.wait_ge(mix_lo, 2 * KD)
            tiles("o1", q_hi, q_lo)
            for k in range(KD):
                mean(2, k)
            variance(2)
            for k in range(KD):
                pe.wait_ge(affine, 3 * KD + k + 1)
                mm = pe.matmul(bank[5][0:NE, :], w_r[:, k, :], x_exact[:, k, :], start=k == 0, stop=k == KD - 1)
            mm.then_inc(router_done, 1)

            def turn_rows(t):
                if t >= 2:
                    pe.wait_ge(rows_copied, t - 1)
                for k in range(KD):
                    mm = pe.transpose(bank[t % 2 * 2 + k // 4][:, k % 4 * P:(k % 4 + 1) * P],
                                      x_exact[:, k, t * P:(t + 1) * P], ident[:, :])
                mm.then_inc(rows_turned, 1)
            pe.wait_ge(route_step, 1)
            for t in range(TT):
                mm = pe.transpose(bank[6][:, t * NE:(t + 1) * NE], logits_e[:, t * P:(t + 1) * P], ident[0:NE, 0:NE])
            mm.then_inc(logits_turned, 1)
            turn_rows(0)
            turn_rows(1)
            pe.wait_ge(route_step, 8)
            for t in range(TT):
                for m in range(t + 1):
                    pe.matmul(bank[7][:, t * NE:(t + 1) * NE], (keep if m == t else ones)[:, :], sel_any[:, m, :],
                              start=m == 0, stop=m == t)
            for m in range(TT):
                mm = pe.matmul(bank[7][:, TT * NE:(TT + 1) * NE], ones[:, :], sel_any[:, m, :],
                               start=m == 0, stop=m == TT - 1)
            mm.then_inc(ranked, 1)
            turn_rows(2)
            turn_rows(3)
            pe.wait_ge(slots_ready, 1)
            pe.wait_ge(rows_copied, TT)
            turn_p(1)

            def turn_list():
                pe.wait_ge(list_loaded, 16)
                pe.transpose(bank[6][:, 0:SLOT_TILES], list_rows[:, :], ident[0:SLOT_TILES, 0:SLOT_TILES]
                             ).then_inc(list_turned, 1)
            embed(1, turn_list)
            pe.wait_ge(tiles_ready, 1)
            pe.wait_ge(drained, DRAINED["turn"])

            def count(e):
                return pe.value_load(tiles_i[0:1, bass.ds(e, 1)], min_val=1, max_val=TT)

            def turn_tile(t):
                for k in range(KD):
                    mm = pe.transpose(bank[6 - t % 2 * 2 + k // 4][:, k % 4 * P:(k % 4 + 1) * P],
                                      xg[:, t, k * P:(k + 1) * P], ident[:, :])
                return mm

            def turn_first(e):
                pe.wait_ge(xg_loaded, 16 * TT * e + 16 * TT)
                turn_tile(0).then_inc(first_turned, 1)

            def turn_x(e):
                def body(n):
                    pe.wait_ge(first_turned, e + 1)
                    pe.nop().then_inc(xg_turned, share(0, n))
                    for t in range(1, n):
                        if t >= 2:
                            pe.wait_ge(xg_ready, TT * e + t - 1)
                        turn_tile(t).then_inc(xg_turned, share(t, n))
                by_tiles(pe, count(e), body)

            q0 = BASE["moe"] // RAW

            def first_half(t, c, e):
                half, up, kh = c // 4, c // 2 % 2, c % 2
                for k in range(4):
                    w, kk = slice(k * FC[half], (k + 1) * FC[half]), kh * 4 + k
                    mm = mm3(bank[4 * up + t][:, 0:FC[half]], x_hi[:, kk, t * P:(t + 1) * P],
                             x_lo[:, kk, t * P:(t + 1) * P], w_hi[c % DEEP][:, w], w_lo[c % DEEP][:, w],
                             kk == 0, kk == KD - 1)
                return mm

            def second_half(t, c):
                for k in range(3):
                    kk = c % 2 * 3 + k
                    r, w = (FE_LAST if kk == KE - 1 else P), slice(k * 512, (k + 1) * 512)
                    mm = mm3(bank[4 * (c // 2) + t][:, :], het_hi[0:r, kk, t * P:(t + 1) * P],
                             het_lo[0:r, kk, t * P:(t + 1) * P], w_hi[c][0:r, w], w_lo[c][0:r, w],
                             kk == 0, kk == KE - 1)
                return mm

            def turn_hidden(e, half, n):
                for t in range(n):
                    pe.wait_ge(he_ready, 8 * e + half * TT + t + 1)
                    for k in range(3):
                        mm = pe.transpose(bank[4 + t][:, k * P:(k + 1) * P],
                                          he[:, t, (3 * half + k) * P:(3 * half + k + 1) * P], ident[:, :])
                    mm.then_inc(he_turned, share(t, n))

            def until_turned(e):
                def body(n):
                    for c in range(8):
                        weights(q0 + 3 * e + c // RAW, c % RAW)
                        if c == 0:
                            pe.wait_ge(xg_ready, TT * e + TT)
                            pe.wait_ge(banks_out, 8 * e + 4)
                        if c == 2:
                            pe.wait_ge(banks_out, 8 * e + 8)
                        if c == 4:
                            pe.wait_ge(silu_ready, 8 * e + TT)
                        if c == 6:
                            pe.wait_ge(het_ready, 8 * e + TT)
                        for t in range(n):
                            mm = first_half(t, c, e)
                        mm.then_inc(chunk_done, 1)
                        if c == 4:
                            turn_hidden(e, 0, n)
                    weights(q0 + 3 * e + 2, 0)
                    pe.wait_ge(silu_ready, 8 * e + 2 * TT)
                    for t in range(n):
                        mm = second_half(t, 0)
                    mm.then_inc(chunk_done, 1)
                    turn_hidden(e, 1, n)
                    if n > 2:
                        pe.wait_ge(het_ready, 8 * e + 2 * TT)
                    turn_first(e + 1)
                by_tiles(pe, count(e), body)

            def second_product(e):
                def body(n):
                    for c in range(1, 4):
                        weights(q0 + 3 * e + 2, c)
                        if c == 2:
                            pe.wait_ge(xg_ready, TT * e + 2 * TT)
                        for t in range(n):
                            mm = second_half(t, c)
                        mm.then_inc(chunk_done, 1)
                by_tiles(pe, count(e), body)

            pe.wait_ge(list_ready, 1)
            turn_first(0)
            turn_x(0)
            with pe.Fori(0, NE) as e:
                until_turned(e)
                pe.wait_ge(het_ready, 8 * e + 2 * TT)
                turn_x(e + 1)
                second_product(e)
            pe.wait_ge(banks_out, 8 + 8 * NE)
            for part in range(4):
                pe.wait_ge(combined, part + 1)
                for k in range(2 * part, 2 * part + 2):
                    if k >= 4:
                        pe.wait_ge(summed, 3 * KD + k - 3)
                    for t in range(TT):
                        mm = pe.transpose(bank[k % 4][:, t * P:(t + 1) * P], y_one[:, t, k * P:(k + 1) * P], ident[:, :])
                    mm.then_inc(acc_turned, 1)
                if part:
                    mean(3, 2 * part - 2)
                    mean(3, 2 * part - 1)
            mean(3, KD - 2)
            mean(3, KD - 1)
            variance(3)
            tiles("gate1", x_hi, x_lo, slots=DEEP, arriving=3 * KD)
            pe.wait_ge(drained, DRAINED["gate1"] + KD)
            pe.wait_ge(embedded, 2 * KD)
            for t in range(TT):
                for k in range(KD):
                    mm = pe.transpose(bank[2 * t + k // 4][:, k % 4 * P:(k % 4 + 1) * P], x_exact[:, k, t * P:(t + 1) * P],
                                      ident[:, :])
                mm.then_inc(final_turned, 1)

        @block.scalar
        def _(act):
            def split_hi(q, j, n, last64=None):
                act.wait_ge(raw_loaded[j], 16 * (q + 1))
                if not isinstance(q, int) or 4 * q + j >= SPLIT:
                    act.wait_ge(chunk_done, 4 * q + j - 1)
                if last64 is None:
                    act.copy(w_hi[j % 2][:, 0:n], raw[j][:, 0:n]).then_inc(hi_ready, 1)
                else:
                    act.wait_ge(last_loaded[j // 2], last64)
                    act.copy(w_hi[j % 2][:, 0:1024], raw[j][:, 0:1024])
                    act.copy(w_hi[j % 2][0:FE_LAST, 1024:1536], raw[j][0:FE_LAST, 1024:1536]).then_inc(hi_ready, 1)

            def second_early(name):
                split_hi(BASE[name] // RAW, 1, SIZE[name])

            def ahead(name, q, j, last):
                n = NEXT_SIZE[name] if last else SIZE[name]
                for c in ahead_of(name, j, q) if n else []:
                    split_hi(q + c // RAW, c % RAW, n)

            def deep_ahead(q, i, j):
                if 4 * i + j + DEEP - 1 < COUNT["gate1"]:
                    c = 4 * q + j + DEEP - 1
                    act.wait_ge(raw_loaded[c % RAW], 16 * (c // RAW + 1))
                    act.wait_ge(chunk_done, c + 1 - DEEP)
                    act.copy(w_hi[c % DEEP][:, 0:SIZE["gate1"]], raw[c % RAW][:, 0:SIZE["gate1"]]).then_inc(hi_ready, 1)

            def tiles_hi(name, dst, scale=1.0):
                def step(q, i, j, last):
                    ahead(name, q, j, last)
                    act.wait_ge(chunk_done, 4 * q + j + 1)
                    act.activation(dst[:, 4 * i + j, :], bank[j][:, :], ACT.Copy, scale=scale).then_inc(out_hi, 1)
                quads(act, name, step, peel=True)

            def values_hi(name):
                def step(q, i, j, last):
                    ahead(name, q, j, last)
                    if j % 2 == 0:
                        return
                    act.wait_ge(chunk_done, 4 * q + j + 1)
                    g = 2 * i + j // 2
                    for t in range(TT):
                        op = act.copy(v_hi[:, t, g * 256:(g + 1) * 256], bank[j // 2 * 4 + t][:, 0:256])
                    op.then_inc(out_hi, 2)
                quads(act, name, step, peel=True)

            def sum_hi(n, k):
                act.wait_ge(summed, KD * n + k + 1)
                act.copy(x_hi[:, k, :], x_exact[:, k, :]).then_inc(y_hi_ready, 1)

            def residual_hi(name, n):
                def step(q, i, j, last):
                    ahead(name, q, j, last)
                    if name != "down":
                        sum_hi(n, 4 * i + j)
                    elif j % 2:
                        sum_hi(n, 2 * i + j // 2)
                quads(act, name, step, peel=True)

            def project_out(j):
                act.wait_ge(chunk_done, BASE["proj0"] + j + 1)
                for s in range(2):
                    op = act.copy(proj[:, 2 * j + s, :], bank[PROJ_BANKS[0][j] + s][:, :])
                op.then_inc(proj_out, 1)

            def affine_tile(n, k):
                g, b = ln_cols[:, n * KD + k:n * KD + k + 1], ln_cols[:, 32 + n * KD + k:33 + n * KD + k]
                act.wait_ge(normed, KD * n + k + 1)
                if n != 2:
                    act.activation(x_hi[:, k, :], x_exact[:, k, :], ACT.Identity, bias=b, scale=g)
                act.activation(x_exact[:, k, :], x_exact[:, k, :], ACT.Identity, bias=b, scale=g).then_inc(affine, 1)

            def norm(n):
                act.preload_act_table_set("sqrt_and_others")
                for k in range(KD):
                    act.wait_ge(centred, KD * n + k + 1)
                    if k >= 2:
                        act.wait_ge(var_done, KD * n + k - 1)
                    act.activation(sq[k % 2][:, :], x_exact[:, k, :], ACT.Square).then_inc(squared, 1)
                q_proj = BASE["proj0"] // RAW
                if n == 0:
                    second_early("gu")
                if n == 1:
                    ahead("proj0", q_proj, 0, False)
                act.wait_ge(var_done, KD * (n + 1))
                act.wait_ge(consts, CONSTS)
                act.activation(rstd[:, :], bank[5][:, :], ACT.Sqrt, bias=eps[:, 0:1]).then_inc(std_ready, 1)
                if n == 1:
                    ahead("proj0", q_proj, 1, False)
                    project_out(0)
                    affine_tile(n, 0)
                    ahead("proj0", q_proj, 2, False)
                    project_out(1)
                    affine_tile(n, 1)
                    affine_tile(n, 2)
                    affine_tile(n, 3)
                    ahead("proj0", q_proj, 3, True)
                    second_early("gate0")
                    for k in range(4, KD):
                        affine_tile(n, k)
                else:
                    for k in range(KD):
                        affine_tile(n, k)

            def turned_p(layer):
                for k in range(KP):
                    act.wait_ge(turned, KD + 1 + KP * layer + k + 1)
                    act.copy(pt_hi[layer][:, k, :], bank[6 + k][:, :]).then_inc(turned_hi, 1)

            def gate(layer, n):
                name = f"gate{layer}"

                def step(q, i, j, last):
                    if layer:
                        deep_ahead(q, i, j)
                    else:
                        ahead(name, q, j, last)
                    act.wait_ge(chunk_done, 4 * q + j + 1)
                    act.activation(sig[:, 4 * i + j, :], bank[j][:, :], ACT.Sigmoid).then_inc(gated, 1)
                quads(act, name, step, peel=True)
                if layer == 0:
                    second_early("q1")
                    for k in range(KD):
                        act.wait_ge(embedded, k + 1)
                        act.copy(x_hi[:, k, :], x_exact[:, k, :]).then_inc(affine, 1)

            split_hi(0, 0, SIZE["q0"])
            split_hi(0, 1, SIZE["q0"])
            for k in range(KD):
                act.wait_ge(turned_out, k + 1)
                act.copy(x_hi[:, k, :], x_exact[:, k, :]).then_inc(turned_hi, 1)
            tiles_hi("q0", q_hi, SCALE)
            tiles_hi("k0", k_hi)
            values_hi("v0")

            def mix_high(h):
                for d in range(DT):
                    act.wait_ge(mixed, DT * h + d + 1)
                    act.copy(q_hi[:, DT * (h % H) + d, :], bank[6 + d][:, :]).then_inc(mix_hi, 1)

            act.preload_act_table_set("natural_log_exp_and_others")
            act.wait_ge(drained, DRAINED["o0"])
            for h in range(H):
                for g, group in enumerate(((3, 2, 1), (0,))):
                    lo, hi = OFF[group[-1]], OFF[group[0]] + WID[group[0]]
                    if h and g == 0:
                        act.wait_ge(a_lo_ready, 2 * h)
                    for n in group:
                        act.wait_ge(z_done, TT * h + TT - n)
                        op = act.activation(ln_a[:, OFF[n]:OFF[n] + WID[n]], bank[n][:, 0:WID[n]], ACT.Abs)
                    op.then_inc(absed, 1)
                    act.wait_ge(absed, 2 * h + g + 1)
                    act.activation(ln_a[:, lo:hi], ln_a[:, lo:hi], ACT.Exp, scale=-1.0).then_inc(exped, 1)
                    act.wait_ge(exped, 2 * h + g + 1)
                    act.activation(ln_a[:, lo:hi], ln_a[:, lo:hi], ACT.Ln, bias=1.0).then_inc(logged, 1)
                for g, (lo, hi) in enumerate(((OFF[1], TRI), (0, OFF[1]))):
                    act.wait_ge(sp_ready, 2 * h + g + 1)
                    act.copy(sp_hi[:, lo:hi], sp[:, lo:hi]).then_inc(sp_hi_ready, 1)
                if h:
                    mix_high(h - 1)
                for g, n in enumerate(reversed(range(TT))):
                    act.wait_ge(diag_cut, TT * h + g + 1)
                    op = act.activation(ln_a[:, OFF[n]:OFF[n] + P], a_diag[:, n, :], ACT.Exp)
                    if n < TT - 1:
                        op = act.activation(ln_a[:, OFF[n] + P:OFF[n] + WID[n]], bank[n][:, P:WID[n]], ACT.Exp)
                    op.then_inc(a_ready, 1)
            mix_high(H - 1)
            residual_hi("o0", 0)
            norm(0)

            def gu_step(q, i, j, last):
                ahead("gu", q, j, last)
                if j % 2 == 0:
                    return
                m = 2 * i + j // 2
                act.wait_ge(chunk_done, 4 * q + j + 1)
                act.activation(h_tmp[j // 2][:, :], bank[j - 1][:, :], ACT.Silu).then_inc(gated, 1)
                act.wait_ge(hidden, m + 1)
                act.copy(h_hi[:, m, :], h_tmp[j // 2][:, :]).then_inc(out_hi, 2)
            quads(act, "gu", gu_step, peel=True)
            residual_hi("down", 1)
            turned_p(0)
            norm(1)
            gate(0, 1)
            tiles_hi("q1", q_hi, SCALE)
            tiles_hi("k1", k_hi)

            act.preload_act_table_set("natural_log_exp_and_others")
            act.wait_ge(f_step, 2)
            act.activation(f_abs[:, :, :], f_pre[:, :, :], ACT.Abs).then_inc(f_act, 1)
            act.wait_ge(f_act, 1)
            act.activation(f_abs[:, :, :], f_abs[:, :, :], ACT.Exp, scale=-1.0).then_inc(f_act, 1)
            act.wait_ge(f_act, 2)
            act.activation(f_abs[:, :, :], f_abs[:, :, :], ACT.Ln, bias=1.0).then_inc(f_act, 1)
            values_hi("v1")
            act.wait_ge(drained, DRAINED["o1"])
            for h in range(H):
                act.wait_ge(row_done, h + 1)
                act.copy(c_row[:, h, :], bank[4 + h % 2][:, :]).then_inc(row_copied, 1)

            def exp_b(h, m):
                s = TT * h + m
                act.wait_ge(z2_step, 3 * s + 3)
                z = zb[:, OB[m]:OB[m] + WB[m]]
                act.activation(z, z, ACT.Exp, bias=neg_max[:, m:m + 1], accum_out=row_sum[:, m:m + 1]
                               ).then_inc(e_ready, 1)

            def turned_b(h):
                for m in range(TT):
                    s = TT * h + m
                    act.wait_ge(w_turned, s + 1)
                    if m == 0 and h:
                        act.wait_ge(mixed, KD + DT * h)
                    src = bank[4 + m % 2][:, 0:WB[m]].rearrange("p (n t) -> p n t", t=P)
                    act.copy(wt_hi[:, 0:m + 1, m * P:(m + 1) * P], src).then_inc(wt_hi_ready, 1)

            for h in range(H):
                for m in range(TT):
                    exp_b(h, m)
                if h:
                    mix_high(H + h - 1)
                turned_b(h)
            mix_high(2 * H - 1)
            residual_hi("o1", 2)
            norm(2)
            for t in range(TT):
                act.wait_ge(rows_turned, t + 1)
                act.copy(x_rows[:, t, 0:512], bank[t % 2 * 2][:, :])
                act.copy(x_rows[:, t, 512:1024], bank[t % 2 * 2 + 1][:, :]).then_inc(rows_copied, 1)
            act.wait_ge(rows_copied, TT)
            act.dma_start(x_dram.rearrange("(t p) d -> p t d", p=P), x_rows[:, :, :]).then_inc(rows_stored, 16)
            act.wait_ge(route_step, 4)
            act.activation(g_exp[:, :], g_diff[:, :], ACT.Exp).then_inc(gate_exp, 1)

            turned_p(1)
            quads(act, "proj1", lambda q, i, j, last: ahead("proj1", q, j, last))
            q0 = BASE["moe"] // RAW
            act.wait_ge(tiles_ready, 1)

            def count(e):
                return act.value_load(tiles_i[0:1, bass.ds(e, 1)], min_val=1, max_val=TT)

            def x_high(e):
                def body(n):
                    for t in range(n):
                        if t:
                            act.wait_ge(xg_turned, TT * e + t + 1)
                        else:
                            act.wait_ge(first_turned, e + 1)
                        for b in range(2):
                            op = act.copy(x_hi[:, 4 * b:4 * b + 4, t * P:(t + 1) * P],
                                                bank[6 - t % 2 * 2 + b][:, :].rearrange("p (k t) -> p k t", t=P))
                        op.then_inc(xg_hi_ready, share(t, n))
                by_tiles(act, count(e), body)


            def deep_hi(e, c):
                e, c = (e, c) if c < 12 else (e + 1, c - 12)
                q, j = q0 + 3 * e + c // RAW, c % RAW
                act.wait_ge(raw_loaded[j], 16 * (q + 1))
                act.wait_ge(chunk_done, 4 * q + j + 1 - DEEP)
                n = 4 * FC[c // 4] if c < 8 else (1536, 1024)[c % 2]
                op = act.copy(w_hi[j][:, 0:n], raw[j][:, 0:n])
                if c in (9, 11):
                    act.wait_ge(last_loaded[c // 2 % 2], 16 * e + 16)
                    op = act.copy(w_hi[j][0:FE_LAST, 1024:1536], raw[j][0:FE_LAST, 1024:1536])
                op.then_inc(hi_ready, 1)

            def hidden_hi(e, half, n):
                for t in range(n):
                    act.wait_ge(he_turned, 8 * e + half * TT + t + 1)
                    act.copy(het_hi[:, 3 * half:3 * half + 3, t * P:(t + 1) * P],
                             bank[4 + t][:, 0:3 * P].rearrange("p (k t) -> p k t", t=P)
                             ).then_inc(het_hi_ready, share(t, n))

            def until_turned(e):
                def body(n):
                    act.preload_act_table_set("silu_and_others")
                    for c in range(9):
                        deep_hi(e, c + DEEP - 1)
                        if c in (1, 5):
                            half = c // 4
                            act.wait_ge(chunk_done, 4 * q0 + 12 * e + c + 1)
                            for t in range(n):
                                act.activation(he[:, t, half * FC[0]:half * FC[0] + FC[half]],
                                               bank[t][:, 0:FC[half]], ACT.Silu).then_inc(silu_ready, share(t, n))
                        if c in (4, 8):
                            hidden_hi(e, c // 8, n)
                by_tiles(act, count(e), body)

            def second_product(e):
                def body(n):
                    for c in range(1, 4):
                        deep_hi(e, 8 + c + DEEP - 1)
                        if c % 2:
                            act.wait_ge(chunk_done, 4 * q0 + 12 * e + 8 + c + 1)
                            for t in range(n):
                                act.copy(y_tok[:, t, c // 2 * 512:(c // 2 + 1) * 512],
                                         bank[4 * (c // 2) + t][:, :]).then_inc(banks_out, share(t, n))
                by_tiles(act, count(e), body)

            act.wait_ge(rows_stored, 16)
            act.wait_ge(chunk_done, 4 * q0)
            for c in range(1, DEEP - 1):
                deep_hi(0, c)
            x_high(0)
            act.nop().then_inc(banks_out, 8)
            with act.Fori(0, NE) as e:
                until_turned(e)
                x_high(e + 1)
                second_product(e)
            act.wait_ge(gate_step, 3)
            for part in range(4):
                f = slice(part * 256, (part + 1) * 256)
                act.wait_ge(y_loaded[part], 32)
                for t in range(TT):
                    op = act.activation(y_one[:, t, f], y_one[:, t, f], ACT.Copy, scale=g_one[:, t:t + 1])
                op.then_inc(y_step, 1)
                if part:
                    sum_hi(3, 2 * part - 2)
                    sum_hi(3, 2 * part - 1)
            sum_hi(3, KD - 2)
            sum_hi(3, KD - 1)
            norm(3)
            gate(1, 3)
            for t in range(TT):
                act.wait_ge(final_turned, t + 1)
                act.copy(o_tok[:, t, 0:512], bank[2 * t][:, :]).then_inc(final_act, 1)

        @block.vector
        def _(dve):
            def minus(dst, a, b):
                return dve.tensor_tensor(dst, a, b, ALU.subtract)

            def split_lo(q, j, n, last64=False):
                dve.wait_ge(hi_ready, 4 * q + j + 1)
                if last64:
                    minus(w_lo[j % 2][:, 0:1024], raw[j][:, 0:1024], w_hi[j % 2][:, 0:1024].bitcast(F32))
                    minus(w_lo[j % 2][0:FE_LAST, 1024:1536], raw[j][0:FE_LAST, 1024:1536],
                          w_hi[j % 2][0:FE_LAST, 1024:1536].bitcast(F32)).then_inc(lo_ready, 1)
                else:
                    minus(w_lo[j % 2][:, 0:n], raw[j][:, 0:n], w_hi[j % 2][:, 0:n].bitcast(F32)).then_inc(lo_ready, 1)

            def second_early(name):
                split_lo(BASE[name] // RAW, 1, SIZE[name])

            def ahead(name, q, j, last):
                n = NEXT_SIZE[name] if last else SIZE[name]
                for c in ahead_of(name, j, q) if n else []:
                    split_lo(q + c // RAW, c % RAW, n)

            def deep_ahead(q, i, j):
                if 4 * i + j + DEEP - 1 < COUNT["gate1"]:
                    c, n = 4 * q + j + DEEP - 1, SIZE["gate1"]
                    dve.wait_ge(hi_ready, c + 1)
                    minus(w_lo[c % DEEP][:, 0:n], raw[c % RAW][:, 0:n], w_hi[c % DEEP][:, 0:n].bitcast(F32)
                          ).then_inc(lo_ready, 1)

            def low(dst, psum, hi, scale=1.0):
                return dve.scalar_tensor_tensor(out=dst, in0=psum, scalar=scale, in1=hi.bitcast(F32),
                                                op0=ALU.mult, op1=ALU.subtract)

            def tiles_lo(name, hi, lo, scale=1.0):
                def step(q, i, j, last):
                    ahead(name, q, j, last)
                    dve.wait_ge(out_hi, OUT_HI[name] + 4 * i + j + 1)
                    low(lo[:, 4 * i + j, :], bank[j][:, :], hi[:, 4 * i + j, :], scale).then_inc(drained, 1)
                quads(dve, name, step, peel=True)

            def values_lo(name):
                def step(q, i, j, last):
                    ahead(name, q, j, last)
                    if j % 2 == 0:
                        return
                    g = 2 * i + j // 2
                    c = slice(g * 256, (g + 1) * 256)
                    dve.wait_ge(out_hi, OUT_HI[name] + 2 * (g + 1))
                    for t in range(TT):
                        op = low(v_lo[:, t, c], bank[j // 2 * 4 + t][:, 0:256], v_hi[:, t, c])
                    op.then_inc(drained, 2)
                quads(dve, name, step, peel=True)

            def sum_exact(k, psum):
                dve.scalar_tensor_tensor(out=x_exact[:, k, :], in0=x_exact[:, k, :], scalar=ALPHA, in1=psum,
                                         op0=ALU.mult, op1=ALU.add).then_inc(summed, 1)

            def sum_low(n, k):
                dve.wait_ge(y_hi_ready, KD * n + k + 1)
                return minus(x_lo[:, k, :], x_exact[:, k, :], x_hi[:, k, :].bitcast(F32))

            def add_residual(n, k, psum):
                sum_exact(k, psum)
                return sum_low(n, k)

            def residual(name, n):
                def step(q, i, j, last):
                    ahead(name, q, j, last)
                    if name != "down":
                        dve.wait_ge(chunk_done, 4 * q + j + 1)
                        add_residual(n, 4 * i + j, bank[j][:, :]).then_inc(drained, 1)
                    elif j % 2:
                        dve.wait_ge(chunk_done, 4 * q + j + 1)
                        add_residual(n, 2 * i + j // 2, bank[j // 2][:, :]).then_inc(drained, 2)
                quads(dve, name, step, peel=True)

            def norm(n):
                dve.wait_ge(mean_done, n + 1)
                for k in range(KD):
                    minus(x_exact[:, k, :], x_exact[:, k, :], bank[4][:, :]).then_inc(centred, 1)
                q_proj = BASE["proj0"] // RAW
                if n == 0:
                    second_early("gu")
                if n == 1:
                    ahead("proj0", q_proj, 0, False)
                dve.wait_ge(std_ready, n + 1)
                dve.reciprocal(rstd[:, :], rstd[:, :]).then_inc(rstd_ready, 1)
                dve.wait_ge(rstd_ready, n + 1)
                dve.wait_ge(squared, KD * (n + 1))
                done = [0, KD, 3 * KD, 4 * KD][n]

                def scale(k):
                    dve.tensor_tensor(x_exact[:, k, :], x_exact[:, k, :], rstd[:, :], ALU.mult).then_inc(normed, 1)

                def low_tile(k):
                    if n != 2:
                        dve.wait_ge(affine, done + k + 1)
                        minus(x_lo[:, k, :], x_exact[:, k, :], x_hi[:, k, :].bitcast(F32)).then_inc(x_ready, 1)
                for k in range(KD):
                    scale(k)
                    if n == 1 and k in (0, 2):
                        ahead("proj0", q_proj, k // 2 + 1, False)
                    if n == 1 and k == 5:
                        ahead("proj0", q_proj, 3, True)
                        second_early("gate0")
                    if k >= 2:
                        low_tile(k - 2)
                low_tile(KD - 2)
                low_tile(KD - 1)

            def turned_p(layer):
                for k in range(KP):
                    dve.wait_ge(turned_hi, KD + KP * layer + k + 1)
                    low(pt_lo[layer][:, k, :], bank[6 + k][:, :], pt_hi[layer][:, k, :]).then_inc(turned_lo, 1)

            def embed(layer, before_last):
                name = f"proj{layer}"

                def step(q, i, j, last):
                    if last:
                        before_last()
                    ahead(name, q, j, last)
                    dve.wait_ge(chunk_done, 4 * q + j + 1)
                    for s in range(2):
                        op = dve.tensor_copy(proj[:, 2 * j + s, :], bank[j % 2 * 2 + s][:, :])
                    op.then_inc(drained, 1)
                quads(dve, name, step)

            def gate(layer):
                name = f"gate{layer}"

                def step(q, i, j, last):
                    if layer:
                        deep_ahead(q, i, j)
                    else:
                        ahead(name, q, j, last)
                    k = 4 * i + j
                    if layer == 0 and k == 0:
                        dve.wait_ge(proj_out, 2)
                    source = bank[PROJ_BANKS[0][k // 2] + k % 2][:, :] if layer == 0 and k >= 4 else proj[:, k, :]
                    dve.wait_ge(gated, GATED[name] + k + 1)
                    dve.tensor_tensor(proj[:, k, :], source, sig[:, k, :], ALU.mult).then_inc(drained, 1)
                    dve.wait_ge(drained, DRAINED[name] + k + 1)
                    dve.tensor_tensor(x_exact[:, k, :], x_exact[:, k, :], proj[:, k, :], ALU.add).then_inc(embedded, 1)
                quads(dve, name, step)
                if layer == 0:
                    second_early("q1")
                    for k in range(KD):
                        dve.wait_ge(affine, 2 * KD + k + 1)
                        minus(x_lo[:, k, :], x_exact[:, k, :], x_hi[:, k, :].bitcast(F32)).then_inc(x_ready, 1)

            dve.wait_ge(built, BUILT)
            dve.memset(eps[:, :], EPS)
            dve.tensor_scalar(neg_ones[:, :], ones[:, :], -1.0, None, ALU.mult)
            dve.tensor_copy(mean_r[:, :], mean_f[:, :])
            dve.tensor_copy(neg_incl[:, :], neg_incl_f[:, :]).then_inc(consts, 1)
            for k in range(KD + 2):
                if k < KD:
                    dve.wait_ge(turned, k + 1)
                    dve.tensor_copy(x_exact[:, k, :], bank[4 + k % 4][:, :]).then_inc(turned_out, 1)
                if k < 2:
                    split_lo(0, k, SIZE["q0"])
                else:
                    dve.wait_ge(turned_hi, k - 1)
                    minus(x_lo[:, k - 2, :], x_exact[:, k - 2, :], x_hi[:, k - 2, :].bitcast(F32)).then_inc(turned_lo, 1)
            dve.wait_ge(turned, KD + 1)
            dve.tensor_copy(ln_cols[:, :], bank[2][:, 0:64]).then_inc(consts, 1)
            tiles_lo("q0", q_hi, q_lo, SCALE)
            tiles_lo("k0", k_hi, k_lo)
            values_lo("v0")

            def mix_low(h):
                for d in range(DT):
                    f = DT * (h % H) + d
                    dve.wait_ge(mix_hi, DT * h + d + 1)
                    low(q_lo[:, f, :], bank[6 + d][:, :], q_hi[:, f, :]).then_inc(mix_lo, 1)

            for h in range(H):
                for g, group in enumerate(((3, 2, 1), (0,))):
                    lo, hi = OFF[group[-1]], OFF[group[0]] + WID[group[0]]
                    dve.wait_ge(logged, 2 * h + g + 1)
                    for n in group:
                        o = slice(OFF[n], OFF[n] + WID[n])
                        op = dve.scalar_tensor_tensor(out=sp[:, o], in0=bank[n][:, 0:WID[n]], scalar=0.0, in1=ln_a[:, o],
                                                      op0=ALU.max, op1=ALU.add)
                    op.then_inc(sp_raw, 1)
                    dve.wait_ge(sp_raw, 2 * h + g + 1)
                    for n in group:
                        o = slice(OFF[n], OFF[n] + P)
                        op = dve.tensor_tensor(sp[:, o], sp[:, o], keep[:, :], ALU.mult)
                    op.then_inc(sp_ready, 1)
                for g, (lo, hi) in enumerate(((OFF[1], TRI), (0, OFF[1]))):
                    dve.wait_ge(sp_hi_ready, 2 * h + g + 1)
                    minus(sp_lo[:, lo:hi], sp[:, lo:hi], sp_hi[:, lo:hi].bitcast(F32)).then_inc(sp_lo_ready, 1)
                if h:
                    mix_low(h - 1)
                for g, n in enumerate(reversed(range(TT))):
                    dve.wait_ge(tail_done, TT * h + g + 1)
                    dve.tensor_tensor(a_diag[:, n, :], bank[n][:, 0:P], floor_a[:, :], ALU.min).then_inc(diag_cut, 1)
                if h:
                    dve.wait_ge(mixed, DT * h)
                for g, (lo, hi) in enumerate(((OFF[1], TRI), (0, OFF[1]))):
                    dve.wait_ge(a_ready, TT * h + (TT - 1, TT)[g])
                    dve.tensor_copy(a_hi[:, lo:hi], ln_a[:, lo:hi]).then_inc(a_hi_ready, 1)
                    dve.wait_ge(a_hi_ready, 2 * h + g + 1)
                    minus(a_lo[:, lo:hi], ln_a[:, lo:hi], a_hi[:, lo:hi].bitcast(F32)).then_inc(a_lo_ready, 1)
            mix_low(H - 1)
            residual("o0", 0)
            norm(0)

            def gu_step(q, i, j, last):
                ahead("gu", q, j, last)
                if j % 2 == 0:
                    return
                m, t = 2 * i + j // 2, h_tmp[j // 2]
                dve.wait_ge(gated, m + 1)
                dve.tensor_tensor(t[:, :], t[:, :], bank[j][:, :], ALU.mult).then_inc(hidden, 1)
                dve.wait_ge(out_hi, OUT_HI["gu"] + 2 * (m + 1))
                minus(h_lo[:, m, :], t[:, :], h_hi[:, m, :].bitcast(F32)).then_inc(drained, 2)
            quads(dve, "gu", gu_step, peel=True)
            residual("down", 1)
            turned_p(0)
            norm(1)
            gate(0)
            tiles_lo("q1", q_hi, q_lo, SCALE)
            dve.wait_ge(f_done, 1)
            dve.tensor_copy(f_row[:, :], bank[4][0:H, :]).then_inc(f_step, 1)
            tiles_lo("k1", k_hi, k_lo)
            dve.wait_ge(f_turned, 1)
            dve.wait_ge(small_loaded, 48)
            for t in range(TT):
                op = dve.tensor_tensor(f_pre[:, t, :], bank[5][:, t * H:(t + 1) * H], b_f[:, :], ALU.add)
            op.then_inc(f_step, 1)
            dve.wait_ge(f_act, 1)
            dve.tensor_scalar(f_pre[:, :, :], f_pre[:, :, :], 0.0, None, ALU.min).then_inc(f_step, 1)
            dve.wait_ge(f_step, 3)
            dve.wait_ge(f_act, 3)
            minus(log_f[:, :, :], f_pre[:, :, :], f_abs[:, :, :]).then_inc(f_step, 1)
            values_lo("v1")

            dve.wait_ge(c_done, 1)
            dve.tensor_copy(c_col[:, :, :], bank[0][:, 0:TT * H].rearrange("p (t h) -> p t h", h=H)).then_inc(c_copied, 1)
            dve.wait_ge(c_copied, 1)
            for h in range(H):
                if h:
                    dve.wait_ge(row_done, h)
                for t in range(TT):
                    op = dve.tensor_scalar(c_diag[:, t, :], ident[:, :], c_col[:, t, h:h + 1], None, ALU.mult)
                op.then_inc(diag_ready, 1)

            def scores_b(h):
                for m in range(TT):
                    s = TT * h + m
                    z, d = zb[:, OB[m]:OB[m] + WB[m]], zb[:, OB[m] + m * P:OB[m] + WB[m]]
                    dve.wait_ge(z2_done, s + 1)
                    if m == 0:
                        dve.wait_ge(row_copied, h + 1)
                    if h:
                        dve.wait_ge(w_turned, TT * (h - 1) + m + 1)
                    dve.scalar_tensor_tensor(out=z, in0=bank[m][:, 0:WB[m]], scalar=c_col[:, m, h:h + 1],
                                             in1=c_row[:, h, 0:WB[m]], op0=ALU.add, op1=ALU.subtract).then_inc(z2_step, 1)
                    dve.wait_ge(z2_step, 3 * s + 1)
                    dve.tensor_tensor(d, d, clip_b[:, :], ALU.min).then_inc(z2_step, 1)
                    dve.wait_ge(z2_step, 3 * s + 2)
                    dve.tensor_reduce(neg_max[:, m:m + 1], z, AX.X, ALU.max, negate=True).then_inc(z2_step, 1)

            def weights_b(h):
                for m in range(TT):
                    s = TT * h + m
                    z = zb[:, OB[m]:OB[m] + WB[m]]
                    dve.wait_ge(e_ready, s + 1)
                    dve.reciprocal(row_inv[:, m:m + 1], row_sum[:, m:m + 1]).then_inc(inv_ready, 1)
                    dve.wait_ge(inv_ready, s + 1)
                    dve.tensor_scalar(z, z, row_inv[:, m:m + 1], None, ALU.mult).then_inc(w_ready, 1)

            for h in range(H):
                scores_b(h)
                if h:
                    mix_low(H + h - 1)
                weights_b(h)
                for m in range(TT):
                    s = TT * h + m
                    dve.wait_ge(wt_hi_ready, s + 1)
                    src = bank[4 + m % 2][:, 0:WB[m]].rearrange("p (n t) -> p n t", t=P)
                    low(wt_lo[:, 0:m + 1, m * P:(m + 1) * P], src, wt_hi[:, 0:m + 1, m * P:(m + 1) * P]).then_inc(wt_ready, 1)
            mix_low(2 * H - 1)
            residual("o1", 2)
            norm(2)

            dve.wait_ge(router_done, 1)
            dve.tensor_copy(logits_e[:, :], bank[5][0:NE, :]).then_inc(route_step, 1)
            dve.wait_ge(logits_turned, 1)
            dve.tensor_copy(logits[:, :, :], bank[6][:, 0:TT * NE].rearrange("p (t e) -> p t e", e=NE)).then_inc(route_step, 1)
            dve.wait_ge(route_step, 2)
            for t in range(TT):
                op = dve.max(top[:, t, :], logits[:, t, :])
            op.then_inc(route_step, 1)
            dve.wait_ge(route_step, 3)
            minus(g_diff[:, :], top[:, :, 1], top[:, :, 0]).then_inc(route_step, 1)
            for t in range(TT):
                op = dve.max_index(top_at[:, t, :], top[:, t, :], logits[:, t, :])
            op.then_inc(route_step, 1)
            dve.wait_ge(route_step, 5)
            dve.tensor_copy(top_f[:, :, :], top_at[:, :, 0:2]).then_inc(route_step, 1)
            dve.wait_ge(route_step, 6)
            for c in range(2):
                for t in range(TT):
                    op = dve.tensor_scalar(sel[:, c, t, :], lanes[:, :], top_f[:, t, c:c + 1], None, ALU.is_equal)
            op.then_inc(route_step, 1)
            dve.wait_ge(route_step, 7)
            dve.tensor_tensor(sel_any[:, :, :], sel[:, 0, :, :], sel[:, 1, :, :], ALU.add).then_inc(route_step, 1)
            dve.wait_ge(ranked, 1)
            for t in range(TT):
                op = dve.tensor_tensor(slot_all[:, t, :], bank[7][:, t * NE:(t + 1) * NE], lane_slots[:, :], ALU.add)
            op.then_inc(slot_step, 1)
            counts = bank[7][:, TT * NE:(TT + 1) * NE]
            for b in tiles_f:
                dve.memset(b[:, NE:], 1.0)
            dve.tensor_scalar(tiles_f[0][:, 0:NE], counts, float(P), 1.0, ALU.is_gt, ALU.add).then_inc(slot_step, 1)
            dve.wait_ge(slot_step, 2)
            for c in range(2):
                dve.tensor_tensor(sel[:, c, :, :], sel[:, c, :, :], slot_all[:, :, :], ALU.mult)
            dve.scalar_tensor_tensor(out=tiles_f[1][:, 0:NE], in0=counts, scalar=2.0 * P, in1=tiles_f[0][:, 0:NE],
                                     op0=ALU.is_gt, op1=ALU.add).then_inc(slot_step, 1)
            dve.wait_ge(slot_step, 3)
            for c in range(2):
                dve.tensor_reduce(slot_f[:, c, :], sel[:, c, :, :], AX.X, ALU.add)
            dve.scalar_tensor_tensor(out=tiles_f[0][:, 0:NE], in0=counts, scalar=3.0 * P, in1=tiles_f[1][:, 0:NE],
                                     op0=ALU.is_gt, op1=ALU.add).then_inc(slot_step, 1)
            dve.wait_ge(slot_step, 4)
            dve.tensor_copy(slot_i[:, :, :], slot_f[:, :, :]).then_inc(slots_ready, 1)
            dve.tensor_copy(tiles_i[:, :], tiles_f[0][:, :]).then_inc(tiles_ready, 1)
            dve.wait_ge(gate_exp, 1)
            dve.tensor_scalar(g_sum[:, :], g_exp[:, :], 1.0, None, ALU.add).then_inc(gate_step, 1)
            dve.wait_ge(gate_step, 1)
            dve.reciprocal(g_one[:, :], g_sum[:, :]).then_inc(gate_step, 1)
            dve.wait_ge(gate_step, 2)
            dve.tensor_tensor(g_two[:, :], g_exp[:, :], g_one[:, :], ALU.mult).then_inc(gate_step, 1)
            turned_p(1)

            def read_list():
                dve.wait_ge(list_turned, 1)
                dve.tensor_copy(place_c[:, :], bank[6][:, 0:SLOT_TILES]).then_inc(list_step, 1)
                dve.wait_ge(list_step, 1)
                dve.tensor_copy(place_i[:, :], place_c[:, :])
                for i in range(2):
                    op = dve.tensor_scalar(past[i][:, :], place_c[:, :], float(SEQ * (i + 1)), -float(SEQ), ALU.is_ge, ALU.mult)
                op.then_inc(list_step, 1)
                dve.wait_ge(list_step, 2)
                dve.tensor_tensor(past[0][:, :], past[0][:, :], past[1][:, :], ALU.add).then_inc(list_step, 1)
                dve.wait_ge(list_step, 3)
                dve.tensor_tensor(token_i[:, :], past[0][:, :], place_c[:, :], ALU.add).then_inc(list_ready, 1)
            embed(1, read_list)

            q0 = BASE["moe"] // RAW
            for t in range(TT):
                dve.memset(he[:, t, FE:], 0.0)

            def count(e):
                return dve.value_load(tiles_i[0:1, bass.ds(e, 1)], min_val=1, max_val=TT)

            def x_low(e):
                def body(n):
                    for t in range(n):
                        dve.wait_ge(xg_hi_ready, TT * e + t + 1)
                        for b in range(2):
                            k, s = slice(4 * b, 4 * b + 4), slice(t * P, (t + 1) * P)
                            op = low(x_lo[:, k, s], bank[6 - t % 2 * 2 + b][:, :].rearrange("p (k t) -> p k t", t=P),
                                     x_hi[:, k, s])
                        op.then_inc(xg_ready, share(t, n))
                by_tiles(dve, count(e), body)

            def deep_lo(e, c):
                e, c = (e, c) if c < 12 else (e + 1, c - 12)
                q, j = q0 + 3 * e + c // RAW, c % RAW
                dve.wait_ge(hi_ready, 4 * q + j + 1)
                n = 4 * FC[c // 4] if c < 8 else (1536, 1024)[c % 2]
                op = minus(w_lo[j][:, 0:n], raw[j][:, 0:n], w_hi[j][:, 0:n].bitcast(F32))
                if c in (9, 11):
                    op = minus(w_lo[j][0:FE_LAST, 1024:1536], raw[j][0:FE_LAST, 1024:1536],
                               w_hi[j][0:FE_LAST, 1024:1536].bitcast(F32))
                op.then_inc(lo_ready, 1)

            def turned_lo_parts(e, half, n):
                for t in range(n):
                    k, s = slice(3 * half, 3 * half + 3), slice(t * P, (t + 1) * P)
                    dve.wait_ge(het_hi_ready, 8 * e + half * TT + t + 1)
                    low(het_lo[:, k, s], bank[4 + t][:, 0:3 * P].rearrange("p (k t) -> p k t", t=P), het_hi[:, k, s]
                        ).then_inc(het_ready, share(t, n))

            def until_turned(e):
                def body(n):
                    for c in range(9):
                        deep_lo(e, c + DEEP - 1)
                        if c in (3, 7):
                            half = c // 4
                            dve.wait_ge(chunk_done, 4 * q0 + 12 * e + c + 1)
                            for t in range(n):
                                o = he[:, t, half * FC[0]:half * FC[0] + FC[half]]
                                dve.wait_ge(silu_ready, 8 * e + half * TT + t + 1)
                                dve.tensor_tensor(o, o, bank[4 + t][:, 0:FC[half]], ALU.mult).then_inc(he_ready, share(t, n))
                        if c in (4, 8):
                            turned_lo_parts(e, c // 8, n)
                by_tiles(dve, count(e), body)

            for c in range(1, DEEP - 1):
                deep_lo(0, c)
            x_low(0)
            with dve.Fori(0, NE) as e:
                until_turned(e)
                x_low(e + 1)
                for c in range(1, 4):
                    deep_lo(e, 8 + c + DEEP - 1)
            def sums(part):
                for k in range(2 * part, 2 * part + 2):
                    dve.wait_ge(acc_turned, k + 1)
                    sum_exact(k, bank[k % 4][:, :])
                sum_low(3, 2 * part).then_inc(drained, 1)
                sum_low(3, 2 * part + 1).then_inc(drained, 1)

            for part in range(4):
                f = slice(part * 256, (part + 1) * 256)
                dve.wait_ge(y_loaded[part], 32)
                dve.wait_ge(y_step, part + 1)
                for t in range(TT):
                    op = dve.scalar_tensor_tensor(out=y_one[:, t, f], in0=y_two[:, t, f], scalar=g_two[:, t:t + 1],
                                                  in1=y_one[:, t, f], op0=ALU.mult, op1=ALU.add)
                op.then_inc(combined, 1)
                if part:
                    sums(part - 1)
            sums(3)
            norm(3)
            gate(1)
            for t in range(TT):
                dve.wait_ge(final_turned, t + 1)
                dve.tensor_copy(o_tok[:, t, 512:1024], bank[2 * t + 1][:, :]).then_inc(final_dve, 1)


_INS = ["x", "p", "a_w_qkv", "a_w_o", "kvf_w", "kvf_b_f", "b_w_q", "b_w_o", "ffn_w_gu", "ffn_w_down",
        "moe_w_router", "moe_w_gu", "moe_w_down", "ple_w_proj", "ple_w_gate", "ln_g", "ln_b"]


def kernel(**inputs):
    import numpy as np
    import concourse.bacc as bacc
    from concourse.bass_utils import run_bass_kernel_spmd

    nc = bacc.Bacc("TRN2", target_bir_lowering=False, num_devices=1)
    arrays, args = {}, []
    for name in _INS:
        a = np.ascontiguousarray(inputs[name])
        arrays[name] = a
        args.append(nc.dram_tensor(name, a.shape, mybir.dt.from_np(a.dtype), kind="ExternalInput").ap())
    args.append(nc.dram_tensor("result", (1, SEQ, D), F32, kind="ExternalOutput").ap())
    build(nc, *args)
    return run_bass_kernel_spmd(nc, [arrays], core_ids=[0]).results[0]["result"]
```
